# Optimizing a Trainium2 kernel written in Bass

```python
import math
import jax, jax.numpy as jnp
from jax import lax
import numpy as np
import jax
import jax.numpy as jnp

D_MODEL = 1024
BATCH = 1
SEQ = 256
DEPTH = 2

CHUNK = 64
N_META = 16
N_A_LAYERS = DEPTH // 2
N_B_LAYERS = DEPTH - N_A_LAYERS
D_RNN = 3 * D_MODEL // 2
N_LRU_BLOCKS = 16
LRU_BLOCK = D_RNN // N_LRU_BLOCKS
LRU_C = 8.0
CONV_A_WIDTH = 4
N_FOX_HEADS = 16
FOX_HEAD_DIM = D_MODEL // N_FOX_HEADS
Q_BLOCK = 128
D_FF = ((8 * D_MODEL // 3 + 255) // 256) * 256
CONV_F_WIDTH = 3
DN_ALPHA = (2 * DEPTH) ** 0.25
DN_BETA = (8 * DEPTH) ** -0.25
LN_EPS = 1e-5


def layer_norm(x, g, b):
    xf = x.astype(jnp.float32)
    mu = jnp.mean(xf, axis=-1, keepdims=True)
    var = jnp.mean(jnp.square(xf - mu), axis=-1, keepdims=True)
    y = (xf - mu) * lax.rsqrt(var + LN_EPS)
    return (y * g.astype(jnp.float32) + b.astype(jnp.float32)).astype(x.dtype)

def causal_dwconv(x, w, b):
    width = w.shape[0]
    length = x.shape[1]
    xp = jnp.pad(x, ((0, 0), (width - 1, 0), (0, 0)))
    y = b
    for k in range(width):
        y = y + xp[:, k:k + length] * w[k]
    return y

def rg_lru(x, w_r, b_r, w_i, b_i, lam):
    bsz, length, width = x.shape
    xb = x.reshape(bsz, length, N_LRU_BLOCKS, LRU_BLOCK)
    r = jax.nn.sigmoid(jnp.einsum('blnc,ncd->blnd', xb, w_r).reshape(bsz, length, width) + b_r)
    i = jax.nn.sigmoid(jnp.einsum('blnc,ncd->blnd', xb, w_i).reshape(bsz, length, width) + b_i)
    log_a = -LRU_C * r.astype(jnp.float32) * jax.nn.softplus(-lam.astype(jnp.float32))
    a = jnp.exp(log_a)
    u = jnp.sqrt(-jnp.expm1(2.0 * log_a)) * (i * x).astype(jnp.float32)

    def combine(left, right):
        a1, b1 = left
        a2, b2 = right
        return a1 * a2, a2 * b1 + b2

    _, h = lax.associative_scan(combine, (a, u), axis=1)
    return h.astype(x.dtype)

def recurrent_mixer(x, w_in, conv_w, conv_b, w_r, b_r, w_i, b_i, lam, w_out):
    gr = x @ w_in
    gate, rec = gr[..., :D_RNN], gr[..., D_RNN:]
    rec = causal_dwconv(rec, conv_w, conv_b)
    h = rg_lru(rec, w_r, b_r, w_i, b_i, lam)
    return (jax.nn.gelu(gate) * h) @ w_out

def conv_ffn(x, w_in, conv_w, conv_b, w_out):
    h = causal_dwconv(x @ w_in, conv_w, conv_b)
    gate, val = h[..., :D_FF], h[..., D_FF:]
    return (jax.nn.gelu(gate) * val) @ w_out

def to_heads_padded(t, lp):
    bsz, length, _ = t.shape
    t = t.reshape(bsz, length, N_FOX_HEADS, FOX_HEAD_DIM).transpose(0, 2, 1, 3)
    return jnp.pad(t, ((0, 0), (0, 0), (0, lp - length), (0, 0)))

def shared_kv(x, kv_w, f_b):
    length = x.shape[1]
    lp = -(-length // Q_BLOCK) * Q_BLOCK
    z = x @ kv_w
    k = to_heads_padded(z[..., :D_MODEL], lp)
    v = to_heads_padded(z[..., D_MODEL:2 * D_MODEL], lp)
    log_f = jax.nn.log_sigmoid(z[..., 2 * D_MODEL:].astype(jnp.float32) + f_b.astype(jnp.float32))
    c = jnp.cumsum(log_f, axis=1).transpose(0, 2, 1)
    c = jnp.pad(c, ((0, 0), (0, 0), (0, lp - length)), mode='edge')
    return k, v, c

def forgetting_attention(q, k, v, c):
    lp = q.shape[2]
    scale = q.shape[-1] ** -0.5
    outs = []
    for q0 in range(0, lp, Q_BLOCK):
        end = q0 + Q_BLOCK
        s = jnp.einsum('bhqd,bhkd->bhqk', q[:, :, q0:end], k[:, :, :end]).astype(jnp.float32) * scale
        s = s + c[:, :, q0:end, None] - c[:, :, None, :end]
        mask = jnp.arange(end)[None, :] <= jnp.arange(q0, end)[:, None]
        s = jnp.where(mask, s, -jnp.inf)
        p = jax.nn.softmax(s, axis=-1).astype(v.dtype)
        outs.append(jnp.einsum('bhqk,bhkd->bhqd', p, v[:, :, :end]))
    return jnp.concatenate(outs, axis=2)

def fox_mixer(x, w_in, w_out, k, v, c):
    bsz, length, _ = x.shape
    qg = x @ w_in
    q = to_heads_padded(qg[..., :D_MODEL], k.shape[2])
    o = forgetting_attention(q, k, v, c)[:, :, :length]
    o = o.transpose(0, 2, 1, 3).reshape(bsz, length, D_MODEL)
    return (o * jax.nn.sigmoid(qg[..., D_MODEL:])) @ w_out

def first_inputs(seed: int = 0) -> dict:
    key = jax.random.key(seed)
    ks = jax.random.split(key, 24)
    f32 = jnp.float32
    d = D_MODEL

    def nrm(k, shape, scale):
        return jax.random.normal(k, shape, f32) * scale

    u = jax.random.uniform(ks[9], (N_A_LAYERS, D_RNN), f32, 0.9, 0.999)
    a0 = u ** (1.0 / LRU_C)
    lam = jnp.log(a0) - jnp.log1p(-a0)

    kv_w = jnp.concatenate([
        nrm(ks[11], (d, d), d ** -0.5),
        nrm(ks[12], (d, d), d ** -0.5 * DN_BETA),
        nrm(ks[13], (d, N_FOX_HEADS), d ** -0.5),
    ], axis=1)

    return {
        "x": nrm(ks[0], (BATCH, SEQ, d), 1.0),
        "meta": nrm(ks[1], (N_META, d), 1.0),
        "a_w_in": nrm(ks[2], (N_A_LAYERS, d, 2 * D_RNN), d ** -0.5),
        "a_conv_w": nrm(ks[3], (N_A_LAYERS, CONV_A_WIDTH, D_RNN), CONV_A_WIDTH ** -0.5),
        "a_conv_b": nrm(ks[4], (N_A_LAYERS, D_RNN), 0.02),
        "a_w_r": nrm(ks[5], (N_A_LAYERS, N_LRU_BLOCKS, LRU_BLOCK, LRU_BLOCK), LRU_BLOCK ** -0.5),
        "a_b_r": nrm(ks[6], (N_A_LAYERS, D_RNN), 0.02),
        "a_w_i": nrm(ks[7], (N_A_LAYERS, N_LRU_BLOCKS, LRU_BLOCK, LRU_BLOCK), LRU_BLOCK ** -0.5),
        "a_b_i": nrm(ks[8], (N_A_LAYERS, D_RNN), 0.02),
        "a_lambda": lam,
        "a_w_out": nrm(ks[10], (N_A_LAYERS, D_RNN, d), D_RNN ** -0.5 * DN_BETA),
        "kv_w": kv_w,
        "kv_f_b": jax.random.uniform(ks[14], (N_FOX_HEADS,), f32, 1.0, 4.0),
        "b_w_in": nrm(ks[15], (N_B_LAYERS, d, 2 * d), d ** -0.5),
        "b_w_out": nrm(ks[16], (N_B_LAYERS, d, d), d ** -0.5 * DN_BETA),
        "f_w_in": nrm(ks[17], (DEPTH, d, 2 * D_FF), d ** -0.5),
        "f_conv_w": nrm(ks[18], (DEPTH, CONV_F_WIDTH, 2 * D_FF), CONV_F_WIDTH ** -0.5),
        "f_conv_b": nrm(ks[19], (DEPTH, 2 * D_FF), 0.02),
        "f_w_out": nrm(ks[20], (DEPTH, D_FF, d), D_FF ** -0.5 * DN_BETA),
        "ln1_g": 1.0 + nrm(ks[21], (DEPTH, d), 0.02),
        "ln1_b": nrm(ks[22], (DEPTH, d), 0.02),
        "ln2_g": 1.0 + nrm(ks[23], (DEPTH, d), 0.02),
        "ln2_b": nrm(jax.random.fold_in(key, 99), (DEPTH, d), 0.02),
    }

def first_block(x, meta, a_w_in, a_conv_w, a_conv_b, a_w_r, a_b_r, a_w_i, a_b_i, a_lambda, a_w_out,
              kv_w, kv_f_b, b_w_in, b_w_out, f_w_in, f_conv_w, f_conv_b, f_w_out,
              ln1_g, ln1_b, ln2_g, ln2_b):
    bsz = x.shape[0]
    h = jnp.concatenate([jnp.broadcast_to(meta.astype(x.dtype), (bsz, N_META, D_MODEL)), x], axis=1)
    k = v = c = None
    for layer in range(DEPTH):
        if layer < N_A_LAYERS:
            mix = recurrent_mixer(h, a_w_in[layer], a_conv_w[layer], a_conv_b[layer],
                                  a_w_r[layer], a_b_r[layer], a_w_i[layer], a_b_i[layer],
                                  a_lambda[layer], a_w_out[layer])
        else:
            if layer == N_A_LAYERS:
                k, v, c = shared_kv(h, kv_w, kv_f_b)
            j = layer - N_A_LAYERS
            mix = fox_mixer(h, b_w_in[j], b_w_out[j], k, v, c)
        h = layer_norm(DN_ALPHA * h + mix, ln1_g[layer], ln1_b[layer])
        ffn = conv_ffn(h, f_w_in[layer], f_conv_w[layer], f_conv_b[layer], f_w_out[layer])
        h = layer_norm(DN_ALPHA * h + ffn, ln2_g[layer], ln2_b[layer])
    return h[:, N_META:]


D_FF_2 = 2752
HEAD_DIM = 64
HEAD_SLOTS = 16
NUM_BUCKETS = 32
T5_MAX_EXACT = 16
T5_MAX_DIST = 128
GATHER_Q_BLOCK = 32
RMS_EPS = 1e-6
NEG_INF = -1e30
MLA_HEADS = 8
MLA_NOPE = 64
MLA_ROPE = 32
MLA_V = 64
MLA_Q_LORA = 256
MLA_KV_LORA = 128
ROPE_THETA = 10000.0
NSA_HEADS = 8
NSA_GROUPS = 2
NSA_HPG = NSA_HEADS // NSA_GROUPS
NSA_CMP_LEN = 32
NSA_CMP_STRIDE = 16
NSA_CMP_HID = 256
NSA_SLC_BLOCK = 64
NSA_SLC_TOP = 8
NSA_WINDOW = 512
NSA_FORCED = 1e6
DIL_PAIRS = ((128, 1), (512, 4), (2048, 16))
DIL_HPG = 4
DIL_SLOTS = len(DIL_PAIRS) * DIL_HPG
MOBA_HEADS = 4
MOBA_BLOCK = 256
MOBA_TOP = 3
EV_SPLITS = (MLA_Q_LORA, MLA_KV_LORA, MLA_ROPE, NSA_HEADS * HEAD_DIM) + (NSA_GROUPS * HEAD_DIM,) * 6 + (3 * NSA_HEADS,)
EV_COLS = sum(EV_SPLITS)
EV_OUT = MLA_HEADS * MLA_V + NSA_HEADS * HEAD_DIM
OD_SPLITS = (DIL_SLOTS * HEAD_DIM,) * 3 + (MOBA_HEADS * HEAD_DIM,) * 3
OD_COLS = sum(OD_SPLITS)
OD_OUT = DIL_HPG * HEAD_DIM + MOBA_HEADS * HEAD_DIM
N_EVEN = (DEPTH + 1) // 2
N_ODD = DEPTH // 2


def split_cols(u, sizes):
    return jnp.split(u, np.cumsum(sizes)[:-1].tolist(), axis=-1)

def rms_norm(x, g):
    x32 = x.astype(jnp.float32)
    y = x32 * lax.rsqrt(jnp.mean(x32 * x32, axis=-1, keepdims=True) + RMS_EPS)
    return (y * g.astype(jnp.float32)).astype(x.dtype)

def masked_softmax(logits, mask):
    l = jnp.where(mask, logits, NEG_INF)
    m = jnp.max(l, axis=-1, keepdims=True)
    e = jnp.where(mask, jnp.exp(l - m), 0.0)
    den = jnp.maximum(jnp.sum(e, axis=-1, keepdims=True), 1e-30)
    return e / den, (m + jnp.log(den))[..., 0]

def t5_bucket(dist):
    n = jnp.maximum(jnp.asarray(dist, jnp.int32), 0)
    nf = jnp.maximum(n, 1).astype(jnp.float32)
    large = T5_MAX_EXACT + (jnp.log(nf / T5_MAX_EXACT) / math.log(T5_MAX_DIST / T5_MAX_EXACT)
                            * (NUM_BUCKETS - T5_MAX_EXACT)).astype(jnp.int32)
    return jnp.where(n < T5_MAX_EXACT, n, jnp.minimum(large, NUM_BUCKETS - 1))

def from_blocks(a):
    n, b, qb = a.shape[:3]
    return jnp.moveaxis(a, 0, 1).reshape(b, n * qb, *a.shape[3:])

def rope_tables(s):
    inv = ROPE_THETA ** (-jnp.arange(0, MLA_ROPE, 2, dtype=jnp.float32) / MLA_ROPE)
    ang = jnp.arange(s, dtype=jnp.float32)[:, None] * inv[None, :]
    return jnp.cos(ang), jnp.sin(ang)

def apply_rope(x, cos, sin):
    x32 = x.astype(jnp.float32)
    half = x.shape[-1] // 2
    x1, x2 = x32[..., :half], x32[..., half:]
    return jnp.concatenate([x1 * cos - x2 * sin, x2 * cos + x1 * sin], axis=-1).astype(x.dtype)

def swiglu(y, w_in, w_out):
    a, b = jnp.split(y @ w_in, 2, axis=-1)
    return (jax.nn.silu(a) * b) @ w_out

def modulate(x, g, shift, scale):
    return rms_norm(x, g) * (1.0 + scale[:, None, :]) + shift[:, None, :]

def causal_dense(q, k, v):
    b, s = q.shape[:2]
    scale = q.shape[-1] ** -0.5
    kpos = jnp.arange(s)

    def block(blk):
        qs = blk * Q_BLOCK
        qb = lax.dynamic_slice_in_dim(q, qs, Q_BLOCK, axis=1)
        qpos = qs + jnp.arange(Q_BLOCK)
        logits = jnp.einsum('bqhd,bkhd->bhqk', qb, k).astype(jnp.float32) * scale
        p, _ = masked_softmax(logits, kpos[None, :] <= qpos[:, None])
        return jnp.einsum('bhqk,bkhd->bqhd', p.astype(v.dtype), v)

    return from_blocks(lax.map(block, jnp.arange(s // Q_BLOCK)))

def band_attn(q, k, v, bias_tab, w, r):
    b, s, g, p_, dh = q.shape
    scale = dh ** -0.5
    nk = w // r + 1
    dist = r * np.arange(nk)
    bias = jnp.transpose(bias_tab[t5_bucket(dist)], (1, 2, 0))[:, :, None, :]
    kp = jnp.pad(k, ((0, 0), (w, 0), (0, 0), (0, 0)))
    vp = jnp.pad(v, ((0, 0), (w, 0), (0, 0), (0, 0)))
    gidx = np.arange(Q_BLOCK)[:, None] + w - dist[None, :]
    dist_j = jnp.asarray(dist)

    def block(blk):
        qs = blk * Q_BLOCK
        qb = lax.dynamic_slice_in_dim(q, qs, Q_BLOCK, axis=1)
        kg = lax.dynamic_slice_in_dim(kp, qs, w + Q_BLOCK, axis=1)[:, gidx]
        vg = lax.dynamic_slice_in_dim(vp, qs, w + Q_BLOCK, axis=1)[:, gidx]
        ok = (qs + jnp.arange(Q_BLOCK)[:, None] - dist_j[None, :]) >= 0
        logits = jnp.einsum('bqgpd,bqkgd->bgpqk', qb, kg).astype(jnp.float32) * scale + bias
        pr, lse = masked_softmax(logits, ok)
        out = jnp.einsum('bgpqk,bqkgd->bqgpd', pr.astype(vg.dtype), vg)
        return out, lse

    outs, lses = lax.map(block, jnp.arange(s // Q_BLOCK))
    lse = jnp.transpose(lses, (1, 0, 4, 2, 3)).reshape(b, s, g, p_)
    return from_blocks(outs), lse

def mla_mixer(cq, ckv, kr, q_norm_g, kv_norm_g, w_uq, w_ukv, qk_g):
    b, s = cq.shape[:2]
    q = (rms_norm(cq, q_norm_g) @ w_uq).reshape(b, s, MLA_HEADS, MLA_NOPE + MLA_ROPE)
    kv = (rms_norm(ckv, kv_norm_g) @ w_ukv).reshape(b, s, MLA_HEADS, MLA_NOPE + MLA_V)
    cos, sin = rope_tables(s)
    q_nope = rms_norm(q[..., :MLA_NOPE], qk_g[0, :MLA_NOPE])
    q_rope = apply_rope(rms_norm(q[..., MLA_NOPE:], qk_g[0, MLA_NOPE:]), cos[:, None, :], sin[:, None, :])
    k_nope = rms_norm(kv[..., :MLA_NOPE], qk_g[1, :MLA_NOPE])
    k_rope = apply_rope(rms_norm(kr, qk_g[1, MLA_NOPE:]), cos, sin)
    qf = jnp.concatenate([q_nope, q_rope], axis=-1)
    kf = jnp.concatenate([k_nope, jnp.broadcast_to(k_rope[:, :, None, :], (b, s, MLA_HEADS, MLA_ROPE))], axis=-1)
    out = causal_dense(qf, kf, kv[..., MLA_NOPE:])
    return out.reshape(b, s, MLA_HEADS * MLA_V)

def nsa_mixer(q, kc, vc, ks, vs, kw, vw, gate_logits, cmp_pe, cmp_w1, cmp_w2, qk_g, bias_tab):
    b, s = q.shape[:2]
    g, p_, dh = NSA_GROUPS, NSA_HPG, HEAD_DIM
    scale = dh ** -0.5
    q = rms_norm(q.reshape(b, s, g, p_, dh), qk_g[0])
    kc, vc, ks, vs, kw, vw = [a.reshape(b, s, g, dh) for a in (kc, vc, ks, vs, kw, vw)]
    ks = rms_norm(ks, qk_g[1])
    kw = rms_norm(kw, qk_g[1])
    t = jnp.arange(s)

    n_cmp = (s - NSA_CMP_LEN) // NSA_CMP_STRIDE + 1
    cstart = np.arange(n_cmp) * NSA_CMP_STRIDE
    cidx = cstart[:, None] + np.arange(NSA_CMP_LEN)[None, :]

    def compress(a, j):
        blk = a[:, cidx] + cmp_pe[j][None, None, :, None, :]
        flat = jnp.moveaxis(blk, 3, 2).reshape(b, n_cmp, g, NSA_CMP_LEN * dh)
        return jax.nn.silu(flat @ cmp_w1[j]) @ cmp_w2[j]

    k_cmp = rms_norm(compress(kc, 0), qk_g[1])
    v_cmp = compress(vc, 1)
    cend = jnp.asarray(cstart + NSA_CMP_LEN - 1)
    mask_c = cend[None, :] <= t[:, None]
    bias_c = jnp.transpose(bias_tab[t5_bucket(t[:, None] - cend[None, :])], (2, 3, 0, 1))
    logits_c = jnp.einsum('bsgpd,bngd->bgpsn', q, k_cmp).astype(jnp.float32) * scale + bias_c
    p_c, _ = masked_softmax(logits_c, mask_c)
    o_c = jnp.einsum('bgpsn,bngd->bsgpd', p_c.astype(v_cmp.dtype), v_cmp)

    n_slc = s // NSA_SLC_BLOCK
    sstart = np.arange(n_slc) * NSA_SLC_BLOCK
    overlap = np.clip(np.minimum(cstart[:, None] + NSA_CMP_LEN, sstart[None, :] + NSA_SLC_BLOCK)
                      - np.maximum(cstart[:, None], sstart[None, :]), 0, None).astype(np.float32) / NSA_CMP_LEN
    imp = jnp.einsum('bgpsn,nm->bgsm', p_c, jnp.asarray(overlap))
    cur = t // NSA_SLC_BLOCK
    ids = jnp.arange(n_slc)[None, :]
    forced = (ids == 0) | (ids == cur[:, None]) | (ids == cur[:, None] - 1)
    score = jnp.where(forced, NSA_FORCED, jnp.where(ids <= cur[:, None], imp, NEG_INF))
    n_sel = min(NSA_SLC_TOP, n_slc)
    top_s, top_i = lax.top_k(score, n_sel)
    sel_ok = top_s > 0.5 * NEG_INF
    k_blk = jnp.transpose(ks.reshape(b, n_slc, NSA_SLC_BLOCK, g, dh), (0, 3, 1, 2, 4))
    v_blk = jnp.transpose(vs.reshape(b, n_slc, NSA_SLC_BLOCK, g, dh), (0, 3, 1, 2, 4))
    bi = jnp.arange(b)[:, None, None, None]
    gi = jnp.arange(g)[None, :, None, None]
    qbn = GATHER_Q_BLOCK

    def sel_block(blk):
        qs = blk * qbn
        qb = lax.dynamic_slice_in_dim(q, qs, qbn, axis=1)
        ib = lax.dynamic_slice_in_dim(top_i, qs, qbn, axis=2)
        okb = lax.dynamic_slice_in_dim(sel_ok, qs, qbn, axis=2)
        kg = k_blk[bi, gi, ib].reshape(b, g, qbn, n_sel * NSA_SLC_BLOCK, dh)
        vg = v_blk[bi, gi, ib].reshape(b, g, qbn, n_sel * NSA_SLC_BLOCK, dh)
        pos = (ib[..., None] * NSA_SLC_BLOCK + jnp.arange(NSA_SLC_BLOCK)).reshape(b, g, qbn, -1)
        dist = (qs + jnp.arange(qbn))[None, None, :, None] - pos
        mask = (jnp.repeat(okb, NSA_SLC_BLOCK, axis=-1) & (dist >= 0))[:, :, None]
        bias = jnp.moveaxis(bias_tab[t5_bucket(dist), gi], -1, 2)
        logits = jnp.einsum('bqgpd,bgqkd->bgpqk', qb, kg).astype(jnp.float32) * scale + bias
        pr, _ = masked_softmax(logits, mask)
        return jnp.einsum('bgpqk,bgqkd->bqgpd', pr.astype(vg.dtype), vg)

    o_s = from_blocks(lax.map(sel_block, jnp.arange(s // qbn)))

    o_w, _ = band_attn(q, kw, vw, bias_tab, NSA_WINDOW - 1, 1)

    gt = jax.nn.sigmoid(gate_logits.astype(jnp.float32)).reshape(b, s, g, p_, 3).astype(q.dtype)
    out = gt[..., 0:1] * o_c + gt[..., 1:2] * o_s + gt[..., 2:3] * o_w
    return out.reshape(b, s, NSA_HEADS * dh)

def dilated_mixer(q, k, v, qk_g, t5_bias):
    b, s = q.shape[:2]
    ng = len(DIL_PAIRS)
    q = rms_norm(q.reshape(b, s, ng, DIL_HPG, HEAD_DIM), qk_g[0])
    k = rms_norm(k.reshape(b, s, ng, DIL_HPG, HEAD_DIM), qk_g[1])
    v = v.reshape(b, s, ng, DIL_HPG, HEAD_DIM)
    outs, lses = [], []
    for gidx, (w, r) in enumerate(DIL_PAIRS):
        tab = t5_bias[:, gidx * DIL_HPG:(gidx + 1) * DIL_HPG][:, :, None]
        o, lse = band_attn(q[:, :, gidx, :, None], k[:, :, gidx], v[:, :, gidx], tab, w, r)
        outs.append(o[:, :, :, 0])
        lses.append(lse[..., 0])
    wts = jax.nn.softmax(jnp.stack(lses), axis=0)
    out = jnp.sum(wts[..., None].astype(q.dtype) * jnp.stack(outs), axis=0)
    return out.reshape(b, s, DIL_HPG * HEAD_DIM)

def moba_mixer(q, k, v, qk_g, bias_tab):
    b, s = q.shape[:2]
    h, dh = MOBA_HEADS, HEAD_DIM
    scale = dh ** -0.5
    q = rms_norm(q.reshape(b, s, h, dh), qk_g[0])
    k = rms_norm(k.reshape(b, s, h, dh), qk_g[1])
    v = v.reshape(b, s, h, dh)
    nb = -(-s // MOBA_BLOCK)
    pad = nb * MOBA_BLOCK - s
    kp = jnp.pad(k, ((0, 0), (0, pad), (0, 0), (0, 0)))
    vp = jnp.pad(v, ((0, 0), (0, pad), (0, 0), (0, 0)))
    k_blk = jnp.transpose(kp.reshape(b, nb, MOBA_BLOCK, h, dh), (0, 3, 1, 2, 4))
    v_blk = jnp.transpose(vp.reshape(b, nb, MOBA_BLOCK, h, dh), (0, 3, 1, 2, 4))
    t = jnp.arange(s)
    own = t // MOBA_BLOCK
    n_top = min(MOBA_TOP, nb - 1)
    if n_top > 0:
        k_mean = jnp.mean(k_blk.astype(jnp.float32), axis=3)
        gate = jnp.einsum('bshd,bhnd->bhsn', q.astype(jnp.float32), k_mean)
        past = jnp.arange(nb)[None, :] < own[:, None]
        top_s, top_i = lax.top_k(jnp.where(past, gate, NEG_INF), n_top)
        sel_ok = top_s > 0.5 * NEG_INF
    bi = jnp.arange(b)[:, None, None, None]
    hi = jnp.arange(h)[None, :, None, None]
    qbn = GATHER_Q_BLOCK

    def block(blk):
        qs = blk * qbn
        qb = lax.dynamic_slice_in_dim(q, qs, qbn, axis=1)
        qpos = qs + jnp.arange(qbn)
        ob = qs // MOBA_BLOCK
        ko = lax.dynamic_slice_in_dim(kp, ob * MOBA_BLOCK, MOBA_BLOCK, axis=1)
        vo = lax.dynamic_slice_in_dim(vp, ob * MOBA_BLOCK, MOBA_BLOCK, axis=1)
        d_own = qpos[:, None] - (ob * MOBA_BLOCK + jnp.arange(MOBA_BLOCK))[None, :]
        logits_own = (jnp.einsum('bqhd,bkhd->bhqk', qb, ko).astype(jnp.float32) * scale
                      + jnp.transpose(bias_tab[t5_bucket(d_own)], (2, 0, 1)))
        mask_own = jnp.broadcast_to(d_own >= 0, logits_own.shape)
        if n_top == 0:
            pr, _ = masked_softmax(logits_own, mask_own)
            return jnp.einsum('bhqk,bkhd->bqhd', pr.astype(vo.dtype), vo)
        ib = lax.dynamic_slice_in_dim(top_i, qs, qbn, axis=2)
        okb = lax.dynamic_slice_in_dim(sel_ok, qs, qbn, axis=2)
        nsel = n_top * MOBA_BLOCK
        kg = k_blk[bi, hi, ib].reshape(b, h, qbn, nsel, dh)
        vg = v_blk[bi, hi, ib].reshape(b, h, qbn, nsel, dh)
        pos = (ib[..., None] * MOBA_BLOCK + jnp.arange(MOBA_BLOCK)).reshape(b, h, qbn, nsel)
        logits_sel = (jnp.einsum('bqhd,bhqkd->bhqk', qb, kg).astype(jnp.float32) * scale
                      + bias_tab[t5_bucket(qpos[None, None, :, None] - pos), hi])
        mask_sel = jnp.repeat(okb, MOBA_BLOCK, axis=-1)
        pr, _ = masked_softmax(jnp.concatenate([logits_sel, logits_own], axis=-1),
                               jnp.concatenate([mask_sel, mask_own], axis=-1))
        pr = pr.astype(v.dtype)
        return (jnp.einsum('bhqk,bhqkd->bqhd', pr[..., :nsel], vg)
                + jnp.einsum('bhqk,bkhd->bqhd', pr[..., nsel:], vo))

    return from_blocks(lax.map(block, jnp.arange(s // qbn))).reshape(b, s, h * dh)

def even_mixer(y, w_in, w_out, q_norm_g, kv_norm_g, w_uq, w_ukv, mla_qk_g, cmp_pe, cmp_w1, cmp_w2, nsa_qk_g, t5_bias):
    cq, ckv, kr, qn, kc, vc, ks, vs, kw, vw, gl = split_cols(y @ w_in, EV_SPLITS)
    o_a = mla_mixer(cq, ckv, kr, q_norm_g, kv_norm_g, w_uq, w_ukv, mla_qk_g)
    tab = t5_bias[:, MLA_HEADS:MLA_HEADS + NSA_HEADS].reshape(NUM_BUCKETS, NSA_GROUPS, NSA_HPG)
    o_b = nsa_mixer(qn, kc, vc, ks, vs, kw, vw, gl, cmp_pe, cmp_w1, cmp_w2, nsa_qk_g, tab)
    return jnp.concatenate([o_a, o_b], axis=-1) @ w_out

def odd_mixer(y, w_in, w_out, dil_qk_g, moba_qk_g, t5_bias):
    qd, kd, vd, qm, km, vm = split_cols(y @ w_in, OD_SPLITS)
    o_c = dilated_mixer(qd, kd, vd, dil_qk_g, t5_bias)
    o_d = moba_mixer(qm, km, vm, moba_qk_g, t5_bias[:, DIL_SLOTS:DIL_SLOTS + MOBA_HEADS])
    return jnp.concatenate([o_c, o_d], axis=-1) @ w_out

def second_inputs(seed: int = 0) -> dict:
    key = jax.random.key(seed)
    keys = iter(jax.random.split(key, 32))

    def nrm(shape, scale):
        return jax.random.normal(next(keys), shape, jnp.float32) * scale

    return {
        'x': nrm((BATCH, SEQ, D_MODEL), 1.0),
        'c': nrm((BATCH, D_MODEL), 1.0),
        't5_bias': nrm((NUM_BUCKETS, HEAD_SLOTS), 0.5),
        'ada_w': nrm((DEPTH, D_MODEL, 9 * D_MODEL), D_MODEL ** -0.5),
        'ada_b': nrm((DEPTH, 9 * D_MODEL), 0.02),
        'norm_g': 1.0 + nrm((DEPTH, 3, D_MODEL), 0.05),
        'ffn_w_in': nrm((DEPTH, 2, D_MODEL, 2 * D_FF_2), D_MODEL ** -0.5),
        'ffn_w_out': nrm((DEPTH, 2, D_FF_2, D_MODEL), D_FF_2 ** -0.5),
        'ev_w_in': nrm((N_EVEN, D_MODEL, EV_COLS), D_MODEL ** -0.5),
        'ev_w_out': nrm((N_EVEN, EV_OUT, D_MODEL), EV_OUT ** -0.5),
        'mla_q_norm_g': 1.0 + nrm((N_EVEN, MLA_Q_LORA), 0.05),
        'mla_kv_norm_g': 1.0 + nrm((N_EVEN, MLA_KV_LORA), 0.05),
        'mla_w_uq': nrm((N_EVEN, MLA_Q_LORA, MLA_HEADS * (MLA_NOPE + MLA_ROPE)), MLA_Q_LORA ** -0.5),
        'mla_w_ukv': nrm((N_EVEN, MLA_KV_LORA, MLA_HEADS * (MLA_NOPE + MLA_V)), MLA_KV_LORA ** -0.5),
        'mla_qk_g': 1.0 + nrm((N_EVEN, 2, MLA_NOPE + MLA_ROPE), 0.05),
        'nsa_cmp_pe': nrm((N_EVEN, 2, NSA_CMP_LEN, HEAD_DIM), 0.1),
        'nsa_cmp_w1': nrm((N_EVEN, 2, NSA_CMP_LEN * HEAD_DIM, NSA_CMP_HID), (NSA_CMP_LEN * HEAD_DIM) ** -0.5),
        'nsa_cmp_w2': nrm((N_EVEN, 2, NSA_CMP_HID, HEAD_DIM), NSA_CMP_HID ** -0.5),
        'nsa_qk_g': 1.0 + nrm((N_EVEN, 2, HEAD_DIM), 0.05),
        'od_w_in': nrm((N_ODD, D_MODEL, OD_COLS), D_MODEL ** -0.5),
        'od_w_out': nrm((N_ODD, OD_OUT, D_MODEL), OD_OUT ** -0.5),
        'dil_qk_g': 1.0 + nrm((N_ODD, 2, HEAD_DIM), 0.05),
        'moba_qk_g': 1.0 + nrm((N_ODD, 2, HEAD_DIM), 0.05),
    }

def second_block(x, c, t5_bias, ada_w, ada_b, norm_g, ffn_w_in, ffn_w_out, ev_w_in, ev_w_out,
              mla_q_norm_g, mla_kv_norm_g, mla_w_uq, mla_w_ukv, mla_qk_g, nsa_cmp_pe, nsa_cmp_w1,
              nsa_cmp_w2, nsa_qk_g, od_w_in, od_w_out, dil_qk_g, moba_qk_g):
    b, d = x.shape[0], x.shape[-1]
    c_act = jax.nn.silu(c)
    for i in range(DEPTH):
        mod = (c_act @ ada_w[i] + ada_b[i]).reshape(b, 3, 3, d)
        y = modulate(x, norm_g[i, 0], mod[:, 0, 0], mod[:, 0, 1])
        x = x + 0.5 * mod[:, 0, 2][:, None, :] * swiglu(y, ffn_w_in[i, 0], ffn_w_out[i, 0])
        y = modulate(x, norm_g[i, 1], mod[:, 1, 0], mod[:, 1, 1])
        j = i // 2
        if i % 2 == 0:
            m = even_mixer(y, ev_w_in[j], ev_w_out[j], mla_q_norm_g[j], mla_kv_norm_g[j], mla_w_uq[j],
                           mla_w_ukv[j], mla_qk_g[j], nsa_cmp_pe[j], nsa_cmp_w1[j], nsa_cmp_w2[j],
                           nsa_qk_g[j], t5_bias)
        else:
            m = odd_mixer(y, od_w_in[j], od_w_out[j], dil_qk_g[j], moba_qk_g[j], t5_bias)
        x = x + mod[:, 1, 2][:, None, :] * m
        y = modulate(x, norm_g[i, 2], mod[:, 2, 0], mod[:, 2, 1])
        x = x + 0.5 * mod[:, 2, 2][:, None, :] * swiglu(y, ffn_w_in[i, 1], ffn_w_out[i, 1])
    return x


def setup_inputs(seed=0):
    out = dict(first_inputs(seed))
    for name, value in second_inputs(seed + 1).items():
        if name != "x":
            out[name + "_2"] = value
    return out


def reference(
    x, meta, a_w_in, a_conv_w, a_conv_b, a_w_r, a_b_r, a_w_i, a_b_i, a_lambda, a_w_out, kv_w,
    kv_f_b, b_w_in, b_w_out, f_w_in, f_conv_w, f_conv_b, f_w_out, ln1_g, ln1_b, ln2_g, ln2_b,
    c_2, t5_bias_2, ada_w_2, ada_b_2, norm_g_2, ffn_w_in_2, ffn_w_out_2, ev_w_in_2, ev_w_out_2,
    mla_q_norm_g_2, mla_kv_norm_g_2, mla_w_uq_2, mla_w_ukv_2, mla_qk_g_2, nsa_cmp_pe_2,
    nsa_cmp_w1_2, nsa_cmp_w2_2, nsa_qk_g_2, od_w_in_2, od_w_out_2, dil_qk_g_2, moba_qk_g_2,
):
    x = first_block(
        x, meta, a_w_in, a_conv_w, a_conv_b, a_w_r, a_b_r, a_w_i, a_b_i, a_lambda, a_w_out,
        kv_w, kv_f_b, b_w_in, b_w_out, f_w_in, f_conv_w, f_conv_b, f_w_out, ln1_g, ln1_b, ln2_g,
        ln2_b,
    )
    return second_block(
        x, c_2, t5_bias_2, ada_w_2, ada_b_2, norm_g_2, ffn_w_in_2, ffn_w_out_2, ev_w_in_2,
        ev_w_out_2, mla_q_norm_g_2, mla_kv_norm_g_2, mla_w_uq_2, mla_w_ukv_2, mla_qk_g_2,
        nsa_cmp_pe_2, nsa_cmp_w1_2, nsa_cmp_w2_2, nsa_qk_g_2, od_w_in_2, od_w_out_2, dil_qk_g_2,
        moba_qk_g_2,
    )


_drawn_inputs = setup_inputs


def setup_inputs(seed=0):
    import zlib

    import numpy as np

    out = dict(_drawn_inputs(seed))
    spreads = {}
    factors = {'a_conv_b': 2.803,
     'a_b_r': 8.0,
     'a_b_i': 8.0,
     'kv_f_b': 3.04,
     'f_conv_b': 6.01,
     'mla_q_norm_g_2': 8.0,
     'mla_kv_norm_g_2': 4.787,
     'mla_qk_g_2': 8.0,
     'nsa_cmp_pe_2': 3.775,
     'nsa_qk_g_2': 8.0,
     'dil_qk_g_2': 8.0,
     'moba_qk_g_2': 8.0}
    for name, (base, spread) in spreads.items():
        noise = np.random.default_rng([zlib.crc32(name.encode()), seed]).standard_normal(out[name].shape)
        drawn = base * np.exp(spread * noise) if base else spread * noise
        out[name] = jnp.asarray(drawn.astype(out[name].dtype))
    for name, factor in factors.items():
        out[name] = (out[name] * factor).astype(out[name].dtype)
    return out
```

```python
import math
import numpy as np
import concourse.bass as bass
from concourse import mybir
from contextlib import ExitStack

D = 1024
KC = D // 128
SEQ, META = 256, 16
T = SEQ + META
DEPTH = 2
D_RNN = 3 * D // 2
LRU = 96
NLRU = D_RNN // LRU
D_FF = 2816
NF = D_FF // 128
D_FF2 = 2752
KH = NF // 2
HEADS = 16
Q0 = META - 2
ALPHA = (2 * DEPTH) ** 0.25
LN_EPS, RMS_EPS = 1e-5, 1e-6
SLOT = 2048
ADA_T = 9 * D // 128
NEG = -1e30
PAR = {}


def column_plan():
    at = 0
    for name, width in [
        ("conv_a_w", 4 * NLRU), ("conv_a_b", NLRU), ("b_r", NLRU), ("b_i", NLRU), ("lam", NLRU),
        ("f_b", 1), ("c", KC),
        ("ln1_g", 16), ("ln1_b", 16), ("ln2_g", 16), ("ln2_b", 16),
        ("conv_f_w", 2 * 3 * 2 * NF), ("conv_f_b", 2 * 2 * NF),
        ("ada_b", 2 * ADA_T), ("norm_g", 2 * 3 * KC),
        ("mla_gq", 1), ("mla_gk", 1), ("mla_qn", 2), ("mla_kvn", 1),
        ("nsa_g", 2), ("dil_g", 2), ("moba_g", 2), ("cmp_pe", 32),
    ]:
        PAR[name] = (at, width)
        at += width
    return at


NPAR = column_plan()


class It:

    def __init__(self, k, j=None, step=0):
        self.k, self.j, self.step = k, j, step

    def of(self, base=0, div=1):
        n = (base + self.k) // div
        return n if self.j is None else self.j * (self.step // div) + n

    def next(self, n=1):
        return It(self.k + n, self.j, self.step)


def sweep(e, n, body, first, last, unroll):
    trips = (n - first - last) // unroll
    assert first + last + trips * unroll == n
    for k in range(first):
        body(It(k), k == 0, False)
    if trips == 1:
        for b in range(unroll):
            body(It(first + b), first + b == 0, False)
    elif trips:
        with e.Fori(0, trips) as j:
            for b in range(unroll):
                body(It(first + b, j, unroll), False, False)
    for k in range(n - last, n):
        body(It(k), k == 0, k == n - 1)


def wait(e, sem, value):
    if not isinstance(value, int) or value > 0:
        e.wait_ge(sem, value)


class Stage:

    def __init__(self, plan, n, cols, rows=128, per=1):
        self.n, self.cols, self.rows, self.per = n, cols, rows, per
        self.U = sum(s.n for s in plan)
        self.A = sum(s.groups for s in plan)
        self.groups = n // per if per else 0
        plan.append(self)


def stage_plan():
    plan, st = [], {}
    for name, spec in [
        ("a_in", (NLRU, 2 * KC * LRU)),
        ("a_out", (KC, NLRU * 128, LRU)),
        ("f_in0", (NF, 2 * KC * 128)),
        ("f_out0", (2 * KC, KH * 128, 128, 2)),
        ("fgate", (1, KC * 128)),
        ("kv", (KC, 2 * KC * 128)),
        ("qg", (KC, 2 * KC * 128)),
        ("b_out", (KC // 2, 2 * KC * 128)),
        ("f_in1", (NF, 2 * KC * 128)),
        ("f_out1", (2 * KC, KH * 128, 128, 2)),
        ("g_in0", (NF, 2 * KC * 128)),
        ("g_out0", (2 * KC, KH * 128, 128, 2)),
        ("ev_in", (8, 2 * KC * 128)),
        ("uq", (1, 2 * 8 * 96, 128, 0)),
        ("ukv", (1, 8 * 128, 128, 0)),
        ("cmp_w1", (4, 8 * 256, 128, 0)),
        ("ev_out", (KC // 2, 2 * KC * 128)),
        ("g_in1", (NF, 2 * KC * 128)),
        ("g_out1", (2 * KC, KH * 128, 128, 2)),
        ("g_in2", (NF, 2 * KC * 128)),
        ("g_out2", (2 * KC, KH * 128, 128, 2)),
        ("od_in", (12, 2 * KC * 128)),
        ("od_out", (KC // 2, 2 * 4 * 128)),
        ("g_in3", (NF, 2 * KC * 128)),
        ("g_out3", (2 * KC, KH * 128, 128, 2)),
    ]:
        st[name] = Stage(plan, *spec)
    return st


LRU_A, LRU_D = 13, 19
X, n = {}, 0
for name, count in [("a", KC), ("f0", KC), ("fox", KC), ("fox_o", KC), ("f1", KC), ("g0", KC), ("ev", KC),
                    ("ev_o", KC), ("g1", KC), ("g2", KC), ("od", KC), ("od_o", 4), ("g3", KC)]:
    X[name] = n
    n += count
NX = {"ln": lambda i: KC * i, "std": lambda i: i}
FORGET_STEPS = 8


def t5_buckets(dist):
    n = np.maximum(dist, 0)
    nf = np.maximum(n, 1).astype(np.float32)
    large = 16 + (np.log(nf / np.float32(16)) / np.float32(math.log(8)) * 16).astype(np.int32)
    return np.where(n < 16, n, np.minimum(large, 31))


def constants():
    f = np.float32
    c = {}
    c["ident"] = np.eye(128, dtype=f)
    p = np.arange(128)
    same64 = (p[:, None] // 64 == p[None, :] // 64)
    c["mean64"] = (same64 / 64).astype(f)
    m96 = np.zeros((128, 128), f)
    m96[:64, :64] = 1 / 64
    m96[64:96, 64:96] = 1 / 32
    c["mean96"] = m96
    rot = np.zeros((128, 128), f)
    for i in range(16):
        rot[64 + 16 + i, 64 + i] = -1
        rot[64 + i, 64 + 16 + i] = 1
    c["rot"] = rot
    inv = np.float32(10000.0) ** (-np.arange(0, 32, 2, dtype=f) / np.float32(32))
    ang = np.arange(SEQ, dtype=f)[:, None] * inv[None, :]
    cos, sin = np.cos(ang).T.astype(f), np.sin(ang).T.astype(f)
    tab = np.zeros((128, 4, SEQ), f)
    tab[:64, 0], tab[64:80, 0], tab[80:96, 0] = 1, cos, cos
    tab[64:80, 1], tab[80:96, 1] = sin, sin
    tab[:, 2:] = tab[:, :2] * f(96 ** -0.5)
    c["rope"] = tab.reshape(128, -1)
    k = np.arange(T)
    c["causal"] = np.where(k[None, :] <= SEQ // 2 + META + p[:, None], 0, NEG).astype(f)
    q = np.arange(2)
    small = np.where(np.arange(META)[None, :] <= Q0 + q[:, None], 0, NEG).astype(f)
    c["causal0"] = np.pad(small, ((0, 126), (0, 0)))
    x = np.arange(512)
    dist = 255 - x
    fam = []
    for keep in [dist >= 0, (dist >= 0) & (dist <= 128), (dist >= 0) & (dist % 4 == 0),
                 (dist >= 0) & (dist % 16 == 0)]:
        row = np.where(keep, t5_buckets(dist), 32)
        fam.append((np.arange(33)[:, None] == row[None, :]).astype(f))
    c["onehot"] = np.concatenate(fam, 1)
    n = np.arange(15)
    cend = 16 * n + 31
    dist = np.arange(SEQ)[None, :] - cend[:, None]
    row = np.where(dist >= 0, t5_buckets(dist), 32)
    c["onehot_c"] = (np.arange(33)[:, None, None] == row[None]).astype(f).reshape(33, -1)
    ok = (dist >= 0).T.reshape(2, 128, 15).transpose(1, 0, 2)
    c["mask_c"] = ok.astype(f).reshape(128, 30)
    return c


CONST = [("ident", 128), ("mean64", 128), ("mean96", 128), ("rot", 128), ("rope", 1024),
         ("causal", T), ("causal0", META), ("mask_c", 30)]


def pack(x):
    f = np.float32
    out = {}
    x = {k: np.asarray(v) for k, v in x.items()}
    h = np.concatenate([x["meta"], x["x"][0]], 0)
    out["h0"] = h.T.reshape(KC, 128, T).transpose(1, 0, 2)

    def two(w, a, b, m=128):
        v = w.reshape(-1, 128, w.shape[1])
        u = [np.stack([v[:, :, i:i + m], v[:, :, j:j + m]], 0) for i, j in zip(a, b)]
        return np.stack(u).transpose(0, 3, 1, 2, 4).reshape(len(u), 128, -1)

    w = x["a_w_in"][0]
    g = [LRU * i for i in range(NLRU)]
    out["a_in"] = two(w, g, [D_RNN + i for i in g], LRU)
    w = x["a_w_out"][0].reshape(NLRU, LRU, KC, 128)
    out["a_out"] = w.transpose(2, 1, 0, 3).reshape(KC, LRU, -1)
    wr, wi = x["a_w_r"][0], x["a_w_i"][0]
    ri = np.stack([wr, wi], 1).reshape(4, 4, 2, LRU, LRU)
    out["a_ri"] = ri.transpose(0, 3, 1, 2, 4).reshape(4, LRU, -1)
    ch = [128 * i for i in range(64)]

    def ffn_out(w):
        w = w.reshape(2, KH, 128, KC, 128)
        return w.transpose(3, 0, 2, 1, 4).reshape(2 * KC, 128, -1)

    for l in range(2):
        out[f"f_in{l}"] = two(x["f_w_in"][l], ch[:NF], [D_FF + i for i in ch[:NF]])
        out[f"f_out{l}"] = ffn_out(x["f_w_out"][l])
    kv = x["kv_w"]
    fg = np.pad(kv[:, 2 * D:], ((0, 0), (0, 112)))
    out["fgate"] = fg.reshape(KC, 128, 128).transpose(1, 0, 2).reshape(1, 128, -1)
    out["kv"] = two(kv, ch[:KC], ch[KC:2 * KC])
    out["qg"] = two(x["b_w_in"][0], ch[:KC], ch[KC:2 * KC])
    out["b_out"] = two(x["b_w_out"][0], ch[0:KC:2], ch[1:KC:2])
    pad = D_FF - D_FF2
    for n in range(4):
        w = x["ffn_w_in_2"][n // 2, n % 2]
        w = np.pad(w.reshape(D, 2, D_FF2), ((0, 0), (0, 0), (0, pad))).reshape(D, -1)
        out[f"g_in{n}"] = two(w, ch[:NF], [D_FF + i for i in ch[:NF]])
        out[f"g_out{n}"] = ffn_out(np.pad(x["ffn_w_out_2"][n // 2, n % 2], ((0, pad), (0, 0))))
    w = x["ev_w_in_2"][0]
    at = dict(cq=0, ckv=256, kr=384, qn=416, kc=928, vc=1056, ks=1184, vs=1312, kw=1440, vw=1568, gl=1696)
    z = lambda n: np.zeros((D, n), f)
    krgl = np.concatenate([z(64), w[:, 384:416], w[:, 1696:1720], z(8)], 1)
    dup = lambda a, g: np.concatenate([w[:, a + 64 * g:a + 64 * g + 64]] * 2, 1)
    chunks = [w[:, 0:128], w[:, 128:256], w[:, 256:384], krgl]
    chunks += [w[:, at["qn"] + 128 * i:at["qn"] + 128 * i + 128] for i in range(4)]
    chunks += [dup(at["ks"], 0), dup(at["ks"], 1), dup(at["kw"], 0), dup(at["kw"], 1)]
    chunks += [w[:, at[n]:at[n] + 128] for n in ("kc", "vc", "vs", "vw")]
    w = np.concatenate(chunks, 1)
    out["ev_in"] = two(w, ch[0:16:2], ch[1:16:2])
    out["uq"] = x["mla_w_uq_2"][0].reshape(2, 128, 768).transpose(1, 0, 2).reshape(1, 128, -1)
    out["ukv"] = x["mla_w_ukv_2"][0].reshape(1, 128, 1024)
    w = x["nsa_cmp_w1_2"][0].reshape(2, 2, 8, 128, 256)
    out["cmp_w1"] = w.transpose(0, 1, 3, 2, 4).reshape(4, 128, -1)
    w = x["nsa_cmp_w2_2"][0].reshape(2, 2, 128, 64)
    out["cmp_w2"] = np.concatenate([w, w], 3).transpose(2, 0, 1, 3).reshape(128, -1)
    out["ev_out"] = two(x["ev_w_out_2"][0], ch[0:KC:2], ch[1:KC:2])
    out["od_in"] = two(x["od_w_in_2"][0], ch[0:24:2], ch[1:24:2])
    out["od_out"] = two(x["od_w_out_2"][0], ch[0:KC:2], ch[1:KC:2])
    w = x["ada_w_2"].reshape(2, KC, 128, ADA_T, 128)
    out["ada"] = w.transpose(0, 3, 2, 1, 4).reshape(2, ADA_T, 128, -1)

    par = np.zeros((128, NPAR), f)

    def put(name, a, at=0):
        o, n = PAR[name]
        assert at + a.shape[1] <= n
        par[:a.shape[0], o + at:o + at + a.shape[1]] = a

    col = lambda v, m=128: np.asarray(v).reshape(-1, m).T
    put("conv_a_w", x["a_conv_w"][0].reshape(4, NLRU, LRU).transpose(2, 1, 0).reshape(LRU, -1))
    for n, s in (("conv_a_b", "a_conv_b"), ("b_r", "a_b_r"), ("b_i", "a_b_i"), ("lam", "a_lambda")):
        put(n, col(x[s][0], LRU))
    put("f_b", x["kv_f_b"][:, None])
    put("c", col(x["c_2"][0]))
    for n in ("ln1_g", "ln1_b", "ln2_g", "ln2_b"):
        put(n, col(x[n]))
    w = x["f_conv_w"].reshape(2, 3, 2 * NF, 128)
    put("conv_f_w", w.transpose(3, 0, 2, 1).reshape(128, -1))
    put("conv_f_b", col(x["f_conv_b"]))
    put("ada_b", col(x["ada_b_2"]))
    put("norm_g", col(x["norm_g_2"]))
    g = x["mla_qk_g_2"][0]
    put("mla_gq", g[0][:, None])
    put("mla_gk", g[1][:, None])
    put("mla_qn", col(x["mla_q_norm_g_2"][0]))
    put("mla_kvn", col(x["mla_kv_norm_g_2"][0]))
    for n in ("nsa", "dil", "moba"):
        g = x[n + "_qk_g_2"][0]
        put(n + "_g", np.concatenate([g, g], 1).T)
    pe = x["nsa_cmp_pe_2"][0].reshape(2, 16, 128)
    put("cmp_pe", pe.transpose(2, 0, 1).reshape(128, 32))
    out["par"] = par
    c = constants()
    out["const"] = np.concatenate([c[n] for n, _ in CONST if n != "rope"], 1)
    out["rope"] = c["rope"][:96]
    out["onehot"], out["onehot_c"] = c["onehot"], c["onehot_c"]
    out["t5"] = np.concatenate([x["t5_bias_2"], np.full((1, HEADS), NEG, f)], 0)
    return out


def build(nc, ap):
    f32, f32r = mybir.dt.float32, mybir.dt.float32r
    ACT, ALU, AX = mybir.ActivationFunctionType, mybir.AluOpType, mybir.AxisListType
    st = stage_plan()
    order = list(st.values())
    TW = SEQ + 128
    toeplitz = nc.dram_tensor("toeplitz", [20, 128, TW], f32, kind="Internal").ap()

    gate_rows = nc.dram_tensor("gate_rows", [4, HEADS, T], f32, kind="Internal").ap()

    CH = T * 4
    where = 16512

    def at(name, shape, dt, offset):
        return nc.alloc_sbuf_tensor_at(name, shape, dt, offset=offset)

    def sb(name, shape, dt=f32):
        nonlocal where
        t = at(name, shape, dt, where)
        size = 4 * math.prod(shape[1:])
        where += -(-size // 32) * 32
        return t

    raw = sb("raw", [128, 2, SLOT])
    whi = sb("whi", [128, 2, SLOT], f32r)
    wlo = sb("wlo", [128, 2, SLOT], f32r)
    res = sb("res", [128, KC, T])
    xhi = sb("xhi", [128, KC, T], f32r)
    xlo = sb("xlo", [128, KC, T], f32r)
    ada_w = sb("ada_w", [128, 2, KC, 128])
    ada_s = sb("ada_s", [128, ADA_T * 128])
    par = sb("par", [128, NPAR])
    const = sb("const_sb", [128, sum(n for c, n in CONST if c != "rope")])
    ones = sb("ones", [128, 128])
    one1 = sb("one1", [128, 1])
    eps = sb("eps", [128, 2])
    std = sb("std", [128, T])
    c_act = sb("c_act", [128, KC])
    mod = sb("mod", [128, 2, ADA_T])
    g8 = sb("g8", [128, 3])
    t5 = sb("t5_sb", [33, HEADS])
    bias_c = sb("bias_c", [128, 2, 8, 15])
    gs = sb("gs", [128, 2, 3 * KC])
    sp8 = sb("sp8", [LRU, NLRU])
    sq = sb("sq", [128, 2, T])
    small = sb("small", [128, 8, 2, 6])
    R0 = where
    W0 = R0 + 44 * CH
    assert W0 + 31616 <= nc.sbuf_usable_end

    hhi = at("hhi", [128, NF, T], f32r, R0)
    hlo = at("hlo", [128, NF, T], f32r, R0 + NF * CH)
    dev = at("dev", [128, KC, T], f32, R0)
    dsq = at("dsq", [128, KC, T], f32, R0 + KC * CH)
    w_ri = at("w_ri", [LRU, 4, 2, LRU], f32, R0 + 16 * CH)
    lam_t = at("lam_t", [LRU, 8, NLRU], f32, W0 + 30464)
    lg, lx, lr, li, la, lt, l2 = (at(n, [LRU, 4, T], f32, W0 + i * 4 * CH)
                                  for i, n in enumerate(("lg", "lx", "lr", "li", "la", "lt", "l2")))
    cg, cv, gg, hf = (at(n, [128, 2, T], f32, W0 + i * 2 * CH)
                      for i, n in enumerate(("cg", "cv", "gg", "hf")))

    z = at("z", [128, 44, T], f32, R0)
    vt = at("vt", [128, KC, 3, 128], f32, R0 + 32 * CH)
    c_lhs = at("c_lhs", [128, 4, T], f32r, W0)
    c_rhs = at("c_rhs", [128, 4, T], f32r, W0 + 4 * CH)
    early = at("early", [2, HEADS, 16], f32, W0 + 8704)
    early_t = at("early_t", [16, HEADS, 2], f32, W0 + 9728)
    early_m = at("early_m", [2, 3, HEADS], f32, W0 + 9856)
    ft = at("ft", [16, 9, T], f32, W0 + 10240)
    c_part = at("c_part", [16, 4, T], f32r, W0 + 20032)
    fr = at("fr", [16, T], f32, W0 + 24384)
    probs = at("probs", [128, 6, 416], f32, W0 + 16384)
    pt = at("pt", [128, 2, 384], f32, W0 + 26368)
    pt_small = at("pt_small", [16, 2, T], f32, W0 + 29440)

    q96 = at("q96", [96, 9, SEQ], f32, R0 + 16 * CH)
    kf = at("kf", [96, 8, SEQ], f32, R0 + 25 * CH)
    zkv = at("zkv", [128, 8, SEQ], f32, R0 + 33 * CH)
    w2_cmp = at("w2_cmp", [128, 2, 2, 128], f32, R0 + 41 * CH)
    a2 = at("a2", [128, 2, 2, SEQ], f32, R0 + 16 * CH)
    x2 = at("x2", [128, 2, 16, 2, 15], f32, R0 + 20 * CH)
    x2_hi = at("x2_hi", [128, 2, 16, 30], f32r, R0 + 24 * CH)
    x2_lo = at("x2_lo", [128, 2, 16, 30], f32r, R0 + 28 * CH)
    v_nsa = at("v_nsa", [128, 4, 128], f32, R0 + 32 * CH)
    hid = at("hid", [128, 2, 2, 30], f32, R0 + 34 * CH)
    v_cmp = at("v_cmp", [15, 2, 64], f32, R0 + 35 * CH)
    k_cmp = at("k_cmp", [128, 30], f32, R0 + 36 * CH)
    gates = at("gates", [128, 2, 24], f32, R0 + 37 * CH)
    v_odd = at("v_odd", [128, 8, 2, 128], f32, R0 + 24 * CH)
    rope = at("rope", [96, 4, SEQ], f32, W0)
    vm = at("vm", [128, 8, 2, 64], f32, W0 + 4096)
    bias_even = at("bias_even", [128, 8, SEQ], f32, W0 + 8192)
    bias_odd = at("bias_odd", [128, 16, SEQ], f32, W0)
    n_sq = at("n_sq", [128, 2, 512], f32, W0 + 16384)
    n_std = at("n_std", [128, 2, 512], f32, W0 + 20480)
    rot_t = at("rot_t", [96, 2, 512], f32, W0 + 24576)
    onehot = at("onehot", [33, 2048], f32, R0 + 22 * CH)
    onehot_c = at("onehot_c", [33, 15 * SEQ], f32, R0 + 22 * CH + 8192)
    t_rows = at("t_rows", [8, 4, 512], f32, R0)

    coff, o = {}, 0
    for name, n in CONST:
        if name != "rope":
            coff[name] = (o, n)
            o += n

    def con(name):
        o, n = coff[name]
        return const[:, o:o + n]

    ident = con("ident")

    def pcol(name, i, rows=128):
        o = PAR[name][0]
        return par[0:rows, o + i:o + i + 1] if isinstance(i, int) else par[0:rows, bass.ds(i + o, 1)]

    def chunk(t, i, t0=0, rows=128, n=1):
        if isinstance(i, int):
            return t[0:rows, i, t0:T] if n == 1 else t[0:rows, i:i + n, t0:T]
        v = t[0:rows, bass.ds(i, n), t0:T]
        return v.rearrange("p o t -> p (o t)") if n == 1 else v

    ctx = ExitStack()
    with ctx:
        ps = ctx.enter_context(nc.psum_tensor("ps", [128, 8, 512], f32))
        sems = {}

        def S(name):
            if name not in sems:
                sems[name] = ctx.enter_context(nc.semaphore(name))
            return sems[name]

        w_loaded = [S("w_loaded0"), S("w_loaded1")]
        w_hi, w_lo, w_used, acc_free = S("w_hi"), S("w_lo"), S("w_used"), S("acc_free")
        block = ctx.enter_context(nc.Block())

        def row(t, i):
            return t[i] if isinstance(i, int) else t[bass.ds(i, 1)].rearrange("o p c -> (o p) c")

        def after(s, it, last):
            if not last:
                return s, it.next()
            i = order.index(s) + 1
            return (order[i], It(0)) if i < len(order) else (None, None)

        class Head:
            pass

        def causal(tile, width):
            o = coff["causal"][0]
            return const[:, o + T - width:o + T]

        fox_steps = []
        for h in range(HEADS):
            j, b = h // 2, h % 2
            p = slice(64 * b, 64 * b + 64)
            r = slice(32 * (h // 4), 32 * (h // 4) + 4)
            s = Head()
            q, k = z[p, 16 + j, :], z[p, j, :]
            ca, cb = c_lhs[r, h % 4, :], c_rhs[r, h % 4, :]
            s.qk = [[(q[:, 16:144], k[:, 0:144]), (ca[:, 16:144], cb[:, 0:144])],
                    [(q[:, 144:T], k[:, 0:T]), (ca[:, 144:T], cb[:, 0:T])]]
            s.cols = [(0, 144), (144, 416)]
            s.bias = [causal(0, 144), causal(1, T)]
            s.turn = [(0, 16, 144, 0), (1, 160, 288, 128), (1, 288, 416, 256)]
            s.small = [(0, 0, 16, 0), (1, 144, 160, 128)]
            c = slice(64 * b, 64 * b + 64)
            s.pv = [(vt[0:16, j, 0, c], 1, 0, 258, 16, 0), (vt[:, j, 1, c], 0, 0, 256, 128, 2),
                    (vt[:, j, 2, c], 0, 256, 384, 128, 130)]
            s.rows, s.half, s.gate, s.mask, s.n_q, s.head = 128, b, None, None, T - Q0, h
            fox_steps.append(s)

        class Run:
            steps_before = pairs_before = 0

            def __init__(self, before, steps, groups, lag, x, t0, out_gate=None, first_pair=0):
                self.steps, self.lag, self.x, self.t0, self.out_gate = steps, lag, x, t0, out_gate
                self.B = before.B + len(before.steps) if before else 0
                self.P = before.P + before.n_pairs if before else 0
                self.first_pair = first_pair
                n = 0
                for size, in_chunk_end in groups:
                    for i in range(size):
                        s = steps[n + i]
                        s.group = list(range(n, n + size))
                        s.ends = i == size - 1
                    n += size
                self.pair_of, self.pair_end, p = [], {}, 0
                for i, s in enumerate(steps):
                    self.pair_of.append(p)
                    if i + 1 == len(steps) or (s.half == 1 and steps[i + 1].half == 0):
                        self.pair_end[i] = p
                        p += 1
                self.n_pairs = p
                for i, s in enumerate(steps):
                    head0 = i == 0 or steps[i - 1].half != s.half
                    headn = i + 1 == len(steps) or steps[i + 1].half != s.half
                    s.first_of_head, s.last_of_head = head0, headn

        fox = Run(None, fox_steps, [(1, 0)] * HEADS, 2, X["fox_o"], Q0, out_gate=24)
        def both(tile, width):
            return [causal(0, 128), causal(1, SEQ)]

        def seq_step(q, k, v, bias, half, gate=None):
            s = Head()
            s.qk = [[(q[:, 0:128], k[:, 0:128])], [(q[:, 128:SEQ], k[:, 0:SEQ])]]
            s.cols = [(0, 128), (128, 384)]
            s.bias = bias
            s.turn = [(0, 0, 128, 0), (1, 128, 256, 128), (1, 256, 384, 256)]
            s.small = []
            s.pv = [(v[0], 0, 0, 256, 128, 0), (v[1], 0, 256, 384, 128, 128)]
            s.half, s.gate, s.mask = half, gate, None
            return s

        def toeplitz_bias(t, i):
            return [t[:, i, 128:SEQ], t[:, i, :]]

        def zc(p, i):
            return z[p, i, META:T]

        halves = [slice(0, 64), slice(64, 128)]
        mla = Run(fox, [seq_step(q96[:, h, :], kf[:, h, :], [vm[:, h, 0, :], vm[:, h, 1, :]],
                                 [causal(0, 128), causal(1, SEQ)], h % 2) for h in range(8)],
                  [(1, 0)] * 8, 2, X["ev_o"], META)
        steps = []
        for h in range(8):
            g, b, p = h // 4, h % 2, halves[h % 2]
            q = zc(p, 4 + h // 2)
            c = slice(64 * g, 64 * g + 64)
            s = Head()
            kc = k_cmp[p, 15 * g:15 * g + 15]
            s.qk = [[(q[:, 0:128], kc)], [(q[:, 128:SEQ], kc)]]
            s.cols = [(0, 15), (16, 31)]
            s.bias = [bias_c[:, t, h, :] for t in range(2)]
            s.turn = [(0, 0, 15, 0), (1, 16, 31, 128)]
            s.small = []
            s.pv = [(v_cmp[0:15, g, :], 0, 0, 256, 15, 0)]
            s.half, s.gate = b, gates[:, :, 3 * h]
            s.mask = [con("mask_c")[:, 15 * t:15 * t + 15] for t in range(2)]
            steps.append(s)
            for i, kz in ((0, 8), (1, 10)):
                steps.append(seq_step(q, zc(p, kz + g), [v_nsa[:, 2 * i, c], v_nsa[:, 2 * i + 1, c]],
                                      toeplitz_bias(bias_even, h), b, gates[:, :, 3 * h + 1 + i]))
        nsa = Run(mla, steps, [(1, 0)] * 24, 2, X["ev_o"] + 4, META, first_pair=4)
        steps = []
        for s in range(4):
            for g in range(3):
                c, p = 2 * g + s // 2, halves[s % 2]
                steps.append(seq_step(zc(p, c), zc(p, 6 + c), [v_odd[:, c, t, p] for t in range(2)],
                                      toeplitz_bias(bias_odd, 4 * g + s), s % 2))
        for h in range(4):
            p = halves[h % 2]
            steps.append(seq_step(zc(p, 18 + h // 2), zc(p, 20 + h // 2),
                                  [v_odd[:, 6 + h // 2, t, p] for t in range(2)],
                                  toeplitz_bias(bias_odd, 12 + h), h % 2))
        odd = Run(nsa, steps, [(3, 0)] * 4 + [(1, 0)] * 4, 4, X["od_o"], META)

        class Norm:

            def __init__(self, src, n, sums, scale, outs, rows=128):
                self.src, self.n, self.sums, self.scale, self.outs, self.rows = src, n, sums, scale, outs, rows

        m64, m96 = con("mean64"), con("mean96")

        def gcol(name, i=0, rows=128):
            o = PAR[name][0] + i
            return par[0:rows, o:o + 1]

        def heads_norm(i, g, n=2):
            v = z[:, i:i + n, META:T]
            return Norm(v, n * SEQ, [(m64, 0, n * SEQ)], 1.0, [(v, g, v)])

        latent_norms = [
            Norm(z[:, 0:2, META:T], SEQ, [(ones[:, :], 0, SEQ), (ones[:, :], SEQ, 2 * SEQ)], D / 256,
                 [(z[:, i, META:T], gcol("mla_qn", i), z[:, i, META:T]) for i in range(2)]),
            Norm(z[:, 2, META:T], SEQ, [(ones[:, :], 0, SEQ)], D / 128,
                 [(z[:, 2, META:T], gcol("mla_kvn"), z[:, 2, META:T])])]
        mla_norms = [Norm(q96[:, 2 * i:2 * i + 2, :], 2 * SEQ, [(m96[0:96, 0:96], 0, 2 * SEQ)], 1.0,
                          [(q96[:, 2 * i:2 * i + 2, :], gcol("mla_gq", 0, 96), q96[:, 2 * i:2 * i + 2, :])], 96)
                     for i in range(4)]
        mla_norms.append(Norm(z[0:96, 3, META:T], SEQ, [(m96[0:96, 0:96], 0, SEQ)], 1.0,
                              [(z[0:96, 3, META:T], gcol("mla_gk", 0, 96), q96[:, 8, :])], 96))
        mla_norms += [Norm(zkv[0:64, 2 * i:2 * i + 2, :], 2 * SEQ, [(m96[0:64, 0:64], 0, 2 * SEQ)], 1.0,
                           [(zkv[0:64, 2 * i:2 * i + 2, :], gcol("mla_gk", 0, 64), kf[0:64, 2 * i:2 * i + 2, :])], 64)
                      for i in range(4)]
        nsa_norms = [heads_norm(4, g8[:, 0:1]), heads_norm(6, g8[:, 0:1]),
                     heads_norm(8, gcol("nsa_g", 1)), heads_norm(10, gcol("nsa_g", 1))]
        cmp_norms = [Norm(k_cmp[:, :], 30, [(m64, 0, 30)], 1.0, [(k_cmp[:, :], gcol("nsa_g", 1), k_cmp[:, :])])]
        odd_norms = [heads_norm(2 * i, g8[:, 1:2] if i < 3 else gcol("dil_g", 1)) for i in range(6)]
        odd_norms += [heads_norm(18, g8[:, 2:3]), heads_norm(20, gcol("moba_g", 1))]
        count = 0
        for lot in (latent_norms, mla_norms, nsa_norms, cmp_norms, odd_norms):
            for item in lot:
                item.i = count
                count += 1

        @block.sync
        def _(e):
            e.dma_start(res[:, :, :], ap["h0"]).then_inc(S("h0_in"), 16)
            e.dma_start(par[:, :], ap["par"]).then_inc(S("par_in"), 16)
            e.dma_start(const[:, :], ap["const"]).then_inc(S("const_in"), 16)

            def load(s, it, name):
                slot, c, src = (s.U + it.k) % 2, s.cols // 2, row(ap[name], it.of())
                e.wait_ge(w_lo, it.of(s.U) + 1)
                for h in range(2):
                    e.dma_start(raw[0:s.rows, slot, h * c:(h + 1) * c], src[:, h * c:(h + 1) * c])\
                        .then_inc(w_loaded[slot], 16)

            def bias_rows(to, n, row):
                e.dma_start(to, bass.AP(toeplitz.tensor, row * 128 * TW + 127, [[TW - 1, 128], [128 * TW, n], [1, SEQ]]))\
                    .then_inc(S("bias_in"), 16)

            def sp_even():
                e.wait_ge(S("h_lo"), 3 * NF)
                e.dma_start(rope[:, :, :].rearrange("p a b -> p (a b)"), ap["rope"]).then_inc(S("rope_in"), 16)

            def sp_nsa():
                e.wait_ge(S("pv_mm"), mla.B + 8)
                for g in range(2):
                    for j in range(2):
                        src = z[64 * g:64 * g + 64, 12 + j, :]
                        e.dma_start(a2[0:64, j, g, :], src[:, META:T]).then_inc(S("a2_in"), 16)
                        e.dma_start(a2[64:128, j, g, 0:SEQ - 1], src[:, META + 1:T]).then_inc(S("a2_in"), 16)

            def sp_forget():
                e.wait_ge(S("forget_step"), FORGET_STEPS)
                e.dma_start(gate_rows.rearrange("c h t -> h c t"), c_part[:, :, :].bitcast(f32))\
                    .then_inc(S("gates_out"), 16)
                e.wait_ge(S("gates_out"), 16)
                for to, row0, part in ((c_lhs, 0, 0), (c_lhs, 1, 1), (c_rhs, 2, 2), (c_rhs, 3, 3)):
                    e.dma_start(to[row0:128:32, :, :].bitcast(f32),
                                gate_rows[part].rearrange("(q h) t -> q h t", q=4)).then_inc(S("forget_in"), 16)

            for name, s in st.items():
                if name == "a_in":
                    def group(it, first, last):
                        for b in range(4):
                            load(s, It(4 * it.k + b, it.j, 4), name)
                            if b == 0:
                                e.wait_ge(S("ri_mm"), it.of() * 4 + 1)
                                e.dma_start(w_ri[:, :, :, :].rearrange("p a b c -> p (a b c)"),
                                            row(ap["a_ri"], it.of())).then_inc(S("ri_in"), 16)
                    sweep(e, 4, group, 1, 1, 1)
                elif name == "cmp_w1":
                    for u in range(4):
                        if u == 3:
                            sp_nsa()
                        load(s, It(u), name)
                else:
                    sweep(e, s.n, lambda it, a, b: load(s, it, name), s.n % 2, 0, 2)
                if name == "g_out0":
                    sp_even()
                if name == "ev_in":
                    e.wait_ge(acc_free, s.A + 3)
                    e.dma_start(w2_cmp[:, :, :, :].rearrange("p a b c -> p (a b c)"), ap["cmp_w2"])\
                        .then_inc(S("w2_in"), 16)
                    bias_rows(bias_even[:, 0:4, :], 4, 16)
                    bias_rows(bias_even[:, 4:8, :], 4, 12)
                if name == "od_in":
                    bias_rows(bias_odd[:, :, :], 16, 0)
                if name == "qg":
                    sp_forget()
            e.wait_ge(acc_free, order[-1].A + order[-1].groups + 2)
            e.dma_start(ap["out"], res[:, :, META:T]).then_inc(S("stored"), 16)
            e.wait_ge(S("stored"), 16)

        @block.gpsimd
        def _(e):
            e.memset(ones[:, :], 1.0 / D).then_inc(S("consts_set"), 1)
            e.memset(one1[:, :], 1.0).then_inc(S("consts_set"), 1)
            e.memset(eps[:, 0:1], LN_EPS).then_inc(S("consts_set"), 1)
            e.memset(eps[:, 1:2], RMS_EPS).then_inc(S("consts_set"), 1)
            e.dma_start(onehot[:, :], ap["onehot"]).then_inc(S("onehot_in"), 16)
            e.dma_start(onehot_c[:, :], ap["onehot_c"]).then_inc(S("onehot_in"), 16)
            e.dma_start(t5[:, :], ap["t5"]).then_inc(S("onehot_in"), 16)
            e.wait_ge(S("t5_out"), 1)
            for to, i, a, n in ((0, 1, 0, 4), (4, 2, 0, 4), (8, 3, 0, 4), (12, 0, 4, 4), (16, 0, 0, 4)):
                e.dma_start(toeplitz[to:to + n], t_rows[a:a + n, i, 0:TW].unsqueeze(1).broadcast_to([n, 128, TW])).then_inc(S("toeplitz_out"), 16)
            e.wait_ge(S("c_act"), 1)
            step = S("ada_step")

            def load(layer, i, b):
                e.dma_start(ada_w[:, b, :, :].rearrange("p k c -> p (k c)"), row(ap["ada"][layer], i))\
                    .then_inc(S(f"ada_in{b}"), 16)

            for layer in range(2):
                def tile(it, first, last):
                    b, n = it.k % 2, it.of(layer * ADA_T) * 4
                    w = ada_w[:, b, :, :]
                    e.wait_ge(S(f"ada_in{b}"), it.of(layer * ADA_T, 2) * 16 + 16)
                    e.tensor_tensor(w, w, c_act[:, :].unsqueeze(2).broadcast_to([128, KC, 128]), ALU.mult)\
                        .then_inc(step, 1)
                    e.wait_ge(step, n + 1)
                    e.tensor_tensor(w[:, 0:4], w[:, 0:4], w[:, 4:8], ALU.add).then_inc(step, 1)
                    e.wait_ge(step, n + 2)
                    e.tensor_tensor(w[:, 0:2], w[:, 0:2], w[:, 2:4], ALU.add).then_inc(step, 1)
                    e.wait_ge(step, n + 3)
                    i = it.of()
                    to = ada_s[:, 128 * i:128 * i + 128] if isinstance(i, int) else ada_s[:, bass.ds(i * 128, 128)]
                    e.tensor_tensor(to, w[:, 0], w[:, 1], ALU.add).then_inc(step, 1)
                    if not (isinstance(i, int) and i >= ADA_T - 2):
                        e.wait_ge(step, n + 4)
                        load(layer, it.of(2), b)

                if layer:
                    e.wait_ge(step, 4 * ADA_T)
                load(layer, 0, 0)
                load(layer, 1, 1)
                if layer:
                    e.wait_ge(S("mod_mm"), 1)
                sweep(e, ADA_T, tile, 0, 2, 2)

        @block.tensor
        def _(e):
            e.nop().then_inc(w_used, 2)
            e.nop().then_inc(S("ri_mm"), 1)
            e.wait_ge(S("consts_set"), 4)

            def mm3(out, s, slot, off, m, hi, lo, start, stop):
                k = s.rows
                e.matmul(out, whi[0:k, slot, off:off + m], hi, start=start, stop=False)
                e.matmul(out, whi[0:k, slot, off:off + m], lo, start=False, stop=False)
                return e.matmul(out, wlo[0:k, slot, off:off + m], hi, start=False, stop=stop)

            def in_unit(s, it, t0, m=128, halves=2, x_from=None):
                slot, acc = (s.U + it.k) % 2, (s.A + it.k) % 2
                e.wait_ge(w_lo, it.of(s.U) + 3)
                e.wait_ge(acc_free, it.of(s.A) + 1)
                for half in range(halves):
                    for k in range(KC):
                        if half == 0 and x_from is not None:
                            e.wait_ge(S("x"), x_from + k + 1)
                        o = mm3(ps[0:m, 2 * acc + half, 0:T - t0], s, slot, (half * KC + k) * m, m,
                                xhi[:, k, t0:T], xlo[:, k, t0:T], k == 0, k == KC - 1)
                o.then_inc(w_used, 1)

            def stage_in(name, t0, x_from, halves=2):
                s = st[name]
                sweep(e, s.n, lambda it, first, last: in_unit(s, it, t0, 128, halves, x_from if first else None),
                      1 if s.n % 2 else 2, 0, 2)

            def column_sums(src, n, m, sem, start=None, stop=None):
                e.matmul(ps[:, 7, 0:n], ones[:, :], src, start=isinstance(m, int) and m == 0,
                         stop=isinstance(m, int) and m == KC - 1).then_inc(S(sem), 1)

            def stage_out(name, hi, lo, t0, chunks, ready, ln=None, rms=None):
                s = st[name]
                n, n_m, rows = T - t0, KC * s.per // s.n, s.rows
                kk = chunks // s.per

                def sums(g, parity):
                    for h in range(n_m):
                        m = g * n_m + h
                        if ln is not None:
                            e.wait_ge(acc_free, g + (s.A + 3))
                            column_sums(chunk(res, m, t0), n, m, "mean_mm")
                        else:
                            e.wait_ge(S("sq"), m + (KC * rms + 1))
                            column_sums(sq[:, (n_m * parity + h) % 2, t0:T], n, m, "sq_mm")

                def unit(it, first, last):
                    slot, g, part = (s.U + it.k) % 2, it.k // s.per, it.k % s.per
                    acc = (s.A + g) % 2
                    e.wait_ge(w_lo, it.of(s.U) + 3)
                    if part == 0:
                        e.wait_ge(acc_free, it.of(0, s.per) + (s.A + 1))
                    if it.k in ready and it.j is None:
                        e.wait_ge(*ready[it.k])
                    for half in range(n_m):
                        for k in range(kk):
                            kx = part * kk + k
                            o = mm3(ps[:, 2 * acc + half, 0:n], s, slot, (half * kk + k) * 128, 128,
                                    hi[0:rows, kx, t0:T], lo[0:rows, kx, t0:T], kx == 0, kx == chunks - 1)
                    o.then_inc(w_used, 1)
                    if part == s.per - 1 and not (it.j is None and g == 0) and not (ln is None and rms is None):
                        sums(it.of(0, s.per) - 1, (g - 1) % 2)
                sweep(e, s.n, unit, 2 * s.per, 0, 2 * s.per)
                if not (ln is None and rms is None):
                    sums(s.n // s.per - 1, (s.n // s.per - 1) % 2)

            def variance(i, t0):
                for k in range(KC):
                    e.wait_ge(S("dsq"), KC * i + k + 1)
                    e.matmul(ps[:, 6, 0:T - t0], ones[:, :], dsq[:, k, t0:T], start=k == 0, stop=k == KC - 1)\
                        .then_inc(S("var_mm"), 1)

            def attention(run):
                n, lag = len(run.steps), run.lag

                def scores(i):
                    s, g = run.steps[i], run.B + i
                    wait(e, S("scored"), g - 1)
                    for tile in range(2):
                        terms = s.qk[tile]
                        for t, (q, k) in enumerate(terms):
                            c0, c1 = s.cols[tile]
                            o = e.matmul(ps[:, 4 + g % 2, c0:c1], q, k, start=t == 0, stop=t == len(terms) - 1)
                    o.then_inc(S("qk_mm"), 1)

                def turn(i):
                    s, g = run.steps[i], run.B + i
                    e.wait_ge(S("prob"), g + 1)
                    wait(e, S("turned"), g - 1)
                    p = probs[:, g % 6, :]
                    for tile, a, b, to in s.small:
                        e.matmul(ps[0:b - a, 2 + g % 2, to:to + 128], p[:, a:b], ident, start=True, stop=True)
                    for tile, a, b, to in s.turn:
                        if b - a == 128:
                            o = e.transpose(ps[:, 6 + g % 2, to:to + 128], p[:, a:b], ident)
                        else:
                            o = e.matmul(ps[0:b - a, 6 + g % 2, to:to + 128], p[:, a:b], ident, start=True, stop=True)
                    o.then_inc(S("turn_mm"), 1)

                def values(i):
                    s, g, pair = run.steps[i], run.B + i, run.P + run.pair_of[i]
                    e.wait_ge(S("turned"), g + 1)
                    if s.first_of_head and s.half == 0:
                        wait(e, S("o_out"), pair - 1)
                    out = ps[64 * s.half:64 * s.half + 64, pair % 2, :]
                    for t, (v, small, a, b, keys, to) in enumerate(s.pv):
                        src = (pt_small if small else pt)[0:keys, g % 2, a:b]
                        o = e.matmul(out[:, to:to + b - a], v, src, start=s.first_of_head and t == 0,
                                     stop=s.last_of_head and t == len(s.pv) - 1)
                    o.then_inc(S("pv_mm"), 1)

                for t in range(n + lag + 1):
                    if t < n:
                        scores(t)
                    if 0 <= t - lag < n:
                        turn(t - lag)
                    if 0 <= t - lag - 1:
                        values(t - lag - 1)

            def pe_fox():
                kv, qg = st["kv"], st["qg"]
                e.wait_ge(acc_free, kv.A + kv.n + 2)
                e.wait_ge(S("const_in"), 16)
                for j in range(KC):
                    wait(e, S("vt"), j - 1)
                    v, b = z[:, 8 + j, :], 6 + j % 2
                    e.transpose(ps[:, b, 0:128], v[:, 16:144], ident)
                    e.transpose(ps[:, b, 128:256], v[:, 144:T], ident)
                    e.matmul(ps[0:16, b, 256:384], v[:, 0:16], ident, start=True, stop=True).then_inc(S("vt_mm"), 1)
                e.wait_ge(acc_free, qg.A + qg.n + 2)
                e.wait_ge(S("forget_in"), 16 * 4)
                for h in range(HEADS):
                    s, r = fox_steps[h], slice(32 * (h // 4), 32 * (h // 4) + 4)
                    q, k = z[64 * (h % 2):64 * (h % 2) + 64, 16 + h // 2, :], z[64 * (h % 2):64 * (h % 2) + 64, h // 2, :]
                    o = ps[0:2, 2, 16 * h:16 * h + 16]
                    wait(e, S("early_mm"), h)
                    e.matmul(o, q[:, Q0:16], k[:, 0:16], start=True, stop=False)
                    e.matmul(o, c_lhs[r, h % 4, Q0:16].bitcast(f32), c_rhs[r, h % 4, 0:16].bitcast(f32),
                             start=False, stop=True).then_inc(S("early_mm"), 1)
                e.wait_ge(S("early"), 4)
                for h in range(HEADS):
                    e.matmul(ps[0:16, 3, 2 * h:2 * h + 2], early[:, h, :], ident[0:2, 0:2], start=True, stop=True)\
                        .then_inc(S("early_mm"), 1)
                e.wait_ge(S("early_t"), 1)
                attention(fox)

            def norms(items):
                for it in items:
                    e.wait_ge(S("n_sq"), it.i + 1)
                    wait(e, S("n_std"), it.i - 1)
                    r = it.rows
                    for t, (m, a, b) in enumerate(it.sums):
                        o = e.matmul(ps[0:r, 4 + it.i % 2, 0:b - a], m, n_sq[0:r, it.i % 2, a:b],
                                     start=t == 0, stop=t == len(it.sums) - 1)
                    o.then_inc(S("n_mm"), 1)

            def modulation(l):
                e.wait_ge(S("ada_step"), 4 * ADA_T * (l + 1))
                for j in range(ADA_T):
                    o = e.matmul(ps[:, 6, j:j + 1], ada_s[:, 128 * j:128 * j + 128], one1[:, :], start=True, stop=True)
                o.then_inc(S("mod_mm"), 1)

            def swiglu(i, x):
                f = NF * (2 + i)
                stage_in(f"g_in{i}", META, x)
                stage_out(f"g_out{i}", hhi, hlo, META, NF, {0: (S("h_lo"), f + KH), 1: (S("h_lo"), f + NF)},
                          rms=[1, 3, 4, None][i])
                if i == 1:
                    modulation(1)

            def pe_even():
                stage_in("ev_in", META, X["ev"])
                s = st["ev_in"]
                e.wait_ge(acc_free, s.A + s.n + 2)
                norms(latent_norms)
                e.wait_ge(S("latent"), 3)
                s = st["uq"]
                e.wait_ge(w_lo, s.U + 3)
                for h in range(8):
                    for k in range(2):
                        o = mm3(ps[0:96, h // 2, SEQ * (h % 2):SEQ * (h % 2) + SEQ], s, s.U % 2, k * 768 + h * 96, 96,
                                xhi[:, k, META:T], xlo[:, k, META:T], k == 0, k == 1)
                o.then_inc(w_used, 1)
                s = st["ukv"]
                e.wait_ge(w_lo, s.U + 3)
                e.wait_ge(S("q_out"), 4)
                for h in range(8):
                    o = mm3(ps[:, h // 2, SEQ * (h % 2):SEQ * (h % 2) + SEQ], s, s.U % 2, h * 128, 128,
                            xhi[:, 2, META:T], xlo[:, 2, META:T], True, True)
                o.then_inc(w_used, 1)
                norms(mla_norms[0:5])
                for i in range(5):
                    n = 512 if i < 4 else SEQ
                    src = q96[:, 2 * i:2 * i + 2, :] if i < 4 else q96[:, 8, :]
                    e.wait_ge(S("n_out"), mla_norms[i].i + 1)
                    wait(e, S("rotated"), i - 1)
                    e.matmul(ps[0:96, 6 + i % 2, 0:n], con("rot")[0:96, 0:96], src, start=True, stop=True)\
                        .then_inc(S("rot_mm"), 1)
                norms(mla_norms[5:])
                e.wait_ge(S("kv_out"), 4)
                for h in range(8):
                    for t in range(2):
                        c = (2 * (h % 4) + t) * 64
                        o = e.transpose(ps[:, h // 4, c:c + 64], zkv[64:128, h, 128 * t:128 * t + 128],
                                        ident[64:128, 64:128])
                o.then_inc(S("vm_mm"), 1)
                e.wait_ge(S("vm"), 1)
                e.wait_ge(S("k_rope"), 1)
                e.wait_ge(S("n_out"), mla_norms[-1].i + 1)
                attention(mla)
                norms(nsa_norms)
                e.wait_ge(S("o_out"), mla.P + 4)
                for i in range(2):
                    for t in range(2):
                        e.transpose(ps[:, 2, 128 * (2 * i + t):128 * (2 * i + t) + 128],
                                    z[:, 14 + i, META + 128 * t:META + 128 * t + 128], ident)
                for t in range(2):
                    o = e.transpose(ps[:, 3, 128 * t:128 * t + 128], z[:, 3, META + 128 * t:META + 128 * t + 128], ident)
                o.then_inc(S("vn_mm"), 1)
                e.wait_ge(S("vn"), 1)
                e.wait_ge(S("x2"), 1)
                s = st["cmp_w1"]
                for j in range(2):
                    for part in range(2):
                        u = s.U + 2 * j + part
                        e.wait_ge(w_lo, u + 3)
                        for m in range(2):
                            for k in range(8):
                                i = 8 * part + k
                                o = mm3(ps[:, 2 * j + m, 0:30], s, u % 2, k * 256 + m * 128, 128,
                                        x2_hi[:, j, i, :], x2_lo[:, j, i, :], i == 0, i == 15)
                        o.then_inc(w_used, 1)
                e.wait_ge(S("hid"), 4)
                e.wait_ge(S("w2_in"), 16)
                for m in range(2):
                    e.matmul(ps[:, 0, 0:30], w2_cmp[:, 0, m, :], hid[:, 0, m, :], start=m == 0, stop=m == 1)
                for g in range(2):
                    for m in range(2):
                        o = e.matmul(ps[0:15, 1, 64 * g:64 * g + 64], hid[:, 1, m, 15 * g:15 * g + 15],
                                     w2_cmp[:, 1, m, 0:64], start=m == 0, stop=m == 1)
                o.then_inc(S("cmp_mm"), 1)
                norms(cmp_norms)
                e.wait_ge(S("n_out"), cmp_norms[0].i + 1)
                e.wait_ge(S("bias_in"), 32)
                attention(nsa)

            def pe_odd():
                stage_in("od_in", META, X["od"])
                s = st["od_in"]
                e.wait_ge(acc_free, s.A + s.n + 2)
                norms(odd_norms)
                for c in range(8):
                    src = z[:, 12 + c if c < 6 else 16 + c, META:T]
                    for t in range(2):
                        o = e.transpose(ps[:, c // 2, 256 * (c % 2) + 128 * t:256 * (c % 2) + 128 * t + 128],
                                        src[:, 128 * t:128 * t + 128], ident)
                    if c % 2:
                        o.then_inc(S("vo_mm"), 1)
                e.wait_ge(S("vo"), 4)
                e.wait_ge(S("bias_in"), 48)
                e.wait_ge(S("n_out"), odd_norms[-1].i + 1)
                attention(odd)

            def pe_second():
                for k in range(KC):
                    e.wait_ge(S("sq"), k + 1)
                    column_sums(sq[:, k % 2, META:T], SEQ, k, "sq_mm")
                modulation(0)
                swiglu(0, X["g0"])
                pe_even()
                stage_out("ev_out", xhi, xlo, META, KC, {0: (S("x"), X["ev_o"] + KC)}, rms=2)
                for i, x in ((1, "g1"), (2, "g2")):
                    swiglu(i, X[x])
                pe_odd()
                stage_out("od_out", xhi, xlo, META, 4, {0: (S("x"), X["od_o"] + 4)}, rms=5)
                swiglu(3, X["g3"])

            e.wait_ge(S("onehot_in"), 48)
            for i, (head, n) in enumerate(((8, 8), (0, 4), (4, 4), (8, 4))):
                o = e.matmul(ps[0:n, 4 + i, :], t5[:, head:head + n], onehot[:, 512 * i:512 * i + 512],
                             start=True, stop=True)
            o.then_inc(S("t5_mm"), 1)
            for t in range(2):
                for k in range(15):
                    c = (15 * t + k) * 8
                    o = e.matmul(ps[:, 0, c:c + 8], onehot_c[:, k * SEQ + 128 * t:k * SEQ + 128 * t + 128],
                                 t5[:, 8:16], start=True, stop=True)
            o.then_inc(S("t5_mm"), 1)
            e.wait_ge(S("t5_out"), 2)

            s = st["a_in"]

            def group(it, first, last):
                for b in range(4):
                    in_unit(s, It(4 * it.k + b, it.j, 4), 0, LRU, 2, 0 if first and b == 0 else None)
                e.wait_ge(S("ri_in"), it.of() * 16 + 16)
                for b in range(4):
                    e.wait_ge(acc_free, it.of() * 4 + (s.A + b + 3))
                    if b > 1:
                        e.wait_ge(S("lru_a"), it.of() * LRU_A + (4 + b - 1))
                    for r in range(2):
                        o = e.matmul(ps[0:LRU, 4 + 2 * (b % 2) + r, 0:T], w_ri[:, b, r, :], lx[:, b, :],
                                     start=True, stop=True)
                    o.then_inc(S("ri_mm"), 1)
            sweep(e, 4, group, 1, 1, 1)
            stage_out("a_out", hhi, hlo, 0, NLRU, {0: (S("lru_d"), 4 * LRU_D)}, ln=0)
            variance(0, 0)
            for l, t0 in ((0, 0), (1, Q0)):
                if l:
                    stage_in("fgate", 0, X["fox"], 1)
                    stage_in("kv", 0, None)
                    stage_in("qg", Q0, None)
                    pe_fox()
                    stage_out("b_out", xhi, xlo, Q0, KC, {0: (S("x"), X["fox_o"] + KC)}, ln=2)
                    variance(2, Q0)
                stage_in(f"f_in{l}", t0, X[f"f{l}"])
                f = NF * l
                stage_out(f"f_out{l}", hhi, hlo, t0, NF, {0: (S("h_lo"), f + KH), 1: (S("h_lo"), f + NF)},
                          ln=2 * l + 1)
                variance(2 * l + 1, t0)
            pe_second()

        @block.scalar
        def _(e):
            def split(s, it):
                if s is None:
                    return
                slot = (s.U + it.k) % 2
                e.wait_ge(w_loaded[slot], it.of(s.U, 2) * 32 + 32)
                e.wait_ge(w_used, it.of(s.U) + 1)
                e.activation(whi[0:s.rows, slot, 0:s.cols], raw[0:s.rows, slot, 0:s.cols], ACT.Copy)\
                    .then_inc(w_hi, 1)

            act = lambda *a, **k: e.activation(*a, **k)

            def log1p_exp(ez, nax, lw, w, base):
                e.wait_ge(S("lp_d"), base[0] + 1)
                act(ez, nax, ACT.Exp).then_inc(S("lp_a"), 1)
                e.wait_ge(S("lp_d"), base[0] + 2)
                act(lw, w, ACT.Ln).then_inc(S("lp_a"), 1)

            e.wait_ge(S("par_in"), 16)
            act(c_act[:, :], par[:, PAR["c"][0]:PAR["c"][0] + KC], ACT.Silu).then_inc(S("c_act"), 1)
            log1p_exp(lam_t[:, 1], lam_t[:, 0], lam_t[:, 3], lam_t[:, 2], (0, 0))
            e.wait_ge(S("h0_in"), 16)
            for k in range(KC):
                act(xhi[:, k, :], res[:, k, :], ACT.Copy).then_inc(S("x_hi"), 1)

            s = st["a_in"]
            split(s, It(0))

            def group(it, first, last):
                a, d, g = it.of() * LRU_A, it.of() * LRU_D, it.of()
                step = S("lru_a")
                for b in range(4):
                    u = It(4 * it.k + b, it.j, 4)
                    acc = (s.A + b) % 2
                    split(*after(s, u, last and b == 3))
                    e.wait_ge(w_used, u.of(s.U) + 3)
                    if not first:
                        e.wait_ge(S("lru_d"), d)
                    act(lg[:, b, :], ps[0:LRU, 2 * acc, 0:T], ACT.Copy)
                    act(lx[:, b, :], ps[0:LRU, 2 * acc + 1, 0:T], ACT.Identity,
                        bias=pcol("conv_a_b", g * 4 + b, LRU), scale=pcol("conv_a_w", g * 16 + (4 * b + 3), LRU))\
                        .then_inc(step, 1)
                for b in range(4):
                    e.wait_ge(S("ri_mm"), g * 4 + (b + 2))
                    act(lr[:, b, :], ps[0:LRU, 4 + 2 * (b % 2), 0:T], ACT.Sigmoid, bias=pcol("b_r", g * 4 + b, LRU))
                    act(li[:, b, :], ps[0:LRU, 5 + 2 * (b % 2), 0:T], ACT.Sigmoid, bias=pcol("b_i", g * 4 + b, LRU))\
                        .then_inc(step, 1)
                e.wait_ge(S("lru_d"), d + 9)
                act(la[:, :, :], lr[:, :, :], ACT.Exp).then_inc(step, 1)
                act(lt[:, :, :], lr[:, :, :], ACT.Tanh, scale=-1.0).then_inc(step, 1)
                e.wait_ge(S("lru_d"), d + 12)
                act(l2[:, :, :], l2[:, :, :], ACT.Sqrt).then_inc(step, 1)
                act(lg[:, :, :], lg[:, :, :], ACT.Gelu_apprx_tanh).then_inc(step, 1)
                e.wait_ge(S("lru_d"), d + 18)
                if first:
                    e.wait_ge(S("toeplitz_out"), 80)
                h = hhi[0:LRU, 4 * g:4 * g + 4, :] if isinstance(g, int) else hhi[0:LRU, bass.ds(g * 4, 4), :]
                act(h, lt[:, :, :], ACT.Copy).then_inc(step, 1)
            sweep(e, 4, group, 1, 1, 1)

            def stage_out(name, t0, rms=None):
                s = st[name]
                n_m = KC * s.per // s.n

                def unit(it, first, last):
                    split(*after(s, it, last))
                    if rms is None or it.k % s.per != s.per - 1:
                        return
                    g = it.of(0, s.per)
                    e.wait_ge(acc_free, g + (s.A + 3))
                    for h in range(n_m):
                        m = g * n_m + h
                        par_ = (n_m * (it.k // s.per) + h) % 2
                        wait(e, S("sq_mm"), m + (KC * rms - 1))
                        act(sq[:, par_, t0:T], chunk(res, m, t0), ACT.Square).then_inc(S("sq"), 1)
                u = 2 * s.per
                sweep(e, s.n, unit, u, u if s.n > u else 0, u)

            def layer_norm(i, gb, l, t0, x=True):
                n = T - t0
                for k in range(KC):
                    e.wait_ge(S("dev"), KC * i + k + 1)
                    act(dsq[:, k, t0:T], dev[:, k, t0:T], ACT.Square).then_inc(S("dsq"), 1)
                e.wait_ge(S("var_mm"), KC * (i + 1))
                act(std[:, 0:n], ps[:, 6, 0:n], ACT.Sqrt, bias=eps[:, 0:1]).then_inc(S("std"), 1)
                for k in range(KC):
                    e.wait_ge(S("scaled"), NX["ln"](i) + k + 1)
                    b = pcol(gb + "_b", KC * l + k)
                    act(res[:, k, t0:T], dev[:, k, t0:T], ACT.Identity, bias=b).then_inc(S("res_n"), 1)
                    if x:
                        act(xhi[:, k, t0:T], dev[:, k, t0:T], ACT.Identity, bias=b).then_inc(S("x_hi"), 1)

            def ffn_conv(l, t0):
                s, n, F = st[f"f_in{l}"], T - t0, NF * l
                W = 3 * 2 * NF * l

                def h_hi(it):
                    e.wait_ge(S("h_mul"), it.of(F) + 1)
                    act(chunk(hhi, it.of(), t0), hf[:, it.k % 2, t0:T], ACT.Copy).then_inc(S("h_hi"), 1)

                def unit(it, first, last):
                    b, acc = it.k % 2, (s.A + it.k) % 2
                    split(*after(s, it, last))
                    e.wait_ge(w_used, it.of(s.U) + 3)
                    wait(e, S("h_mul"), it.of(F) - 1)
                    for half, buf in ((0, cg), (1, cv)):
                        act(buf[:, b, t0:T], ps[:, 2 * acc + half, 0:n], ACT.Identity,
                            bias=pcol("conv_f_b", it.of() + (2 * NF * l + NF * half)),
                            scale=pcol("conv_f_w", it.of() * 3 + (W + 3 * NF * half + 2)))\
                            .then_inc(S("tap2"), 1)
                    if not first:
                        h_hi(it.next(-1))
                    e.wait_ge(S("tap0"), it.of(F) + 1)
                    act(gg[:, b, t0:T], cg[:, b, t0:T], ACT.Gelu_apprx_tanh).then_inc(S("gelu"), 1)
                sweep(e, s.n, unit, 2, 2, 2)
                h_hi(It(s.n - 1))

            def attention(run):
                n, lag = len(run.steps), run.lag

                def exps(i):
                    joint = len(run.steps[i].group) > 1
                    for j in run.steps[i].group:
                        s, g = run.steps[j], run.B + j
                        if joint:
                            e.wait_ge(S("joint_max"), i // 3 + 1)
                        e.wait_ge(S("scored"), run.B + i + 1)
                        for tile in range(2):
                            a, b = s.cols[tile]
                            p = probs[:, g % 6, a:b]
                            m = small[:, (run.B + i) % 8, tile, 3:4] if joint else small[:, g % 8, tile, 0:1]
                            o = act(p, p, ACT.Exp, bias=m, scale=-1.0, accum_out=small[:, g % 8, tile, 1:2])
                        o.then_inc(S("exp"), 1)

                def turned(i):
                    s, g = run.steps[i], run.B + i
                    e.wait_ge(S("turn_mm"), g + 1)
                    wait(e, S("pv_mm"), g - 1)
                    if s.small:
                        act(pt_small[0:16, g % 2, 0:2], early_t[:, s.head, :], ACT.Copy)
                        act(pt_small[0:16, g % 2, 2:258], ps[0:16, 2 + g % 2, 0:256], ACT.Copy)
                    r = s.turn[0][2] - s.turn[0][1]
                    w = s.turn[-1][3] + 128
                    act(pt[0:r, g % 2, 0:w], ps[0:r, 6 + g % 2, 0:w], ACT.Copy).then_inc(S("turned"), 1)

                def out_hi(p):
                    g = run.P + p
                    e.wait_ge(S("o_out"), g + 1)
                    act(xhi[:, run.first_pair + p, run.t0:T], sq[:, g % 2, run.t0:T], ACT.Copy).then_inc(S("x_hi"), 1)

                for t in range(n + lag + 3):
                    if t < n and run.steps[t].ends:
                        exps(t)
                    if 0 <= t - lag < n:
                        turned(t - lag)
                    if t - lag - 2 in run.pair_end:
                        out_hi(run.pair_end[t - lag - 2])

            def evacuate(name, t0, base, step=1, half=0, func=ACT.Copy):
                s = st[name]

                def unit(it, first, last):
                    split(*after(s, it, last))
                    e.wait_ge(w_used, it.of(s.U) + 3)
                    act(chunk(z, it.of() * step + base, t0), ps[:, 2 * ((s.A + it.k) % 2) + half, 0:T - t0], func)\
                        .then_inc(S("half_out"), 1)
                sweep(e, s.n, unit, 2, 2, 2)

            def act_fox():
                s = st["fgate"]
                split(*after(s, It(0), True))
                e.wait_ge(w_used, s.U + 3)
                act(ft[:, 0], ps[0:16, 2 * (s.A % 2), 0:T], ACT.Identity, bias=pcol("f_b", 0, 16)).then_inc(S("fg_x"), 1)
                log1p_exp(ft[:, 2], ft[:, 1], ft[:, 4], ft[:, 3], (13, 2))
                evacuate("kv", 0, 0)
                evacuate("qg", Q0, 24, half=1, func=ACT.Sigmoid)
                for j in range(KC):
                    e.wait_ge(S("vt_mm"), j + 1)
                    act(vt[0:16, j, 0, :], ps[0:16, 6 + j % 2, 256:384], ACT.Copy)
                    act(vt[:, j, 1:3, :], ps[:, 6 + j % 2, 0:256].rearrange("p (a b) -> p a b", a=2), ACT.Copy)\
                        .then_inc(S("vt"), 1)
                e.wait_ge(S("early"), 2)
                act(early[:, :, :], early[:, :, :], ACT.Exp).then_inc(S("early_exp"), 1)
                e.wait_ge(S("early_mm"), 2 * HEADS)
                act(early_t[:, :, :], ps[0:16, 3, 0:2 * HEADS].rearrange("p (h q) -> p h q", q=2), ACT.Copy)\
                    .then_inc(S("early_t"), 1)
                attention(fox)
            def norms(items):
                def root(it):
                    e.wait_ge(S("n_mm"), it.i + 1)
                    wait(e, S("n_out"), it.i - 1)
                    act(n_std[0:it.rows, it.i % 2, 0:it.n], ps[0:it.rows, 4 + it.i % 2, 0:it.n], ACT.Sqrt,
                        bias=eps[0:it.rows, 1:2], scale=it.scale).then_inc(S("n_std"), 1)
                for at_, it in enumerate(items):
                    wait(e, S("n_mm"), it.i - 1)
                    size = it.sums[-1][2]
                    o = n_sq[0:it.rows, it.i % 2, 0:size]
                    src = it.src
                    if len(src.shape) == 3:
                        o = o.rearrange("p (a b) -> p a b", a=2)
                    act(o, src, ACT.Square).then_inc(S("n_sq"), 1)
                    if at_:
                        root(items[at_ - 1])
                root(items[-1])

            def rms_norm(r, l, s):
                e.wait_ge(S("sq_mm"), KC * (r + 1))
                act(std[:, 0:SEQ], ps[:, 7, 0:SEQ], ACT.Sqrt, bias=eps[:, 1:2]).then_inc(S("std"), 1)
                for k in range(KC):
                    e.wait_ge(S("scaled"), KC * (4 + r) + k + 1)
                    act(xhi[:, k, META:T], dev[:, k, META:T], ACT.Identity, bias=mod[:, l, 24 * s + k:24 * s + k + 1])\
                        .then_inc(S("x_hi"), 1)

            def swiglu(i):
                s, F = st[f"g_in{i}"], NF * (2 + i)

                def h_hi(it):
                    e.wait_ge(acc_free, it.of(s.A) + 3)
                    act(chunk(hhi, it.of(), META), hf[:, it.k % 2, META:T], ACT.Copy).then_inc(S("h_hi"), 1)

                def unit(it, first, last):
                    b, acc = it.k % 2, (s.A + it.k) % 2
                    split(*after(s, it, last))
                    if not first:
                        h_hi(it.next(-1))
                    e.wait_ge(w_used, it.of(s.U) + 3)
                    act(gg[:, b, META:T], ps[:, 2 * acc, 0:SEQ], ACT.Silu).then_inc(S("gelu"), 1)
                sweep(e, s.n, unit, 2, 2, 2)
                h_hi(It(s.n - 1))
                stage_out(f"g_out{i}", META, rms=[1, 3, 4, None][i])

            def act_even():
                rms_norm(1, 0, 1)
                evacuate("ev_in", META, 0, step=2)
                s = st["ev_in"]
                e.wait_ge(acc_free, s.A + s.n + 2)
                norms(latent_norms)
                e.wait_ge(S("n_out"), 2)
                for k in range(3):
                    act(xhi[:, k, META:T], z[:, k, META:T], ACT.Copy).then_inc(S("latent_hi"), 1)
                split(st["ukv"], It(0))
                e.wait_ge(w_used, st["uq"].U + 3)
                for i in range(4):
                    act(q96[:, 2 * i:2 * i + 2, :], ps[0:96, i, :].rearrange("p (a b) -> p a b", a=2), ACT.Copy)\
                        .then_inc(S("q_out"), 1)
                split(st["cmp_w1"], It(0))
                e.wait_ge(S("q_out"), 4)
                norms(mla_norms[0:5])
                e.wait_ge(S("rotated"), 5)
                act(kf[64:96, :, :], z[64:96, 3, META:T].unsqueeze(1).broadcast_to([32, 8, SEQ]), ACT.Copy)\
                    .then_inc(S("k_rope"), 1)
                e.wait_ge(S("kv_out"), 4)
                norms(mla_norms[5:])
                e.wait_ge(S("vm_mm"), 1)
                for i in range(2):
                    o = act(vm[:, 4 * i:4 * i + 4, :, :].rearrange("p h t c -> p (h t c)"), ps[:, i, :], ACT.Copy)
                o.then_inc(S("vm"), 1)
                attention(mla)
                norms(nsa_norms)
                e.wait_ge(S("vn_mm"), 1)
                act(v_nsa[:, :, :].rearrange("p a b -> p (a b)"), ps[:, 2, :], ACT.Copy)
                act(gates[:, :, :], ps[:, 3, 0:256].rearrange("p (t c) -> p t c", t=2)[:, :, 96:120], ACT.Sigmoid)\
                    .then_inc(S("vn"), 1)
                e.wait_ge(S("x2_f"), 8)
                act(x2_hi[:, :, :, :].rearrange("p j i c -> p (j i c)"),
                    x2[:, :, :, :, :].rearrange("p j i g n -> p (j i g n)"), ACT.Copy).then_inc(S("x2_hi"), 1)
                c = st["cmp_w1"]
                for u in range(1, 4):
                    split(c, It(u))
                for u in (1, 3):
                    e.wait_ge(w_used, c.U + u + 3)
                    for m in range(2):
                        act(hid[:, u // 2, m, :], ps[:, u - 1 + m, 0:30], ACT.Silu).then_inc(S("hid"), 1)
                split(*after(c, It(3), True))
                e.wait_ge(S("cmp_mm"), 1)
                act(k_cmp[:, :], ps[:, 0, 0:30], ACT.Copy)
                act(v_cmp[:, :, :].rearrange("p a b -> p (a b)"), ps[0:15, 1, 0:128], ACT.Copy).then_inc(S("cmp_out"), 1)
                e.wait_ge(S("cmp_out"), 1)
                norms(cmp_norms)
                attention(nsa)

            def act_odd():
                rms_norm(4, 1, 1)
                evacuate("od_in", META, 0, step=2)
                s = st["od_in"]
                e.wait_ge(acc_free, s.A + s.n + 2)
                norms(odd_norms)
                for i in range(4):
                    e.wait_ge(S("vo_mm"), i + 1)
                    act(v_odd[:, 2 * i:2 * i + 2, :, :].rearrange("p a t c -> p (a t c)"), ps[:, i, :], ACT.Copy)\
                        .then_inc(S("vo"), 1)
                attention(odd)

            def act_second():
                for k in range(KC):
                    e.wait_ge(S("res_n"), 3 * KC + k + 1)
                    wait(e, S("sq_mm"), k - 1)
                    act(sq[:, k % 2, META:T], res[:, k, META:T], ACT.Square).then_inc(S("sq"), 1)
                rms_norm(0, 0, 0)
                swiglu(0)
                act_even()
                stage_out("ev_out", META, rms=2)
                rms_norm(2, 0, 2)
                swiglu(1)
                rms_norm(3, 1, 0)
                swiglu(2)
                act_odd()
                stage_out("od_out", META, rms=5)
                rms_norm(5, 1, 2)
                swiglu(3)

            stage_out("a_out", 0)
            layer_norm(0, "ln1", 0, 0)
            for l, t0 in ((0, 0), (1, Q0)):
                if l:
                    act_fox()
                    stage_out("b_out", Q0)
                    layer_norm(2, "ln1", 1, Q0)
                ffn_conv(l, t0)
                stage_out(f"f_out{l}", t0)
                layer_norm(2 * l + 1, "ln2", l, t0, x=l == 0)
            act_second()

        @block.vector
        def _(e):
            e.nop().then_inc(w_lo, 2)
            e.nop().then_inc(acc_free, 2)
            tt, stt, ts = e.tensor_tensor, e.scalar_tensor_tensor, e.tensor_scalar

            def split(s, it):
                if s is None:
                    return
                slot = (s.U + it.k) % 2
                e.wait_ge(w_hi, it.of(s.U) + 1)
                tt(wlo[0:s.rows, slot, 0:s.cols], raw[0:s.rows, slot, 0:s.cols],
                   whi[0:s.rows, slot, 0:s.cols].bitcast(f32), ALU.subtract).then_inc(w_lo, 1)

            def log1p_exp(t, base):
                n, step = [base[0]], S("lp_d")

                def go(ins, sem=None):
                    ins.then_inc(step, 1)
                    n[0] += 1
                    e.wait_ge(step, n[0])
                x, nax, ez, w, lw, out, d, eq, r = t
                go(stt(nax, x, -1.0, x, ALU.mult, ALU.min))
                e.wait_ge(S("lp_a"), base[1] + 1)
                go(ts(w, ez, 1.0, None, ALU.add))
                go(ts(d, w, -1.0, None, ALU.add))
                go(ts(eq, d, 0.0, None, ALU.is_equal))
                go(tt(d, d, eq, ALU.add))
                go(e.reciprocal(r, d))
                go(tt(r, r, ez, ALU.mult))
                go(tt(eq, eq, ez, ALU.mult))
                e.wait_ge(S("lp_a"), base[1] + 2)
                go(tt(out, lw, r, ALU.mult))
                go(tt(out, out, eq, ALU.add))
                return n[0]

            e.wait_ge(S("t5_mm"), 1)
            for i, n in enumerate((8, 4, 4, 4)):
                o = e.tensor_copy(t_rows[0:n, i, :], ps[0:n, 4 + i, :])
            o.then_inc(S("t5_out"), 1)
            e.wait_ge(S("t5_mm"), 2)
            e.tensor_copy(bias_c[:, :, :, :].rearrange("p t h k -> p t k h"),
                          ps[:, 0, 0:240].rearrange("p (t k h) -> p t k h", t=2, h=8)).then_inc(S("t5_out"), 1)
            e.wait_ge(S("par_in"), 16)
            o = PAR["lam"][0]
            lam = par[0:LRU, o:o + NLRU]
            L = lam_t
            done = log1p_exp((lam, L[:, 0], L[:, 1], L[:, 2], L[:, 3], L[:, 4], L[:, 5], L[:, 6], L[:, 7]), (0, 0))
            ts(L[:, 0], lam, -1.0, 0.0, ALU.mult, ALU.max).then_inc(S("lp_d"), 1)
            e.wait_ge(S("lp_d"), done + 1)
            tt(L[:, 0], L[:, 0], L[:, 4], ALU.add).then_inc(S("lp_d"), 1)
            e.wait_ge(S("lp_d"), done + 2)
            ts(sp8[:, :], L[:, 0], -8.0, None, ALU.mult).then_inc(S("lp_d"), 1)
            e.wait_ge(S("lp_d"), done + 3)
            for k in range(KC):
                e.wait_ge(S("x_hi"), k + 1)
                tt(xlo[:, k, :], res[:, k, :], xhi[:, k, :].bitcast(f32), ALU.subtract).then_inc(S("x"), 1)

            s = st["a_in"]
            split(s, It(0))

            def group(it, first, last):
                a, g, step = it.of() * LRU_A, it.of(), S("lru_d")
                n = [it.of() * LRU_D, 0]

                def go(ins, hold=True):
                    ins.then_inc(step, 1)
                    n[1] += 1
                    if hold:
                        e.wait_ge(step, n[0] + n[1])
                for b in range(4):
                    u = It(4 * it.k + b, it.j, 4)
                    acc = (s.A + b) % 2
                    split(*after(s, u, last and b == 3))
                    e.wait_ge(S("lru_a"), a + (b + 1))
                    for tap in (2, 1, 0):
                        d = 3 - tap
                        o = stt(lx[:, b, d:T], ps[0:LRU, 2 * acc + 1, 0:T - d],
                                pcol("conv_a_w", g * 16 + (4 * b + tap), LRU), lx[:, b, d:T], ALU.mult, ALU.add)
                        if tap:
                            go(o)
                        else:
                            o.then_inc(acc_free, 1)
                e.wait_ge(S("lru_a"), a + 8)
                spg = sp8[:, 4 * g:4 * g + 4] if isinstance(g, int) else sp8[:, bass.ds(g * 4, 4)]
                go(tt(lr[:, :, :], lr[:, :, :], spg.unsqueeze(2).broadcast_to([LRU, 4, T]), ALU.mult), False)
                go(tt(li[:, :, :], li[:, :, :], lx[:, :, :], ALU.mult), False)
                e.wait_ge(S("lru_a"), a + 9)
                go(tt(l2[:, :, :], la[:, :, :], la[:, :, :], ALU.mult))
                e.wait_ge(S("lru_a"), a + 10)
                go(stt(l2[:, :, :], l2[:, :, :], 1.0, lt[:, :, :], ALU.add, ALU.mult))
                e.wait_ge(S("lru_a"), a + 11)
                go(tt(li[:, :, :], li[:, :, :], l2[:, :, :], ALU.mult))
                for b in range(4):
                    go(e.tensor_tensor_scan(lt[:, b, :], la[:, b, :], li[:, b, :], 0.0, ALU.mult, ALU.add), b == 3)
                e.wait_ge(S("lru_a"), a + 12)
                go(tt(lt[:, :, :], lt[:, :, :], lg[:, :, :], ALU.mult))
                e.wait_ge(S("lru_a"), a + 13)
                h = (slice(0, LRU), slice(4 * g, 4 * g + 4) if isinstance(g, int) else bass.ds(g * 4, 4))
                go(tt(hlo[h], lt[:, :, :], hhi[h].bitcast(f32), ALU.subtract), False)
                assert n[1] == LRU_D
            sweep(e, 4, group, 1, 1, 1)

            def stage_out(name, t0, gate=None, final=False):
                s = st[name]
                n, n_m = T - t0, KC * s.per // s.n

                def unit(it, first, last):
                    split(*after(s, it, last))
                    if it.k % s.per != s.per - 1:
                        return
                    g, acc = it.of(0, s.per), (s.A + it.k // s.per) % 2
                    e.wait_ge(w_used, it.of(s.U) + 3)
                    if gate is None:
                        r = chunk(res, g * n_m, t0, n=n_m)
                        p = ps[:, 2 * acc, 0:n] if n_m == 1 else ps[:, 2 * acc:2 * acc + 2, 0:n]
                        stt(r, r, ALPHA, p, ALU.mult, ALU.add).then_inc(acc_free, 1)
                        return
                    for h in range(n_m):
                        m = g * n_m + h
                        r = chunk(res, m, t0)
                        l, o = gate
                        col = mod[:, l, o + m:o + m + 1] if isinstance(m, int) else mod[:, l, bass.ds(m + o, 1)]
                        o = stt(r, ps[:, 2 * acc + h, 0:n], col, r, ALU.mult, ALU.add)
                    o.then_inc(acc_free, 1)
                u = 2 * s.per
                sweep(e, s.n, unit, u, u if s.n > u else 0, u)

            def layer_norm(i, gb, l, t0, x=None):
                n = T - t0
                e.wait_ge(S("mean_mm"), KC * (i + 1))
                for k in range(KC):
                    tt(dev[:, k, t0:T], res[:, k, t0:T], ps[:, 7, 0:n], ALU.subtract).then_inc(S("dev"), 1)
                e.wait_ge(S("std"), NX["std"](i) + 1)
                e.reciprocal(std[:, 0:n], std[:, 0:n]).then_inc(S("rstd"), 1)
                e.wait_ge(S("rstd"), NX["std"](i) + 1)
                for k in range(KC):
                    stt(dev[:, k, t0:T], dev[:, k, t0:T], pcol(gb + "_g", KC * l + k), std[:, 0:n], ALU.mult, ALU.mult)\
                        .then_inc(S("scaled"), 1)
                if x is not None:
                    for k in range(KC):
                        e.wait_ge(S("x_hi"), x + k + 1)
                        tt(xlo[:, k, t0:T], res[:, k, t0:T], xhi[:, k, t0:T].bitcast(f32), ALU.subtract)\
                            .then_inc(S("x"), 1)

            def ffn_conv(l, t0):
                s, n, F = st[f"f_in{l}"], T - t0, NF * l
                W = 3 * 2 * NF * l

                def mul(it):
                    b = it.k % 2
                    e.wait_ge(S("gelu"), it.of(F) + 1)
                    e.wait_ge(acc_free, it.of(s.A) + 3)
                    wait(e, S("h_hi"), it.of(F) - 1)
                    tt(hf[:, b, t0:T], gg[:, b, t0:T], cv[:, b, t0:T], ALU.mult).then_inc(S("h_mul"), 1)

                def low(it):
                    e.wait_ge(S("h_hi"), it.of(F) + 1)
                    tt(chunk(hlo, it.of(), t0), hf[:, it.k % 2, t0:T], chunk(hhi, it.of(), t0).bitcast(f32),
                       ALU.subtract).then_inc(S("h_lo"), 1)

                def unit(it, first, last):
                    b, acc = it.k % 2, (s.A + it.k) % 2
                    split(*after(s, it, last))
                    if not first:
                        mul(it.next(-1))
                    e.wait_ge(S("tap2"), it.of(F) * 2 + 2)
                    for tap in (1, 0):
                        d = 2 - tap
                        for half, buf in ((0, cg), (1, cv)):
                            if tap == 0:
                                e.wait_ge(S("tap1"), it.of(F) * 2 + (1 + half))
                            o = stt(buf[:, b, t0 + d:T], ps[:, 2 * acc + half, 0:n - d],
                                    pcol("conv_f_w", it.of() * 3 + (W + 3 * NF * half + tap)),
                                    buf[:, b, t0 + d:T], ALU.mult, ALU.add)
                            o.then_inc(S("tap1") if tap else acc_free if half else S("tap0"), 1)
                    if not first:
                        low(it.next(-1))
                sweep(e, s.n, unit, 2, 2, 2)
                mul(It(s.n - 1))
                low(It(s.n - 1))

            soft = [0]
            half_base = {'kv': 0, 'qg': KC, 'ev_in': 2 * KC, 'od_in': 3 * KC}
            def attention(run):
                n, lag = len(run.steps), run.lag
                step = S("soft_step")

                def go(ins):
                    ins.then_inc(step, 1)
                    soft[0] += 1
                    e.wait_ge(step, soft[0])

                def scored(i):
                    s, g = run.steps[i], run.B + i
                    e.wait_ge(S("qk_mm"), g + 1)
                    wait(e, S("turn_mm"), g - 5)
                    for tile in range(2):
                        a, b = s.cols[tile]
                        o = e.tensor_tensor_reduce(out=probs[:, g % 6, a:b], in0=ps[:, 4 + g % 2, a:b],
                                                   in1=s.bias[tile], scale=-1.0, scalar=3e38, op0=ALU.add,
                                                   op1=ALU.min, accum_out=small[:, g % 8, tile, 0:1])
                    o.then_inc(S("scored"), 1)
                    if s.ends and len(s.group) > 1:
                        e.wait_ge(S("scored"), g + 1)
                        m = [small[:, (run.B + j) % 8, :, 0] for j in s.group]
                        out = small[:, g % 8, :, 3]
                        go(tt(out, m[0], m[1], ALU.min))
                        tt(out, out, m[2], ALU.min).then_inc(S("joint_max"), 1)

                def normal(i):
                    s, g = run.steps[i], run.B + i
                    e.wait_ge(S("exp"), g + 1)
                    r = g % 8
                    den = small[:, r, :, 1]
                    if s.mask is not None:
                        for tile in range(2):
                            a, b = s.cols[tile]
                            p = probs[:, g % 6, a:b]
                            go(e.tensor_tensor_reduce(out=p, in0=p, in1=s.mask[tile], scale=1.0, scalar=0.0,
                                                      op0=ALU.mult, op1=ALU.add, accum_out=small[:, r, tile, 1:2]))
                        go(ts(den, den, 1e-30, None, ALU.max))
                    if len(s.group) > 1:
                        d = [small[:, (run.B + j) % 8, :, 1] for j in s.group]
                        go(tt(small[:, r, :, 4], d[0], d[1], ALU.add))
                        go(tt(small[:, r, :, 4], small[:, r, :, 4], d[2], ALU.add))
                        den = small[:, r, :, 4]
                    go(e.reciprocal(small[:, r, :, 5], den))
                    if s.gate is not None:
                        go(tt(small[:, r, :, 5], small[:, r, :, 5], s.gate, ALU.mult))
                    for j in s.group:
                        for tile in range(2):
                            a, b = run.steps[j].cols[tile]
                            p = probs[:, (run.B + j) % 6, a:b]
                            o = ts(p, p, small[:, r, tile, 5:6], None, ALU.mult)
                        o.then_inc(S("prob"), 1)

                def out(p, i):
                    g = run.P + p
                    e.wait_ge(S("pv_mm"), run.B + i + 1)
                    if p >= 2:
                        e.wait_ge(S("x"), run.x + p - 1)
                    o, nq = sq[:, g % 2, run.t0:T], T - run.t0
                    if run.out_gate is not None:
                        o = tt(o, ps[:, g % 2, 0:nq], z[:, run.out_gate + p, run.t0:T], ALU.mult)
                    else:
                        o = e.tensor_copy(o, ps[:, g % 2, 0:nq])
                    o.then_inc(S("o_out"), 1)

                def out_lo(p):
                    c = run.first_pair + p
                    e.wait_ge(S("x_hi"), run.x + p + 1)
                    tt(xlo[:, c, run.t0:T], sq[:, (run.P + p) % 2, run.t0:T], xhi[:, c, run.t0:T].bitcast(f32),
                       ALU.subtract).then_inc(S("x"), 1)

                for t in range(n + lag + 4):
                    if t < n:
                        scored(t)
                    if 0 <= t - 1 < n and run.steps[t - 1].ends:
                        normal(t - 1)
                    if t - lag - 2 in run.pair_end:
                        out(run.pair_end[t - lag - 2], t - lag - 2)
                    if t - lag - 3 in run.pair_end:
                        out_lo(run.pair_end[t - lag - 3])

            def evacuate(name, t0, base, step=1, half=1, scale=None):
                s = st[name]

                def unit(it, first, last):
                    split(*after(s, it, last))
                    e.wait_ge(S("half_out"), it.of(half_base[name]) + 1)
                    p, o = ps[:, 2 * ((s.A + it.k) % 2) + half, 0:T - t0], chunk(z, it.of() * step + base, t0)
                    (e.tensor_copy(o, p) if scale is None else ts(o, p, scale, None, ALU.mult)).then_inc(acc_free, 1)
                sweep(e, s.n, unit, 2, 2, 2)

            def dve_fox():
                step, n = S("forget_step"), [0]

                def go(ins, hold=True):
                    ins.then_inc(step, 1)
                    n[0] += 1
                    if hold:
                        e.wait_ge(step, n[0])
                split(*after(st["fgate"], It(0), True))
                e.wait_ge(S("fg_x"), 1)
                go(e.memset(c_lhs[:, :, :].bitcast(f32), 1.0), False)
                go(e.memset(c_rhs[:, :, :].bitcast(f32), 1.0), False)
                e.memset(ft[:, 8], 1.0).then_inc(acc_free, 1)
                e.wait_ge(acc_free, st["fgate"].A + 3)
                f = [ft[:, i] for i in range(9)]
                log1p_exp((f[0], f[1], f[2], f[3], f[4], f[5], f[6], f[7], fr[:, :]), (13, 2))
                go(stt(f[0], f[0], 0.0, f[5], ALU.min, ALU.subtract))
                go(e.tensor_tensor_scan(f[1], f[8], f[0], 0.0, ALU.mult, ALU.add))
                go(e.tensor_copy(c_part[:, 0], f[1]))
                go(tt(c_part[:, 1], f[1], c_part[:, 0].bitcast(f32), ALU.subtract))
                go(ts(c_part[:, 2], c_part[:, 0].bitcast(f32), -1.0, None, ALU.mult))
                go(ts(c_part[:, 3], c_part[:, 1].bitcast(f32), -1.0, None, ALU.mult))
                assert n[0] == FORGET_STEPS
                evacuate("kv", 0, 8)
                evacuate("qg", Q0, 16, half=0, scale=64 ** -0.5)
                e.wait_ge(S("early_mm"), HEADS)
                m = con("causal0")[0:2, :].unsqueeze(1).broadcast_to([2, HEADS, 16])
                es = S("early_step")
                p0 = ps[0:2, 2, 0:256].rearrange("p (h k) -> p h k", k=16)
                tt(early[:, :, :], p0, m, ALU.add).then_inc(es, 1)
                e.wait_ge(es, 1)
                e.reduce_max(early_m[:, 0], early[:, :, :], AX.X).then_inc(es, 1)
                e.wait_ge(es, 2)
                tt(early[:, :, :], early[:, :, :], early_m[:, 0].unsqueeze(2).broadcast_to([2, HEADS, 16]),
                   ALU.subtract).then_inc(S("early"), 2)
                e.wait_ge(S("early_exp"), 1)
                e.reduce_sum(early_m[:, 1], early[:, :, :], AX.X).then_inc(es, 1)
                e.wait_ge(es, 3)
                e.reciprocal(early_m[:, 2], early_m[:, 1]).then_inc(es, 1)
                e.wait_ge(es, 4)
                tt(early[:, :, :], early[:, :, :], early_m[:, 2].unsqueeze(2).broadcast_to([2, HEADS, 16]),
                   ALU.mult).then_inc(S("early"), 2)
                attention(fox)
            def norms(items):
                for it in items:
                    r, b = it.rows, it.i % 2
                    e.wait_ge(S("n_std"), it.i + 1)
                    sd = n_std[0:r, b, 0:it.n]
                    e.reciprocal(sd, sd).then_inc(S("n_rstd"), 1)
                    e.wait_ge(S("n_rstd"), it.i + 1)
                    for src, g, dst in it.outs:
                        d = sd.rearrange("p (a b) -> p a b", a=2) if len(src.shape) == 3 else sd[:, 0:src.shape[-1]]
                        o = stt(dst, src, g, d, ALU.mult, ALU.mult)
                    o.then_inc(S("n_out"), 1)

            def modulation(l):
                e.wait_ge(S("mod_mm"), l + 1)
                m, step = mod[:, l, :], S("mod_step")
                o = PAR["ada_b"][0] + ADA_T * l
                tt(m, ps[:, 6, 0:ADA_T], par[:, o:o + ADA_T], ALU.add).then_inc(step, 1)
                e.wait_ge(step, 3 * l + 1)
                v = m.rearrange("p (s c k) -> p s c k", s=3, c=3)
                o = PAR["norm_g"][0] + 3 * KC * l
                g = par[:, o:o + 3 * KC].rearrange("p (s k) -> p s k", s=3)
                stt(gs[:, l, :].rearrange("p (s k) -> p s k", s=3), v[:, :, 1, :], 1.0, g, ALU.add, ALU.mult)\
                    .then_inc(step, 1)
                ts(v[:, 0:3:2, 2, :], v[:, 0:3:2, 2, :], 0.5, None, ALU.mult).then_inc(step, 1)
                e.wait_ge(step, 3 * l + 3)

            def rms_norm(r, l, s, x):
                e.wait_ge(S("std"), 4 + r + 1)
                e.reciprocal(std[:, 0:SEQ], std[:, 0:SEQ]).then_inc(S("rstd"), 1)
                e.wait_ge(S("rstd"), 4 + r + 1)
                for k in range(KC):
                    stt(dev[:, k, META:T], res[:, k, META:T], gs[:, l, KC * s + k:KC * s + k + 1], std[:, 0:SEQ],
                        ALU.mult, ALU.mult).then_inc(S("scaled"), 1)
                for k in range(KC):
                    e.wait_ge(S("x_hi"), x + k + 1)
                    stt(xlo[:, k, META:T], dev[:, k, META:T], mod[:, l, 24 * s + k:24 * s + k + 1],
                        xhi[:, k, META:T].bitcast(f32), ALU.add, ALU.subtract).then_inc(S("x"), 1)

            def swiglu(i, l, sub):
                s, F = st[f"g_in{i}"], NF * (2 + i)

                def low(it):
                    e.wait_ge(S("h_hi"), it.of(F) + 1)
                    tt(chunk(hlo, it.of(), META), hf[:, it.k % 2, META:T], chunk(hhi, it.of(), META).bitcast(f32),
                       ALU.subtract).then_inc(S("h_lo"), 1)

                def unit(it, first, last):
                    b, acc = it.k % 2, (s.A + it.k) % 2
                    split(*after(s, it, last))
                    if not first:
                        low(it.next(-1))
                    e.wait_ge(S("gelu"), it.of(F) + 1)
                    tt(hf[:, b, META:T], ps[:, 2 * acc + 1, 0:SEQ], gg[:, b, META:T], ALU.mult).then_inc(acc_free, 1)
                sweep(e, s.n, unit, 2, 2, 2)
                low(It(s.n - 1))
                stage_out(f"g_out{i}", META, gate=(l, 24 * sub + 16))

            def dve_even():
                rms_norm(1, 0, 1, X["ev"])
                evacuate("ev_in", META, 1, step=2)
                for i, name in enumerate(("nsa_g", "dil_g", "moba_g")):
                    o = ts(g8[:, i:i + 1], gcol(name), 0.125, None, ALU.mult)
                o.then_inc(S("g8"), 1)
                e.wait_ge(S("g8"), 1)
                norms(latent_norms)
                for k in range(3):
                    e.wait_ge(S("latent_hi"), k + 1)
                    tt(xlo[:, k, META:T], z[:, k, META:T], xhi[:, k, META:T].bitcast(f32), ALU.subtract)\
                        .then_inc(S("latent"), 1)
                split(st["ukv"], It(0))
                split(st["cmp_w1"], It(0))
                e.wait_ge(S("rope_in"), 16)
                norms(mla_norms[0:5])
                e.wait_ge(w_used, st["ukv"].U + 3)
                for i in range(4):
                    e.tensor_copy(zkv[:, 2 * i:2 * i + 2, :], ps[:, i, :].rearrange("p (a b) -> p a b", a=2))\
                        .then_inc(S("kv_out"), 1)
                for i in range(5):
                    two = i < 4
                    n = 512 if two else SEQ
                    src = q96[:, 2 * i:2 * i + 2, :] if two else q96[:, 8, :]
                    dst = src if two else z[0:96, 3, META:T]
                    c, s = (rope[:, 2 + j, :] if two else rope[:, j, :] for j in range(2))
                    t0, t1, p = rot_t[:, 0, 0:n], rot_t[:, 1, 0:n], ps[0:96, 6 + i % 2, 0:n]
                    if two:
                        c, s = (v.unsqueeze(1).broadcast_to([96, 2, SEQ]) for v in (c, s))
                        t0, t1, p = (v.rearrange("p (a b) -> p a b", a=2) for v in (t0, t1, p))
                    e.wait_ge(S("rot_mm"), i + 1)
                    tt(t0, src, c, ALU.mult).then_inc(S("rot_step"), 1)
                    tt(t1, p, s, ALU.mult).then_inc(S("rot_step"), 1)
                    e.wait_ge(S("rot_step"), 2 * i + 2)
                    if not two:
                        dst, t0, t1 = dst[64:96], t0[64:96], t1[64:96]
                    tt(dst, t0, t1, ALU.add).then_inc(S("rotated"), 1)
                    e.wait_ge(S("rotated"), i + 1)
                norms(mla_norms[5:])
                attention(mla)
                norms(nsa_norms)
                for j in range(2):
                    for g in range(2):
                        for hi in range(2):
                            e.wait_ge(S("a2_in"), 16 * 8)
                            v = a2[:, j, g, :].rearrange("p (m l two) -> p l m two", l=8, two=2)
                            o = PAR["cmp_pe"][0] + 16 * j + 8 * hi
                            pe = par[:, o:o + 8].unsqueeze(2).broadcast_to([128, 8, 15])
                            tt(x2[:, j, 8 * hi:8 * hi + 8, g, :], v[:, :, hi:hi + 15, 0], pe, ALU.add)\
                                .then_inc(S("x2_f"), 1)
                e.wait_ge(S("x2_hi"), 1)
                tt(x2_lo[:, :, :, :].rearrange("p j i c -> p (j i c)"),
                   x2[:, :, :, :, :].rearrange("p j i g n -> p (j i g n)"),
                   x2_hi[:, :, :, :].rearrange("p j i c -> p (j i c)").bitcast(f32), ALU.subtract).then_inc(S("x2"), 1)
                c = st["cmp_w1"]
                for u in range(1, 4):
                    split(c, It(u))
                split(*after(c, It(3), True))
                norms(cmp_norms)
                attention(nsa)

            def dve_odd():
                rms_norm(4, 1, 1, X["od"])
                evacuate("od_in", META, 1, step=2)
                norms(odd_norms)
                attention(odd)

            def dve_second():
                modulation(0)
                rms_norm(0, 0, 0, X["g0"])
                swiglu(0, 0, 0)
                dve_even()
                stage_out("ev_out", META, gate=(0, 24 + 16))
                rms_norm(2, 0, 2, X["g1"])
                swiglu(1, 0, 2)
                modulation(1)
                rms_norm(3, 1, 0, X["g2"])
                swiglu(2, 1, 0)
                dve_odd()
                stage_out("od_out", META, gate=(1, 24 + 16))
                rms_norm(5, 1, 2, X["g3"])
                swiglu(3, 1, 2)

            stage_out("a_out", 0)
            layer_norm(0, "ln1", 0, 0, X["f0"])
            for l, t0 in ((0, 0), (1, Q0)):
                if l:
                    dve_fox()
                    stage_out("b_out", Q0)
                    layer_norm(2, "ln1", 1, Q0, X["f1"])
                ffn_conv(l, t0)
                stage_out(f"f_out{l}", t0)
                layer_norm(2 * l + 1, "ln2", l, t0, X["fox"] if l == 0 else None)
            dve_second()


def kernel(**inputs):
    import concourse.bacc as bacc
    from concourse.bass_utils import run_bass_kernel_spmd

    nc = bacc.Bacc("TRN2", target_bir_lowering=False, num_devices=1)
    arrays = {name: np.ascontiguousarray(a) for name, a in pack(inputs).items()}
    ap = {name: nc.dram_tensor(name, a.shape, mybir.dt.from_np(a.dtype), kind="ExternalInput").ap()
          for name, a in arrays.items()}
    ap["out"] = nc.dram_tensor("out", [128, KC, SEQ], mybir.dt.float32, kind="ExternalOutput").ap()
    build(nc, ap)
    r = run_bass_kernel_spmd(nc, [arrays], core_ids=[0])
    return r.results[0]["out"].transpose(1, 0, 2).reshape(D, SEQ).T[None]
```

```python
import math
import numpy as np
import concourse.bass as bass
from concourse import mybir
from contextlib import ExitStack

D = 1024
KC = D // 128
SEQ, META = 256, 16
T = SEQ + META
DEPTH = 2
D_RNN = 3 * D // 2
LRU = 96
NLRU = D_RNN // LRU
D_FF = 2816
NF = D_FF // 128
D_FF2 = 2752
KH = NF // 2
HEADS = 16
Q0 = META - 2
ALPHA = (2 * DEPTH) ** 0.25
LN_EPS, RMS_EPS = 1e-5, 1e-6
RING = 4
SLOT = 2048
ADA_T = 9 * D // 128
MOD_N = ADA_T // 3
NEG = -1e30
PAR = {}


def column_plan():
    at = 0
    for name, width in [
        ("conv_a_w", 4 * NLRU), ("conv_a_b", NLRU), ("b_r", NLRU), ("b_i", NLRU), ("lam", NLRU),
        ("f_b", 1), ("c", KC),
        ("ln1_g", 16), ("ln1_b", 16), ("ln2_g", 16), ("ln2_b", 16),
        ("conv_f_w", 2 * 3 * 2 * NF), ("conv_f_b", 2 * 2 * NF),
        ("ada_b", 2 * ADA_T), ("norm_g", 2 * 3 * KC),
        ("mla_gq", 1), ("mla_gk", 1), ("mla_qn", 2), ("mla_kvn", 1),
        ("nsa_g", 2), ("dil_g", 2), ("moba_g", 2), ("cmp_pe", 32),
    ]:
        PAR[name] = (at, width)
        at += width
    return at


NPAR = column_plan()


class It:

    def __init__(self, k, j=None, step=0):
        self.k, self.j, self.step = k, j, step

    def of(self, base=0, div=1):
        n = (base + self.k) // div
        return n if self.j is None else self.j * (self.step // div) + n

    def next(self, n=1):
        return It(self.k + n, self.j, self.step)


def sweep(e, n, body, first, last, unroll=RING):
    first = min(first, n)
    trips = max(0, n - first - last) // unroll
    last = n - first - trips * unroll
    for k in range(first):
        body(It(k), k == 0, False)
    if trips == 1:
        for b in range(unroll):
            body(It(first + b), first + b == 0, False)
    elif trips:
        with e.Fori(0, trips) as j:
            for b in range(unroll):
                body(It(first + b, j, unroll), False, False)
    for k in range(n - last, n):
        body(It(k), k == 0, k == n - 1)


def wait(e, sem, value):
    if not isinstance(value, int) or value > 0:
        e.wait_ge(sem, value)


class Stage:

    def __init__(self, plan, n, cols, rows=128, per=1):
        self.n, self.cols, self.rows, self.per = n, cols, rows, per
        self.U = sum(s.n for s in plan)
        self.A = sum(s.groups for s in plan)
        self.groups = n // per if per else 0
        plan.append(self)


def stage_plan():
    plan, st = [], {}
    for name, spec in [
        ("a_in", (NLRU, 2 * KC * LRU)),
        ("a_out", (KC, NLRU * 128, LRU)),
        ("f_in0", (NF, 2 * KC * 128)),
        ("f_out0", (2 * KC, KH * 128, 128, 2)),
        ("fgate", (1, KC * 128)),
        ("kv", (KC, 2 * KC * 128)),
        ("qg", (KC, 2 * KC * 128)),
        ("b_out", (KC // 2, 2 * KC * 128)),
        ("f_in1", (NF, 2 * KC * 128)),
        ("f_out1", (2 * KC, KH * 128, 128, 2)),
        ("g_in0", (NF, 2 * KC * 128)),
        ("g_out0", (2 * KC, KH * 128, 128, 2)),
        ("ev_in", (8, 2 * KC * 128)),
        ("uq", (1, 2 * 8 * 96, 128, 0)),
        ("ukv", (1, 8 * 128, 128, 0)),
        ("cmp_w1", (4, 8 * 256, 128, 0)),
        ("ev_out", (KC // 2, 2 * KC * 128)),
        ("g_in1", (NF, 2 * KC * 128)),
        ("g_out1", (2 * KC, KH * 128, 128, 2)),
        ("g_in2", (NF, 2 * KC * 128)),
        ("g_out2", (2 * KC, KH * 128, 128, 2)),
        ("od_in", (12, 2 * KC * 128)),
        ("od_out", (KC // 2, 2 * 4 * 128)),
        ("g_in3", (NF, 2 * KC * 128)),
        ("g_out3", (2 * KC, KH * 128, 128, 2)),
    ]:
        st[name] = Stage(plan, *spec)
    return st


LRU_A, LRU_D = 8, 11
GROUPS = NLRU // 4
X, n = {}, 0
for name, count in [("a", KC), ("f0", KC), ("fox", KC), ("fox_o", KC), ("f1", KC), ("g0", KC), ("ev", KC),
                    ("ev_o", KC), ("g1", KC), ("g2", KC), ("od", KC), ("od_o", 4), ("g3", KC)]:
    X[name] = n
    n += count
NX = {"ln": lambda i: KC * i, "std": lambda i: i}
FORGET_STEPS = 8


def t5_buckets(dist):
    n = np.maximum(dist, 0)
    nf = np.maximum(n, 1).astype(np.float32)
    large = 16 + (np.log(nf / np.float32(16)) / np.float32(math.log(8)) * 16).astype(np.int32)
    return np.where(n < 16, n, np.minimum(large, 31))


def constants():
    f = np.float32
    c = {}
    c["ident"] = np.eye(128, dtype=f)
    p = np.arange(128)
    same64 = (p[:, None] // 64 == p[None, :] // 64)
    c["mean64"] = (same64 / 64).astype(f)
    for name, second in (("head64", 64), ("head96", 32)):
        c[name] = np.zeros((128, 64), f)
        c[name][:64, 32], c[name][64:64 + second, 33] = 1 / 64, 1 / second
    c["expand"] = np.kron(np.eye(32, dtype=f), np.ones((1, 64), f))
    rot = np.zeros((128, 128), f)
    for i in range(16):
        rot[64 + 16 + i, 64 + i] = -1
        rot[64 + i, 64 + 16 + i] = 1
    c["rot"] = rot
    inv = np.float32(10000.0) ** (-np.arange(0, 32, 2, dtype=f) / np.float32(32))
    ang = np.arange(SEQ, dtype=f)[:, None] * inv[None, :]
    cos, sin = np.cos(ang).T.astype(f), np.sin(ang).T.astype(f)
    tab = np.zeros((128, 4, SEQ), f)
    tab[:64, 0], tab[64:80, 0], tab[80:96, 0] = 1, cos, cos
    tab[64:80, 1], tab[80:96, 1] = sin, sin
    tab[:, 2:] = tab[:, :2] * f(96 ** -0.5)
    c["rope"] = tab.reshape(128, -1)
    k = np.arange(T)
    c["causal"] = np.where(k[None, :] <= SEQ // 2 + META + p[:, None], 0, NEG).astype(f)
    q = np.arange(2)
    small = np.where(np.arange(META)[None, :] <= Q0 + q[:, None], 0, NEG).astype(f)
    c["causal0"] = np.pad(small, ((0, 126), (0, 0)))
    x = np.arange(512)
    dist = 255 - x
    fam = []
    for keep in [dist >= 0, (dist >= 0) & (dist <= 128), (dist >= 0) & (dist % 4 == 0),
                 (dist >= 0) & (dist % 16 == 0)]:
        row = np.where(keep, t5_buckets(dist), 32)
        fam.append((np.arange(33)[:, None] == row[None, :]).astype(f))
    c["onehot"] = np.concatenate(fam, 1)
    n = np.arange(15)
    cend = 16 * n + 31
    dist = np.arange(SEQ)[None, :] - cend[:, None]
    ok = (dist >= 0).T.reshape(2, 128, 15).transpose(1, 0, 2)
    c["mask_c"] = ok.astype(f).reshape(128, 30)
    return c


CONST = [("ident", 128), ("mean64", 128), ("head64", 64), ("head96", 64), ("rot", 128),
         ("causal", T), ("causal0", META), ("mask_c", 30)]


def pack(x):
    f = np.float32
    out = {}
    x = {k: np.asarray(v) for k, v in x.items()}
    h = np.concatenate([x["meta"], x["x"][0]], 0)
    out["h0"] = h.T.reshape(KC, 128, T).transpose(1, 0, 2)

    def two(w, a, b, m=128):
        v = w.reshape(-1, 128, w.shape[1])
        u = [np.stack([v[:, :, i:i + m], v[:, :, j:j + m]], 0) for i, j in zip(a, b)]
        return np.stack(u).transpose(0, 3, 1, 2, 4).reshape(len(u), 128, -1)

    w = x["a_w_in"][0]
    g = [LRU * i for i in range(NLRU)]
    out["a_in"] = two(w, g, [D_RNN + i for i in g], LRU)
    w = x["a_w_out"][0].reshape(NLRU, LRU, KC, 128)
    out["a_out"] = w.transpose(2, 1, 0, 3).reshape(KC, LRU, -1)
    wr, wi = x["a_w_r"][0], x["a_w_i"][0]
    ri = np.stack([wr, wi], 1).reshape(4, 4, 2, LRU, LRU)
    out["a_ri"] = ri.transpose(0, 3, 1, 2, 4).reshape(4, LRU, -1)
    ch = [128 * i for i in range(64)]

    def ffn_out(w):
        w = w.reshape(2, KH, 128, KC, 128)
        return w.transpose(3, 0, 2, 1, 4).reshape(2 * KC, 128, -1)

    for l in range(2):
        out[f"f_in{l}"] = two(x["f_w_in"][l], ch[:NF], [D_FF + i for i in ch[:NF]])
        out[f"f_out{l}"] = ffn_out(x["f_w_out"][l])
    kv = x["kv_w"]
    fg = np.pad(kv[:, 2 * D:], ((0, 0), (0, 112)))
    out["fgate"] = fg.reshape(KC, 128, 128).transpose(1, 0, 2).reshape(1, 128, -1)
    out["kv"] = two(kv, ch[:KC], ch[KC:2 * KC])
    out["qg"] = two(x["b_w_in"][0], ch[:KC], ch[KC:2 * KC])
    out["b_out"] = two(x["b_w_out"][0], ch[0:KC:2], ch[1:KC:2])
    pad = D_FF - D_FF2
    for n in range(4):
        w = x["ffn_w_in_2"][n // 2, n % 2]
        w = np.pad(w.reshape(D, 2, D_FF2), ((0, 0), (0, 0), (0, pad))).reshape(D, -1)
        out[f"g_in{n}"] = two(w, ch[:NF], [D_FF + i for i in ch[:NF]])
        out[f"g_out{n}"] = ffn_out(np.pad(x["ffn_w_out_2"][n // 2, n % 2], ((0, pad), (0, 0))))
    w = x["ev_w_in_2"][0]
    at = dict(cq=0, ckv=256, kr=384, qn=416, kc=928, vc=1056, ks=1184, vs=1312, kw=1440, vw=1568, gl=1696)
    z = lambda n: np.zeros((D, n), f)
    krgl = np.concatenate([z(64), w[:, 384:416], w[:, 1696:1720], z(8)], 1)
    dup = lambda a, g: np.concatenate([w[:, a + 64 * g:a + 64 * g + 64]] * 2, 1)
    chunks = [w[:, 0:128], w[:, 128:256], w[:, 256:384], krgl]
    chunks += [w[:, at["qn"] + 128 * i:at["qn"] + 128 * i + 128] for i in range(4)]
    chunks += [dup(at["ks"], 0), dup(at["ks"], 1), dup(at["kw"], 0), dup(at["kw"], 1)]
    chunks += [w[:, at[n]:at[n] + 128] for n in ("kc", "vc", "vs", "vw")]
    w = np.concatenate(chunks, 1)
    out["ev_in"] = two(w, ch[0:16:2], ch[1:16:2])
    out["uq"] = x["mla_w_uq_2"][0].reshape(2, 128, 768).transpose(1, 0, 2).reshape(1, 128, -1)
    out["ukv"] = x["mla_w_ukv_2"][0].reshape(1, 128, 1024)
    w = x["nsa_cmp_w1_2"][0].reshape(2, 2, 8, 128, 256)
    out["cmp_w1"] = w.transpose(0, 1, 3, 2, 4).reshape(4, 128, -1)
    w = x["nsa_cmp_w2_2"][0].reshape(2, 2, 128, 64)
    out["cmp_w2"] = np.concatenate([w, w], 3).transpose(2, 0, 1, 3).reshape(128, -1)
    out["ev_out"] = two(x["ev_w_out_2"][0], ch[0:KC:2], ch[1:KC:2])
    out["od_in"] = two(x["od_w_in_2"][0], ch[0:24:2], ch[1:24:2])
    out["od_out"] = two(x["od_w_out_2"][0], ch[0:KC:2], ch[1:KC:2])
    w = x["ada_w_2"].reshape(2, KC, 128, ADA_T, 128)
    out["ada"] = w.transpose(0, 3, 2, 1, 4).reshape(2 * ADA_T, 128, -1)

    par = np.zeros((128, NPAR), f)

    def put(name, a, at=0):
        o, n = PAR[name]
        assert at + a.shape[1] <= n
        par[:a.shape[0], o + at:o + at + a.shape[1]] = a

    col = lambda v, m=128: np.asarray(v).reshape(-1, m).T
    put("conv_a_w", x["a_conv_w"][0].reshape(4, NLRU, LRU).transpose(2, 1, 0).reshape(LRU, -1))
    for n, s in (("conv_a_b", "a_conv_b"), ("b_r", "a_b_r"), ("b_i", "a_b_i"), ("lam", "a_lambda")):
        put(n, col(x[s][0], LRU))
    put("f_b", x["kv_f_b"][:, None])
    put("c", col(x["c_2"][0]))
    for n in ("ln1_g", "ln1_b", "ln2_g", "ln2_b"):
        put(n, col(x[n]))
    w = x["f_conv_w"].reshape(2, 3, 2 * NF, 128)
    put("conv_f_w", w.transpose(3, 0, 2, 1).reshape(128, -1))
    put("conv_f_b", col(x["f_conv_b"]))
    put("ada_b", col(x["ada_b_2"]))
    put("norm_g", col(x["norm_g_2"]))
    g = x["mla_qk_g_2"][0]
    put("mla_gq", g[0][:, None])
    put("mla_gk", g[1][:, None])
    put("mla_qn", col(x["mla_q_norm_g_2"][0]))
    put("mla_kvn", col(x["mla_kv_norm_g_2"][0]))
    for n in ("nsa", "dil", "moba"):
        g = x[n + "_qk_g_2"][0]
        put(n + "_g", np.concatenate([g, g], 1).T)
    pe = x["nsa_cmp_pe_2"][0].reshape(2, 16, 128)
    put("cmp_pe", pe.transpose(2, 0, 1).reshape(128, 32))
    out["par"] = par
    c = constants()
    out["const"] = np.concatenate([c[n] for n, _ in CONST], 1)
    out["rope"], out["expand"] = c["rope"][:96], c["expand"]
    out["onehot"] = c["onehot"]
    out["t5"] = np.concatenate([x["t5_bias_2"], np.full((1, HEADS), NEG, f)], 0)
    return out


def build(nc, ap):
    f32, f32r = mybir.dt.float32, mybir.dt.float32r
    ACT, ALU, AX = mybir.ActivationFunctionType, mybir.AluOpType, mybir.AxisListType
    st = stage_plan()
    order = list(st.values())
    TW = SEQ + 128
    toeplitz = nc.dram_tensor("toeplitz", [20, 128, TW], f32, kind="Internal").ap()

    gate_rows = nc.dram_tensor("gate_rows", [4, HEADS, T], f32, kind="Internal").ap()

    CH = T * 4
    FIRST = 16512
    where = FIRST

    def at(name, shape, dt, offset):
        return nc.alloc_sbuf_tensor_at(name, shape, dt, offset=offset)

    def sb(name, shape, dt=f32):
        nonlocal where
        t = at(name, shape, dt, where)
        size = 4 * math.prod(shape[1:])
        where += -(-size // 32) * 32
        return t

    raw = sb("raw", [128, RING, SLOT])
    whi = sb("whi", [128, 2, SLOT], f32r)
    res = sb("res", [128, KC, T])
    xhi = sb("xhi", [128, KC, T], f32r)
    xlo = sb("xlo", [128, KC, T], f32r)
    ada_w = sb("ada_w", [128, 2, KC, 128])
    ada_s = sb("ada_s", [128, MOD_N * 128])
    par = sb("par", [128, NPAR])
    const = sb("const_sb", [128, sum(n for c, n in CONST)])
    ones = sb("ones", [128, 128])
    one1 = sb("one1", [128, 1])
    eps = sb("eps", [128, 2])
    std = sb("std", [128, T])
    c_act = sb("c_act", [128, KC])
    mod = sb("mod", [128, 2, ADA_T])
    g8 = sb("g8", [128, 3])
    t5 = sb("t5_sb", [33, HEADS])
    gs = sb("gs", [128, 2, 3 * KC])
    sp8 = sb("sp8", [LRU, NLRU])
    expand = sb("expand_sb", [32, 2048], f32r)
    sq = sb("sq", [128, 2, T])
    small = sb("small", [128, 8, 2, 6])
    R0 = where
    W0 = R0 + 44 * CH
    wlo = at("wlo", [128, RING, SLOT], f32r, FIRST)
    W_SIZE = 36 * CH + 512
    assert W0 + W_SIZE <= nc.sbuf_usable_end

    hhi = at("hhi", [128, NF, T], f32r, R0)
    hlo = at("hlo", [128, NF, T], f32r, R0 + NF * CH)
    dev = at("dev", [128, KC, T], f32, R0)
    dsq = at("dsq", [128, KC, T], f32, R0 + KC * CH)
    w_ri = at("w_ri", [LRU, 4, 2, LRU], f32, R0 + 16 * CH)
    lam_t = at("lam_t", [LRU, 8, NLRU], f32, W0 + W_SIZE - 512)
    lr, li, la, lt, l2 = (at(n, [LRU, 4, T], f32, W0 + i * 4 * CH)
                          for i, n in enumerate(("lr", "li", "la", "lt", "l2")))
    lg, lx = (at(n, [LRU, 2, 4, T], f32, W0 + (20 + 8 * i) * CH) for i, n in enumerate(("lg", "lx")))
    cg, cv, gg, hf = (at(n, [128, 2, T], f32, W0 + i * 2 * CH)
                      for i, n in enumerate(("cg", "cv", "gg", "hf")))

    z = at("z", [128, 44, T], f32, R0)
    vt = at("vt", [128, KC, 3, 128], f32, R0 + 32 * CH)
    c_lhs = at("c_lhs", [128, 4, T], f32r, W0)
    c_rhs = at("c_rhs", [128, 4, T], f32r, W0 + 4 * CH)
    early = at("early", [2, HEADS, 16], f32, W0 + 8704)
    early_t = at("early_t", [16, HEADS, 2], f32, W0 + 9728)
    early_m = at("early_m", [2, 3, HEADS], f32, W0 + 9856)
    ft = at("ft", [16, 9, T], f32, W0 + 10240)
    c_part = at("c_part", [16, 4, T], f32r, W0 + 20032)
    fr = at("fr", [16, T], f32, W0 + 24384)
    probs = at("probs", [128, 6, 416], f32, W0 + 16384)
    pt = at("pt", [128, 2, 384], f32, W0 + 26368)
    pt_small = at("pt_small", [16, 2, T], f32, W0 + 29440)

    q96 = at("q96", [96, 9, SEQ], f32, R0 + 16 * CH)
    kf = at("kf", [96, 8, SEQ], f32, R0 + 25 * CH)
    zkv = at("zkv", [128, 8, SEQ], f32, R0 + 33 * CH)
    w2_cmp = at("w2_cmp", [128, 2, 2, 128], f32, R0 + 41 * CH)
    a2 = at("a2", [128, 2, 2, SEQ], f32, R0 + 16 * CH)
    x2 = at("x2", [128, 2, 16, 2, 15], f32, R0 + 20 * CH)
    x2_hi = at("x2_hi", [128, 2, 16, 30], f32r, R0 + 24 * CH)
    x2_lo = at("x2_lo", [128, 2, 16, 30], f32r, R0 + 28 * CH)
    v_nsa = at("v_nsa", [128, 4, 128], f32, R0 + 32 * CH)
    hid = at("hid", [128, 2, 2, 30], f32, R0 + 34 * CH)
    hid_t = at("hid_t", [30, 2, 256], f32, R0 + 38 * CH)
    v_cmp = at("v_cmp", [15, 2, 64], f32, R0 + 35 * CH)
    k_cmp = at("k_cmp", [128, 30], f32, R0 + 36 * CH)
    gates = at("gates", [128, 2, 24], f32, R0 + 37 * CH)
    v_odd = at("v_odd", [128, 8, 2, 128], f32, R0 + 24 * CH)
    rope = at("rope", [96, 4, SEQ], f32, W0)
    vm = at("vm", [128, 8, 2, 64], f32, W0 + 4096)
    bias_even = at("bias_even", [128, 8, SEQ], f32, W0 + 8192)
    bias_odd = at("bias_odd", [128, 16, SEQ], f32, W0)
    lat_hi = at("lat_hi", [128, 3, SEQ], f32r, W0 + 31744)
    lat_lo = at("lat_lo", [128, 3, SEQ], f32r, W0 + 34816)
    n_sq = at("n_sq", [128, 2, 512], f32, W0 + 16384)
    n_std = at("n_std", [128, 2, SEQ], f32, W0 + 20480)
    h_std = at("h_std", [32, SEQ], f32, W0 + 22528)
    h_hi = at("h_hi", [32, SEQ], f32r, W0 + 23552)
    h_lo = at("h_lo", [32, SEQ], f32r, W0 + 24576)
    rot_t = at("rot_t", [96, 2, 512], f32, W0 + 25600)
    onehot = at("onehot", [33, 2048], f32, R0 + 22 * CH)
    expand_f = at("expand_f", [32, 2048], f32, R0 + 8192)
    t_rows = at("t_rows", [8, 4, 512], f32, R0)

    coff, o = {}, 0
    for name, n in CONST:
        coff[name] = (o, n)
        o += n

    def con(name):
        o, n = coff[name]
        return const[:, o:o + n]

    ident = con("ident")

    def pcol(name, i, rows=128):
        o = PAR[name][0]
        return par[0:rows, o + i:o + i + 1] if isinstance(i, int) else par[0:rows, bass.ds(i + o, 1)]

    def chunk(t, i, t0=0, rows=128, n=1):
        if isinstance(i, int):
            return t[0:rows, i, t0:T] if n == 1 else t[0:rows, i:i + n, t0:T]
        v = t[0:rows, bass.ds(i, n), t0:T]
        return v.rearrange("p o t -> p (o t)") if n == 1 else v

    ctx = ExitStack()
    with ctx:
        ps = ctx.enter_context(nc.psum_tensor("ps", [128, 8, 512], f32))
        sems = {}

        def S(name):
            if name not in sems:
                sems[name] = ctx.enter_context(nc.semaphore(name))
            return sems[name]

        w_loaded = [S(f"w_loaded{slot}") for slot in range(RING)]
        w_hi, w_lo, w_used, acc_free = S("w_hi"), S("w_lo"), S("w_used"), S("acc_free")
        block = ctx.enter_context(nc.Block())

        def row(t, i):
            return t[i] if isinstance(i, int) else t[bass.ds(i, 1)].rearrange("o p c -> (o p) c")

        def ahead(s, it):
            k = it.k + 2
            if it.j is not None or k < s.n:
                return s, it.next(2)
            i = order.index(s) + 1
            while i < len(order) and k - s.n >= order[i].n:
                k, s, i = k - s.n, order[i], i + 1
            return (order[i], It(k - s.n)) if i < len(order) else (None, None)

        class Head:
            pass

        def causal(tile, width):
            o = coff["causal"][0]
            return const[:, o + T - width:o + T]

        fox_steps = []
        for h in range(HEADS):
            j, b = h // 2, h % 2
            p = slice(64 * b, 64 * b + 64)
            r = slice(32 * (h // 4), 32 * (h // 4) + 4)
            s = Head()
            q, k = z[p, 16 + j, :], z[p, j, :]
            ca, cb = c_lhs[r, h % 4, :], c_rhs[r, h % 4, :]
            s.qk = [[(q[:, 16:144], k[:, 0:144]), (ca[:, 16:144], cb[:, 0:144])],
                    [(q[:, 144:T], k[:, 0:T]), (ca[:, 144:T], cb[:, 0:T])]]
            s.cols = [(0, 144), (144, 416)]
            s.bias = [causal(0, 144), causal(1, T)]
            s.turn = [(0, 16, 144, 0), (1, 160, 288, 128), (1, 288, 416, 256)]
            s.small = [(0, 0, 16, 0), (1, 144, 160, 128)]
            c = slice(64 * b, 64 * b + 64)
            s.pv = [(vt[0:16, j, 0, c], 1, 0, 258, 16, 0), (vt[:, j, 1, c], 0, 0, 256, 128, 2),
                    (vt[:, j, 2, c], 0, 256, 384, 128, 130)]
            s.rows, s.half, s.gate, s.mask, s.n_q, s.head = 128, b, None, None, T - Q0, h
            fox_steps.append(s)

        class Run:
            steps_before = pairs_before = 0

            def __init__(self, before, steps, groups, lag, x, t0, out_gate=None, first_pair=0):
                self.steps, self.lag, self.x, self.t0, self.out_gate = steps, lag, x, t0, out_gate
                self.B = before.B + len(before.steps) if before else 0
                self.P = before.P + before.n_pairs if before else 0
                self.first_pair = first_pair
                n = 0
                for size, in_chunk_end in groups:
                    for i in range(size):
                        s = steps[n + i]
                        s.group = list(range(n, n + size))
                        s.ends = i == size - 1
                    n += size
                self.pair_of, self.pair_end, p = [], {}, 0
                for i, s in enumerate(steps):
                    self.pair_of.append(p)
                    if i + 1 == len(steps) or (s.half == 1 and steps[i + 1].half == 0):
                        self.pair_end[i] = p
                        p += 1
                self.n_pairs = p
                for i, s in enumerate(steps):
                    head0 = i == 0 or steps[i - 1].half != s.half
                    headn = i + 1 == len(steps) or steps[i + 1].half != s.half
                    s.first_of_head, s.last_of_head = head0, headn

        fox = Run(None, fox_steps, [(1, 0)] * HEADS, 2, X["fox_o"], Q0, out_gate=24)
        def both(tile, width):
            return [causal(0, 128), causal(1, SEQ)]

        def seq_step(q, k, v, bias, half, gate=None):
            s = Head()
            s.qk = [[(q[:, 0:128], k[:, 0:128])], [(q[:, 128:SEQ], k[:, 0:SEQ])]]
            s.cols = [(0, 128), (128, 384)]
            s.bias = bias
            s.turn = [(0, 0, 128, 0), (1, 128, 256, 128), (1, 256, 384, 256)]
            s.small = []
            s.pv = [(v[0], 0, 0, 256, 128, 0), (v[1], 0, 256, 384, 128, 128)]
            s.half, s.gate, s.mask = half, gate, None
            return s

        def toeplitz_bias(t, i):
            return [t[:, i, 128:SEQ], t[:, i, :]]

        def zc(p, i):
            return z[p, i, META:T]

        halves = [slice(0, 64), slice(64, 128)]
        mla = Run(fox, [seq_step(q96[:, h, :], kf[:, h, :], [vm[:, h, 0, :], vm[:, h, 1, :]],
                                 [causal(0, 128), causal(1, SEQ)], h % 2) for h in range(8)],
                  [(1, 0)] * 8, 2, X["ev_o"], META)
        steps = []
        for h in range(8):
            g, b, p = h // 4, h % 2, halves[h % 2]
            q = zc(p, 4 + h // 2)
            c = slice(64 * g, 64 * g + 64)
            s = Head()
            kc = k_cmp[p, 15 * g:15 * g + 15]
            s.qk = [[(q[:, 0:128], kc[:, 0:7])], [(q[:, 128:SEQ], kc)]]
            s.cols = [(0, 7), (16, 31)]
            s.bias = [bias_even[:, h, 128 + 31:SEQ:16], bias_even[:, h, 31:SEQ:16]]
            s.turn = [(0, 0, 7, 0), (1, 16, 31, 128)]
            s.small = []
            s.pv = [(v_cmp[0:7, g, :], 0, 0, 128, 7, 0), (v_cmp[0:15, g, :], 0, 128, 256, 15, 128)]
            s.half, s.gate = b, gates[:, :, 3 * h]
            s.mask = [con("mask_c")[:, 0:7], con("mask_c")[:, 15:30]]
            steps.append(s)
            for i, kz in ((0, 8), (1, 10)):
                steps.append(seq_step(q, zc(p, kz + g), [v_nsa[:, 2 * i, c], v_nsa[:, 2 * i + 1, c]],
                                      toeplitz_bias(bias_even, h), b, gates[:, :, 3 * h + 1 + i]))
        nsa = Run(mla, steps, [(1, 0)] * 24, 2, X["ev_o"] + 4, META, first_pair=4)
        steps = []
        for s in range(4):
            for g in range(3):
                c, p = 2 * g + s // 2, halves[s % 2]
                steps.append(seq_step(zc(p, c), zc(p, 6 + c), [v_odd[:, c, t, p] for t in range(2)],
                                      toeplitz_bias(bias_odd, 4 * g + s), s % 2))
        for h in range(4):
            p = halves[h % 2]
            steps.append(seq_step(zc(p, 18 + h // 2), zc(p, 20 + h // 2),
                                  [v_odd[:, 6 + h // 2, t, p] for t in range(2)],
                                  toeplitz_bias(bias_odd, 12 + h), h % 2))
        odd = Run(nsa, steps, [(3, 0)] * 4 + [(1, 0)] * 4, 4, X["od_o"], META)

        class Norm:

            def __init__(self, src, n, sums, scale, outs, rows=128):
                self.src, self.n, self.sums, self.scale, self.outs, self.rows = src, n, sums, scale, outs, rows


        def gcol(name, i=0, rows=128):
            o = PAR[name][0] + i
            return par[0:rows, o:o + 1]

        class Heads:

            def __init__(self, src, first, table, g, dst, rows=128, step=2):
                self.src, self.table, self.g, self.dst, self.rows = src, table, g, dst, rows
                self.firsts = [first, first + step] if len(src.shape) == 3 else [first]
                self.n = SEQ * len(self.firsts)

        def heads_norm(i, first, g):
            v = z[:, i:i + 2, META:T]
            return Heads(v, first, con("head64"), g, v)

        latent_norms = [
            Norm(z[:, 0:2, META:T], SEQ, [(ones[:, :], 0, SEQ), (ones[:, :], SEQ, 2 * SEQ)], D / 256,
                 [(z[:, i, META:T], gcol("mla_qn", i), z[:, i, META:T]) for i in range(2)]),
            Norm(z[:, 2, META:T], SEQ, [(ones[:, :], 0, SEQ)], D / 128,
                 [(z[:, 2, META:T], gcol("mla_kvn"), z[:, 2, META:T])])]
        k_gain = gcol("mla_gk", 0, 64)
        mla_heads = [Heads(q96[:, 2 * i:2 * i + 2, :], 4 * i, con("head96"), gcol("mla_gq", 0, 96),
                           q96[:, 2 * i:2 * i + 2, :], 96) for i in range(4)]
        mla_heads.append(Heads(z[0:96, 3, META:T], 16, con("head96"), gcol("mla_gk", 0, 96), q96[:, 8, :], 96))
        mla_heads += [Heads(zkv[0:64, 2 * i:2 * i + 2, :], 18 + 2 * i, con("head64"), k_gain,
                            kf[0:64, 2 * i:2 * i + 2, :], 64, 1) for i in range(4)]
        nsa_heads = [heads_norm(4 + 2 * i, 4 * i, g8[:, 0:1] if i < 2 else gcol("nsa_g", 1)) for i in range(4)]
        odd_heads = [heads_norm(2 * i, 4 * i, g8[:, 1:2] if i < 3 else gcol("dil_g", 1)) for i in range(6)]
        odd_heads += [heads_norm(18, 24, g8[:, 2:3]), heads_norm(20, 28, gcol("moba_g", 1))]
        cmp_norms = [Norm(k_cmp[:, :], 30, [(con("mean64"), 0, 30)], 1.0,
                          [(k_cmp[:, :], gcol("nsa_g", 1), k_cmp[:, :])])]
        for i, item in enumerate(latent_norms + cmp_norms):
            item.i = i
        for i, item in enumerate(mla_heads + nsa_heads + odd_heads):
            item.i = i
        lots = [mla_heads, nsa_heads, odd_heads]

        @block.sync
        def _(e):
            e.dma_start(res[:, :, :], ap["h0"]).then_inc(S("h0_in"), 16)
            e.dma_start(par[:, :], ap["par"]).then_inc(S("par_in"), 16)

            def load(s, it, name):
                slot, c, src = (s.U + it.k) % RING, s.cols // 2, row(ap[name], it.of())
                wait(e, w_used, it.of(s.U) - (RING - 3))
                for h in range(2):
                    e.dma_start(raw[0:s.rows, slot, h * c:(h + 1) * c], src[:, h * c:(h + 1) * c])\
                        .then_inc(w_loaded[slot], 16)

            def bias_rows(to, n, row):
                skewed = [[TW - 1, 128], [128 * TW, n], [1, SEQ]]
                e.dma_start(to, bass.AP(toeplitz.tensor, row * 128 * TW + 127, skewed))\
                    .then_inc(S("bias_in"), 16)

            def sp_even():
                e.wait_ge(S("h_lo"), 3 * NF)
                e.dma_start(rope[:, :, :].rearrange("p a b -> p (a b)"), ap["rope"]).then_inc(S("rope_in"), 16)

            def sp_nsa():
                e.wait_ge(S("pv_mm"), mla.B + 8)
                for g in range(2):
                    for j in range(2):
                        src = z[64 * g:64 * g + 64, 12 + j, :]
                        e.dma_start(a2[0:64, j, g, :], src[:, META:T]).then_inc(S("a2_in"), 16)
                        e.dma_start(a2[64:128, j, g, 0:SEQ - 1], src[:, META + 1:T]).then_inc(S("a2_in"), 16)

            def sp_forget():
                e.wait_ge(S("forget_step"), FORGET_STEPS)
                e.dma_start(gate_rows.rearrange("c h t -> h c t"), c_part[:, :, :].bitcast(f32))\
                    .then_inc(S("gates_out"), 16)
                e.wait_ge(S("gates_out"), 16)
                for to, row0, part in ((c_lhs, 0, 0), (c_lhs, 1, 1), (c_rhs, 2, 2), (c_rhs, 3, 3)):
                    e.dma_start(to[row0:128:32, :, :].bitcast(f32),
                                gate_rows[part].rearrange("(q h) t -> q h t", q=4)).then_inc(S("forget_in"), 16)

            for name, s in st.items():
                if name == "a_in":
                    def group(it, first, last):
                        for b in range(4):
                            load(s, It(4 * it.k + b, it.j, 4), name)
                            if b == 3:
                                e.wait_ge(S("ri_mm"), it.of() * 4 + 1)
                                e.dma_start(w_ri[:, :, :, :].rearrange("p a b c -> p (a b c)"),
                                            row(ap["a_ri"], it.of())).then_inc(S("ri_in"), 16)
                    sweep(e, GROUPS, group, 1, 1, 1)
                elif name == "cmp_w1":
                    for u in range(4):
                        load(s, It(u), name)
                    sp_nsa()
                else:
                    sweep(e, s.n, lambda it, a, b: load(s, it, name), s.n % RING, 0)
                if name == "g_out0":
                    sp_even()
                if name == "ev_in":
                    e.wait_ge(acc_free, s.A + 3)
                    e.dma_start(w2_cmp[:, :, :, :].rearrange("p a b c -> p (a b c)"), ap["cmp_w2"])\
                        .then_inc(S("w2_in"), 16)
                    bias_rows(bias_even[:, 0:4, :], 4, 16)
                    bias_rows(bias_even[:, 4:8, :], 4, 12)
                if name == "od_in":
                    bias_rows(bias_odd[:, :, :], 16, 0)
                if name == "qg":
                    sp_forget()
            e.wait_ge(acc_free, order[-1].A + order[-1].groups + 2)
            e.dma_start(ap["out"], res[:, :, META:T]).then_inc(S("stored"), 16)
            e.wait_ge(S("stored"), 16)

        @block.gpsimd
        def _(e):
            e.memset(ones[:, :], 1.0 / D).then_inc(S("consts_set"), 1)
            e.memset(one1[:, :], 1.0).then_inc(S("consts_set"), 1)
            e.memset(eps[:, 0:1], LN_EPS).then_inc(S("consts_set"), 1)
            e.memset(eps[:, 1:2], RMS_EPS).then_inc(S("consts_set"), 1)
            e.wait_ge(S("t5_out"), 1)
            e.dma_start(expand_f[:, :], ap["expand"]).then_inc(S("expand_in"), 16)
            for to, i, a, n in ((0, 1, 0, 4), (4, 2, 0, 4), (8, 3, 0, 4), (12, 0, 4, 4), (16, 0, 0, 4)):
                e.dma_start(toeplitz[to:to + n], t_rows[a:a + n, i, 0:TW].unsqueeze(1).broadcast_to([n, 128, TW]))\
                    .then_inc(S("toeplitz_out"), 16)
            e.dma_start(const[:, :], ap["const"]).then_inc(S("const_in"), 16)
            e.wait_ge(S("expand_in"), 16)
            e.tensor_copy(expand[:, :], expand_f[:, :]).then_inc(S("expand"), 1)
            e.wait_ge(S("c_act"), 1)
            step = S("ada_step")

            def load(i, b):
                e.dma_start(ada_w[:, b, :, :].rearrange("p k c -> p (k c)"), row(ap["ada"], i))\
                    .then_inc(S(f"ada_in{b}"), 16)

            load(0, 0)
            load(1, 1)
            for part in range(2 * ADA_T // MOD_N):
                def tile(it, first, last):
                    b, n = it.k % 2, it.of(part * MOD_N) * 4
                    w = ada_w[:, b, :, :]
                    e.wait_ge(S(f"ada_in{b}"), it.of(part * MOD_N, 2) * 16 + 16)
                    e.tensor_tensor(w, w, c_act[:, :].unsqueeze(2).broadcast_to([128, KC, 128]), ALU.mult)\
                        .then_inc(step, 1)
                    e.wait_ge(step, n + 1)
                    e.tensor_tensor(w[:, 0:4], w[:, 0:4], w[:, 4:8], ALU.add).then_inc(step, 1)
                    e.wait_ge(step, n + 2)
                    e.tensor_tensor(w[:, 0:2], w[:, 0:2], w[:, 2:4], ALU.add).then_inc(step, 1)
                    e.wait_ge(step, n + 3)
                    if first and part:
                        e.wait_ge(S("mod_mm"), part)
                    i = it.of()
                    to = ada_s[:, 128 * i:128 * i + 128] if isinstance(i, int) else ada_s[:, bass.ds(i * 128, 128)]
                    e.tensor_tensor(to, w[:, 0], w[:, 1], ALU.add).then_inc(step, 1)
                    if part * MOD_N + it.k + 2 < 2 * ADA_T:
                        e.wait_ge(step, n + 4)
                        load(it.of(part * MOD_N + 2), b)
                sweep(e, MOD_N, tile, 2, 2, 2)

        @block.tensor
        def _(e):
            e.nop().then_inc(w_used, 2)
            e.nop().then_inc(S("ri_mm"), 1)
            e.wait_ge(S("consts_set"), 4)

            def mm3(out, s, slot, off, m, hi, lo, start, stop):
                k = s.rows
                e.matmul(out, whi[0:k, slot % 2, off:off + m], hi, start=start, stop=False)
                e.matmul(out, whi[0:k, slot % 2, off:off + m], lo, start=False, stop=False)
                return e.matmul(out, wlo[0:k, slot, off:off + m], hi, start=False, stop=stop)

            def in_unit(s, it, t0, m=128, halves=2, x_from=None):
                slot, acc = (s.U + it.k) % RING, (s.A + it.k) % 2
                e.wait_ge(w_lo, it.of(s.U) + 3)
                e.wait_ge(acc_free, it.of(s.A) + 1)
                for half in range(halves):
                    for k in range(KC):
                        if half == 0 and x_from is not None:
                            e.wait_ge(S("x"), x_from + k + 1)
                        o = mm3(ps[0:m, 2 * acc + half, 0:T - t0], s, slot, (half * KC + k) * m, m,
                                xhi[:, k, t0:T], xlo[:, k, t0:T], k == 0, k == KC - 1)
                o.then_inc(w_used, 1)

            def stage_in(name, t0, x_from, halves=2):
                s = st[name]
                sweep(e, s.n, lambda it, first, last: in_unit(s, it, t0, 128, halves, x_from if first else None),
                      2, 0)

            def column_sums(src, n, m, sem):
                e.matmul(ps[:, 7, 0:n], ones[:, :], src, start=isinstance(m, int) and m == 0,
                         stop=isinstance(m, int) and m == KC - 1).then_inc(S(sem), 1)

            def stage_out(name, hi, lo, t0, chunks, ready, ln=None, rms=None):
                s = st[name]
                n, n_m, rows = T - t0, KC * s.per // s.n, s.rows
                kk = chunks // s.per

                def sums(g, parity):
                    for h in range(n_m):
                        m = g * n_m + h
                        if ln is not None:
                            e.wait_ge(acc_free, g + (s.A + 3))
                            column_sums(chunk(res, m, t0), n, m, "mean_mm")
                        else:
                            e.wait_ge(S("sq"), m + (KC * rms + 1))
                            column_sums(sq[:, (n_m * parity + h) % 2, t0:T], n, m, "sq_mm")

                def unit(it, first, last):
                    slot, g, part = (s.U + it.k) % RING, it.k // s.per, it.k % s.per
                    acc = (s.A + g) % 2
                    e.wait_ge(w_lo, it.of(s.U) + 3)
                    if part == 0:
                        e.wait_ge(acc_free, it.of(0, s.per) + (s.A + 1))
                    if it.k in ready and it.j is None:
                        e.wait_ge(*ready[it.k])
                    for half in range(n_m):
                        for k in range(kk):
                            kx = part * kk + k
                            o = mm3(ps[:, 2 * acc + half, 0:n], s, slot, (half * kk + k) * 128, 128,
                                    hi[0:rows, kx, t0:T], lo[0:rows, kx, t0:T], kx == 0, kx == chunks - 1)
                    o.then_inc(w_used, 1)
                    if part == s.per - 1 and not (it.j is None and g == 0) and not (ln is None and rms is None):
                        sums(it.of(0, s.per) - 1, (g - 1) % 2)
                sweep(e, s.n, unit, RING, 0)
                if not (ln is None and rms is None):
                    sums(s.n // s.per - 1, (s.n // s.per - 1) % 2)

            def modulation(part):
                e.wait_ge(S("ada_step"), 4 * MOD_N * (part + 1))
                wait(e, S("mod_in"), part)
                for j in range(MOD_N):
                    o = e.matmul(ps[:, 5, j:j + 1], ada_s[:, 128 * j:128 * j + 128], one1[:, :],
                                 start=True, stop=True)
                o.then_inc(S("mod_mm"), 1)

            def variance(i, t0):
                for k in range(KC):
                    e.wait_ge(S("dsq"), KC * i + k + 1)
                    e.matmul(ps[:, 6, 0:T - t0], ones[:, :], dsq[:, k, t0:T], start=k == 0, stop=k == KC - 1)\
                        .then_inc(S("var_mm"), 1)

            def attention(run):
                n, lag = len(run.steps), run.lag

                def scores(i):
                    s, g = run.steps[i], run.B + i
                    wait(e, S("scored"), g - 1)
                    for tile in range(2):
                        terms = s.qk[tile]
                        for t, (q, k) in enumerate(terms):
                            c0, c1 = s.cols[tile]
                            o = e.matmul(ps[:, 4 + g % 2, c0:c1], q, k, start=t == 0, stop=t == len(terms) - 1)
                    o.then_inc(S("qk_mm"), 1)

                def turn(i):
                    s, g = run.steps[i], run.B + i
                    e.wait_ge(S("prob"), g + 1)
                    wait(e, S("turned"), g - 1)
                    p = probs[:, g % 6, :]
                    for tile, a, b, to in s.small:
                        e.matmul(ps[0:b - a, 2 + g % 2, to:to + 128], p[:, a:b], ident, start=True, stop=True)
                    for tile, a, b, to in s.turn:
                        if b - a == 128:
                            o = e.transpose(ps[:, 6 + g % 2, to:to + 128], p[:, a:b], ident)
                        else:
                            o = e.matmul(ps[0:b - a, 6 + g % 2, to:to + 128], p[:, a:b], ident,
                                         start=True, stop=True)
                    o.then_inc(S("turn_mm"), 1)

                def values(i):
                    s, g, pair = run.steps[i], run.B + i, run.P + run.pair_of[i]
                    e.wait_ge(S("turned"), g + 1)
                    if s.first_of_head and s.half == 0:
                        wait(e, S("o_out"), pair - 1)
                    out = ps[64 * s.half:64 * s.half + 64, pair % 2, :]
                    for t, (v, small, a, b, keys, to) in enumerate(s.pv):
                        src = (pt_small if small else pt)[0:keys, g % 2, a:b]
                        o = e.matmul(out[:, to:to + b - a], v, src,
                                     start=s.first_of_head and t == 0,
                                     stop=s.last_of_head and t == len(s.pv) - 1)
                    o.then_inc(S("pv_mm"), 1)

                for t in range(n + lag + 1):
                    if t < n:
                        scores(t)
                    if 0 <= t - lag < n:
                        turn(t - lag)
                    if 0 <= t - lag - 1:
                        values(t - lag - 1)

            def pe_fox():
                kv, qg = st["kv"], st["qg"]
                e.wait_ge(acc_free, kv.A + kv.n + 2)
                e.wait_ge(S("const_in"), 16)
                for j in range(KC):
                    wait(e, S("vt"), j - 1)
                    v, b = z[:, 8 + j, :], 6 + j % 2
                    e.transpose(ps[:, b, 0:128], v[:, 16:144], ident)
                    e.transpose(ps[:, b, 128:256], v[:, 144:T], ident)
                    e.matmul(ps[0:16, b, 256:384], v[:, 0:16], ident, start=True, stop=True).then_inc(S("vt_mm"), 1)
                e.wait_ge(acc_free, qg.A + qg.n + 2)
                e.wait_ge(S("forget_in"), 16 * 4)
                for h in range(HEADS):
                    s, r = fox_steps[h], slice(32 * (h // 4), 32 * (h // 4) + 4)
                    p = slice(64 * (h % 2), 64 * (h % 2) + 64)
                    q, k = z[p, 16 + h // 2, :], z[p, h // 2, :]
                    o = ps[0:2, 2, 16 * h:16 * h + 16]
                    wait(e, S("early_mm"), h)
                    e.matmul(o, q[:, Q0:16], k[:, 0:16], start=True, stop=False)
                    e.matmul(o, c_lhs[r, h % 4, Q0:16].bitcast(f32), c_rhs[r, h % 4, 0:16].bitcast(f32),
                             start=False, stop=True).then_inc(S("early_mm"), 1)
                e.wait_ge(S("early"), 4)
                for h in range(HEADS):
                    e.matmul(ps[0:16, 3, 2 * h:2 * h + 2], early[:, h, :], ident[0:2, 0:2], start=True, stop=True)\
                        .then_inc(S("early_mm"), 1)
                e.wait_ge(S("early_t"), 1)
                attention(fox)

            def norms(items):
                for it in items:
                    e.wait_ge(S("n_sq"), it.i + 1)
                    wait(e, S("n_std"), it.i - 1)
                    r = it.rows
                    for t, (m, a, b) in enumerate(it.sums):
                        o = e.matmul(ps[0:r, 4 + it.i % 2, 0:b - a], m, n_sq[0:r, it.i % 2, a:b],
                                     start=t == 0, stop=t == len(it.sums) - 1)
                    o.then_inc(S("n_mm"), 1)

            def heads(lot):
                for at_, it in enumerate(lot):
                    e.wait_ge(S("h_sq"), it.i + 1)
                    for t, first in enumerate(it.firsts):
                        o = e.matmul(ps[0:32, 4, 0:SEQ], it.table[0:it.rows, 32 - first:64 - first],
                                     n_sq[0:it.rows, it.i % 2, SEQ * t:SEQ * t + SEQ],
                                     start=at_ == 0 and t == 0, stop=at_ == len(lot) - 1 and t == len(it.firsts) - 1)
                    o.then_inc(S("h_mm"), 1)
                e.wait_ge(S("expand"), 1)
                e.wait_ge(S("h_rstd"), 3 * lots.index(lot) + 3)
                for it in lot:
                    wait(e, S("h_out"), it.i - 2)
                    for t, first in enumerate(it.firsts):
                        for part in (h_hi, h_lo):
                            o = e.matmul(ps[0:it.rows, 5 + it.i % 3, SEQ * t:SEQ * t + SEQ],
                                         expand[:, 64 * first:64 * first + it.rows], part[:, :],
                                         start=part is h_hi, stop=part is h_lo)
                    o.then_inc(S("h_mm2"), 1)

            def swiglu(i, x):
                f = NF * (2 + i)
                stage_in(f"g_in{i}", META, x)
                stage_out(f"g_out{i}", hhi, hlo, META, NF, {0: (S("h_lo"), f + KH), 1: (S("h_lo"), f + NF)},
                          rms=[1, 3, 4, None][i])

            def pe_even():
                s = st["ev_in"]
                for u in range(s.n):
                    in_unit(s, It(u), META, 128, 2, X["ev"] if u == 0 else None)
                    if u == 3:
                        norms(latent_norms)
                e.wait_ge(acc_free, s.A + s.n + 2)
                e.wait_ge(S("latent"), 3)
                s = st["uq"]
                e.wait_ge(w_lo, s.U + 3)
                for h in range(8):
                    for k in range(2):
                        to = SEQ * (h % 2)
                        o = mm3(ps[0:96, h // 2, to:to + SEQ], s, s.U % RING, k * 768 + h * 96, 96,
                                lat_hi[:, k, :], lat_lo[:, k, :], k == 0, k == 1)
                o.then_inc(w_used, 1)
                s = st["ukv"]
                e.wait_ge(w_lo, s.U + 3)
                e.wait_ge(S("q_out"), 4)
                for h in range(8):
                    o = mm3(ps[:, h // 2, SEQ * (h % 2):SEQ * (h % 2) + SEQ], s, s.U % RING, h * 128, 128,
                            lat_hi[:, 2, :], lat_lo[:, 2, :], True, True)
                o.then_inc(w_used, 1)
                e.wait_ge(S("kv_out"), 4)
                for h in range(8):
                    for t in range(2):
                        c = (2 * (h % 4) + t) * 64
                        o = e.transpose(ps[:, h // 4, c:c + 64], zkv[64:128, h, 128 * t:128 * t + 128],
                                        ident[64:128, 64:128])
                o.then_inc(S("vm_mm"), 1)
                heads(mla_heads)
                for i in range(5):
                    n = 512 if i < 4 else SEQ
                    src = q96[:, 2 * i:2 * i + 2, :] if i < 4 else q96[:, 8, :]
                    e.wait_ge(S("h_out"), mla_heads[i].i + 1)
                    wait(e, S("rotated"), i - 1)
                    e.matmul(ps[0:96, 2 + i % 2, 0:n], con("rot")[0:96, 0:96], src, start=True, stop=True)\
                        .then_inc(S("rot_mm"), 1)
                e.wait_ge(S("vm"), 1)
                e.wait_ge(S("k_rope"), 1)
                e.wait_ge(S("h_out"), mla_heads[-1].i + 1)
                attention(mla)
                heads(nsa_heads)
                e.wait_ge(S("o_out"), mla.P + 4)
                for i in range(2):
                    for t in range(2):
                        e.transpose(ps[:, 2, 128 * (2 * i + t):128 * (2 * i + t) + 128],
                                    z[:, 14 + i, META + 128 * t:META + 128 * t + 128], ident)
                for t in range(2):
                    o = e.transpose(ps[:, 3, 128 * t:128 * t + 128], z[:, 3, META + 128 * t:META + 128 * t + 128], ident)
                o.then_inc(S("vn_mm"), 1)
                e.wait_ge(S("vn"), 1)
                e.wait_ge(S("x2"), 1)
                s = st["cmp_w1"]
                for j in range(2):
                    for part in range(2):
                        u = s.U + 2 * j + part
                        e.wait_ge(w_lo, u + 3)
                        for k in range(8):
                            i, c = 8 * part + k, slice(256 * k, 256 * k + 256)
                            hi, lo, out = x2_hi[:, j, i, :], x2_lo[:, j, i, :], ps[0:30, 2 * j, 0:256]
                            e.matmul(out, hi, whi[:, u % 2, c], start=i == 0, stop=False)
                            e.matmul(out, hi, wlo[:, u % RING, c], start=False, stop=False)
                            o = e.matmul(out, lo, whi[:, u % 2, c], start=False, stop=i == 15)
                        o.then_inc(w_used, 1)
                for j in range(2):
                    e.wait_ge(S("hid_t"), j + 1)
                    for m in range(2):
                        o = e.matmul(ps[:, 1 + 2 * j, 32 * m:32 * m + 30], hid_t[:, j, 128 * m:128 * m + 128],
                                     ident[0:30, 0:30], start=True, stop=True)
                    o.then_inc(S("hid_mm"), 1)
                e.wait_ge(S("hid"), 2)
                e.wait_ge(S("w2_in"), 16)
                for m in range(2):
                    e.matmul(ps[:, 0, 0:30], w2_cmp[:, 0, m, :], hid[:, 0, m, :], start=m == 0, stop=m == 1)
                for g in range(2):
                    for m in range(2):
                        o = e.matmul(ps[0:15, 1, 64 * g:64 * g + 64], hid[:, 1, m, 15 * g:15 * g + 15],
                                     w2_cmp[:, 1, m, 0:64], start=m == 0, stop=m == 1)
                o.then_inc(S("cmp_mm"), 1)
                norms(cmp_norms)
                e.wait_ge(S("n_out"), cmp_norms[0].i + 1)
                e.wait_ge(S("bias_in"), 32)
                attention(nsa)

            def pe_odd():
                stage_in("od_in", META, X["od"])
                s = st["od_in"]
                e.wait_ge(acc_free, s.A + s.n + 2)
                for c in range(8):
                    src = z[:, 12 + c if c < 6 else 16 + c, META:T]
                    for t in range(2):
                        o = e.transpose(ps[:, c // 2, 256 * (c % 2) + 128 * t:256 * (c % 2) + 128 * t + 128],
                                        src[:, 128 * t:128 * t + 128], ident)
                    if c % 2:
                        o.then_inc(S("vo_mm"), 1)
                heads(odd_heads)
                e.wait_ge(S("vo"), 4)
                e.wait_ge(S("bias_in"), 48)
                e.wait_ge(S("h_out"), odd_heads[-1].i + 1)
                attention(odd)

            def pe_second():
                for k in range(KC):
                    e.wait_ge(S("sq"), k + 1)
                    column_sums(sq[:, k % 2, META:T], SEQ, k, "sq_mm")
                swiglu(0, X["g0"])
                modulation(4)
                pe_even()
                stage_out("ev_out", xhi, xlo, META, KC, {0: (S("x"), X["ev_o"] + KC)}, rms=2)
                modulation(5)
                for i, x in ((1, "g1"), (2, "g2")):
                    swiglu(i, X[x])
                pe_odd()
                stage_out("od_out", xhi, xlo, META, 4, {0: (S("x"), X["od_o"] + 4)}, rms=5)
                swiglu(3, X["g3"])

            e.wait_ge(S("onehot_in"), 32)
            for i, (head, n) in enumerate(((8, 8), (0, 4), (4, 4), (8, 4))):
                o = e.matmul(ps[0:n, 4 + i, :], t5[:, head:head + n], onehot[:, 512 * i:512 * i + 512],
                             start=True, stop=True)
            o.then_inc(S("t5_mm"), 1)

            s = st["a_in"]

            def gates(c, b):
                a = c * LRU_A
                if b == 0:
                    e.wait_ge(S("ri_in"), c * 16 + 16)
                e.wait_ge(acc_free, s.A + 4 * c + b + 3)
                if c or b > 1:
                    e.wait_ge(S("lru_a"), a + b - 1 if b > 1 else a - LRU_A + b + 3)
                for r in range(2):
                    o = e.matmul(ps[0:LRU, 4 + 2 * (b % 2) + r, 0:T], w_ri[:, b, r, :], lx[:, c % 2, b, :],
                                 start=True, stop=True)
                o.then_inc(S("ri_mm"), 1)

            def a_out():
                s = st["a_out"]

                def products(u, k0, k1):
                    slot, acc = (s.U + u) % RING, (s.A + u) % 2
                    for k in range(k0, k1):
                        o = mm3(ps[:, 2 * acc, 0:T], s, slot, k * 128, 128, hhi[0:LRU, k, :], hlo[0:LRU, k, :],
                                k == 0, k == NLRU - 1)
                    if k1 == NLRU:
                        o.then_inc(w_used, 1)
                for u in range(2):
                    e.wait_ge(w_lo, s.U + u + 3)
                    e.wait_ge(acc_free, s.A + u + 1)
                    if u == 0:
                        e.wait_ge(S("lru_d"), 3 * LRU_D)
                    products(u, 0, NLRU - 4)
                e.wait_ge(S("lru_d"), 4 * LRU_D)
                for u in range(2):
                    products(u, NLRU - 4, NLRU)
                for u in range(2, s.n):
                    e.wait_ge(w_lo, s.U + u + 3)
                    e.wait_ge(acc_free, s.A + u + 1)
                    products(u, 0, NLRU)
                    column_sums(res[:, u - 2, :], T, u - 2, "mean_mm")
                for u in range(s.n - 2, s.n):
                    e.wait_ge(acc_free, s.A + u + 3)
                    column_sums(res[:, u, :], T, u, "mean_mm")

            for g in range(GROUPS + 1):
                for b in range(4):
                    if g < GROUPS:
                        in_unit(s, It(4 * g + b), 0, LRU, 2, 0 if g == b == 0 else None)
                    if g == 1 and b == 0:
                        e.wait_ge(S("t5_out"), 1)
                    if g and b < 2:
                        gates(g - 1, 2 * b)
                        gates(g - 1, 2 * b + 1)
            a_out()
            variance(0, 0)
            modulation(0)
            for l, t0 in ((0, 0), (1, Q0)):
                if l:
                    stage_in("fgate", 0, X["fox"], 1)
                    stage_in("kv", 0, None)
                    stage_in("qg", Q0, None)
                    pe_fox()
                    stage_out("b_out", xhi, xlo, Q0, KC, {0: (S("x"), X["fox_o"] + KC)}, ln=2)
                    variance(2, Q0)
                    modulation(2)
                stage_in(f"f_in{l}", t0, X[f"f{l}"])
                f = NF * l
                stage_out(f"f_out{l}", hhi, hlo, t0, NF, {0: (S("h_lo"), f + KH), 1: (S("h_lo"), f + NF)},
                          ln=2 * l + 1)
                variance(2 * l + 1, t0)
                modulation(2 * l + 1)
            pe_second()

        @block.scalar
        def _(e):
            def split(s, it):
                if s is None:
                    return
                slot = (s.U + it.k) % RING
                e.wait_ge(w_loaded[slot], it.of(s.U, RING) * 32 + 32)
                e.wait_ge(w_used, it.of(s.U) + 1)
                e.activation(whi[0:s.rows, slot % 2, 0:s.cols], raw[0:s.rows, slot, 0:s.cols], ACT.Copy)\
                    .then_inc(w_hi, 1)

            act = lambda *a, **k: e.activation(*a, **k)

            def log1p_exp(ez, nax, lw, w, base):
                e.wait_ge(S("lp_d"), base[0] + 1)
                act(ez, nax, ACT.Exp).then_inc(S("lp_a"), 1)
                e.wait_ge(S("lp_d"), base[0] + 2)
                act(lw, w, ACT.Ln).then_inc(S("lp_a"), 1)

            e.dma_start(onehot[:, :], ap["onehot"]).then_inc(S("onehot_in"), 16)
            e.dma_start(t5[:, :], ap["t5"]).then_inc(S("onehot_in"), 16)
            e.wait_ge(S("h0_in"), 16)
            for k in range(KC):
                act(xhi[:, k, :], res[:, k, :], ACT.Copy).then_inc(S("x_hi"), 1)
            s = st["a_in"]
            split(s, It(0))
            split(s, It(1))
            e.wait_ge(S("par_in"), 16)
            act(c_act[:, :], par[:, PAR["c"][0]:PAR["c"][0] + KC], ACT.Silu).then_inc(S("c_act"), 1)
            log1p_exp(lam_t[:, 1], lam_t[:, 0], lam_t[:, 3], lam_t[:, 2], (0, 0))

            step = S("lru_a")

            def high(c):
                e.wait_ge(S("lru_d"), c * LRU_D + 10)
                if c == 0:
                    e.wait_ge(S("toeplitz_out"), 80)
                    e.wait_ge(S("expand"), 1)
                act(hhi[0:LRU, 4 * c:4 * c + 4, :], lt[:, :, :], ACT.Copy).then_inc(S("lru_hi"), 1)

            for g in range(GROUPS + 1):
                c = g - 1
                d, v = c * LRU_D, g % 2
                for b in range(4):
                    if g < GROUPS:
                        u = It(4 * g + b)
                        acc = (s.A + b) % 2
                        e.wait_ge(w_used, u.of(s.U) + 3)
                        if g > 1:
                            e.wait_ge(S("lru_d"), d - 1)
                        act(lg[:, v, b, :], ps[0:LRU, 2 * acc, 0:T], ACT.Copy)
                        act(lx[:, v, b, :], ps[0:LRU, 2 * acc + 1, 0:T], ACT.Identity,
                            bias=pcol("conv_a_b", g * 4 + b, LRU), scale=pcol("conv_a_w", g * 16 + (4 * b + 3), LRU))\
                            .then_inc(S("lru_x"), 1)
                        split(*ahead(s, u))
                    if g == 0:
                        continue
                    if c and b == 0:
                        e.wait_ge(S("lru_d"), d - 2)
                    if b < 2:
                        for h in (2 * b, 2 * b + 1):
                            e.wait_ge(S("ri_mm"), c * 4 + h + 2)
                            act(lr[:, h, :], ps[0:LRU, 4 + 2 * (h % 2), 0:T], ACT.Sigmoid,
                                bias=pcol("b_r", c * 4 + h, LRU))
                            act(li[:, h, :], ps[0:LRU, 5 + 2 * (h % 2), 0:T], ACT.Sigmoid,
                                bias=pcol("b_i", c * 4 + h, LRU)).then_inc(step, 1)
                    if c and b == 0:
                        high(c - 1)
                    if b == 2:
                        e.wait_ge(S("lru_d"), d + 1)
                        act(la[:, :, :], lr[:, :, :], ACT.Exp).then_inc(step, 1)
                        act(lt[:, :, :], lr[:, :, :], ACT.Tanh, scale=-1.0).then_inc(step, 1)
                    if b == 3:
                        e.wait_ge(S("lru_d"), d + 4)
                        act(l2[:, :, :], l2[:, :, :], ACT.Sqrt).then_inc(step, 1)
                        act(lg[:, c % 2], lg[:, c % 2], ACT.Gelu_apprx_tanh).then_inc(step, 1)
            high(GROUPS - 1)

            def stage_out(name, t0, rms=None):
                s = st[name]
                n_m = KC * s.per // s.n

                def squares(it):
                    g = it.of(0, s.per)
                    e.wait_ge(acc_free, g + (s.A + 3))
                    for h in range(n_m):
                        m = g * n_m + h
                        par_ = (n_m * (it.k // s.per) + h) % 2
                        wait(e, S("sq_mm"), m + (KC * rms - 1))
                        act(sq[:, par_, t0:T], chunk(res, m, t0), ACT.Square).then_inc(S("sq"), 1)

                def unit(it, first, last):
                    if rms is not None and it.k % s.per == s.per - 1:
                        squares(it)
                    split(*ahead(s, it))
                sweep(e, s.n, unit, RING, RING)

            def layer_norm(i, gb, l, t0, x=True):
                n = T - t0
                for k in range(KC):
                    e.wait_ge(S("dev"), KC * i + k + 1)
                    act(dsq[:, k, t0:T], dev[:, k, t0:T], ACT.Square).then_inc(S("dsq"), 1)
                e.wait_ge(S("var_mm"), KC * (i + 1))
                act(std[:, 0:n], ps[:, 6, 0:n], ACT.Sqrt, bias=eps[:, 0:1]).then_inc(S("std"), 1)
                for k in range(KC):
                    e.wait_ge(S("scaled"), NX["ln"](i) + k + 1)
                    b = pcol(gb + "_b", KC * l + k)
                    act(res[:, k, t0:T], dev[:, k, t0:T], ACT.Identity, bias=b).then_inc(S("res_n"), 1)
                    if x:
                        act(xhi[:, k, t0:T], dev[:, k, t0:T], ACT.Identity, bias=b).then_inc(S("x_hi"), 1)

            def ffn_conv(l, t0):
                s, n, F = st[f"f_in{l}"], T - t0, NF * l
                W = 3 * 2 * NF * l

                def h_hi(it):
                    e.wait_ge(S("h_mul"), it.of(F) + 1)
                    act(chunk(hhi, it.of(), t0), hf[:, it.k % 2, t0:T], ACT.Copy).then_inc(S("h_hi"), 1)

                def unit(it, first, last):
                    b, acc = it.k % 2, (s.A + it.k) % 2
                    e.wait_ge(w_used, it.of(s.U) + 3)
                    wait(e, S("h_mul"), it.of(F) - 1)
                    for half, buf in ((0, cg), (1, cv)):
                        act(buf[:, b, t0:T], ps[:, 2 * acc + half, 0:n], ACT.Identity,
                            bias=pcol("conv_f_b", it.of() + (2 * NF * l + NF * half)),
                            scale=pcol("conv_f_w", it.of() * 3 + (W + 3 * NF * half + 2)))\
                            .then_inc(S("tap2"), 1)
                    if not first:
                        h_hi(it.next(-1))
                    split(*ahead(s, it))
                    e.wait_ge(S("tap0"), it.of(F) + 1)
                    act(gg[:, b, t0:T], cg[:, b, t0:T], ACT.Gelu_apprx_tanh).then_inc(S("gelu"), 1)
                sweep(e, s.n, unit, 2, 2)
                h_hi(It(s.n - 1))

            def attention(run):
                n, lag = len(run.steps), run.lag

                def exps(i):
                    joint = len(run.steps[i].group) > 1
                    for j in run.steps[i].group:
                        s, g = run.steps[j], run.B + j
                        if joint:
                            e.wait_ge(S("joint_max"), i // 3 + 1)
                        e.wait_ge(S("scored"), run.B + i + 1)
                        for tile in range(2):
                            a, b = s.cols[tile]
                            p = probs[:, g % 6, a:b]
                            m = small[:, (run.B + i) % 8, tile, 3:4] if joint else small[:, g % 8, tile, 0:1]
                            o = act(p, p, ACT.Exp, bias=m, scale=-1.0, accum_out=small[:, g % 8, tile, 1:2])
                        o.then_inc(S("exp"), 1)

                def turned(i):
                    s, g = run.steps[i], run.B + i
                    e.wait_ge(S("turn_mm"), g + 1)
                    wait(e, S("pv_mm"), g - 1)
                    if s.small:
                        act(pt_small[0:16, g % 2, 0:2], early_t[:, s.head, :], ACT.Copy)
                        act(pt_small[0:16, g % 2, 2:258], ps[0:16, 2 + g % 2, 0:256], ACT.Copy)
                    blocks = s.turn if s.mask is not None else [(0, 0, 128, 256)]
                    for tile, a, b, to in blocks:
                        w = slice(to if s.mask is not None else 0, to + 128)
                        o = act(pt[0:b - a, g % 2, w], ps[0:b - a, 6 + g % 2, w], ACT.Copy)
                    o.then_inc(S("turned"), 1)

                def out_hi(p):
                    g = run.P + p
                    e.wait_ge(S("o_out"), g + 1)
                    act(xhi[:, run.first_pair + p, run.t0:T], sq[:, g % 2, run.t0:T], ACT.Copy).then_inc(S("x_hi"), 1)

                for t in range(n + lag + 3):
                    if t < n and run.steps[t].ends:
                        exps(t)
                    if 0 <= t - lag < n:
                        turned(t - lag)
                    if t - lag - 2 in run.pair_end:
                        out_hi(run.pair_end[t - lag - 2])

            def evacuate(name, t0, base, step=1, half=0, func=ACT.Copy, between={}):
                s = st[name]

                def unit(it, first, last):
                    e.wait_ge(w_used, it.of(s.U) + 3)
                    act(chunk(z, it.of() * step + base, t0), ps[:, 2 * ((s.A + it.k) % 2) + half, 0:T - t0], func)\
                        .then_inc(S("half_out"), 1)
                    split(*ahead(s, it))
                    if it.j is None and it.k in between:
                        between[it.k]()
                sweep(e, s.n, unit, 2, 2)

            def act_fox():
                s = st["fgate"]
                e.wait_ge(w_used, s.U + 3)
                act(ft[:, 0], ps[0:16, 2 * (s.A % 2), 0:T], ACT.Identity, bias=pcol("f_b", 0, 16)).then_inc(S("fg_x"), 1)
                split(*ahead(s, It(0)))
                log1p_exp(ft[:, 2], ft[:, 1], ft[:, 4], ft[:, 3], (13, 2))
                evacuate("kv", 0, 0)
                evacuate("qg", Q0, 24, half=1, func=ACT.Sigmoid)
                for j in range(KC):
                    e.wait_ge(S("vt_mm"), j + 1)
                    act(vt[0:16, j, 0, :], ps[0:16, 6 + j % 2, 256:384], ACT.Copy)
                    act(vt[:, j, 1:3, :], ps[:, 6 + j % 2, 0:256].rearrange("p (a b) -> p a b", a=2), ACT.Copy)\
                        .then_inc(S("vt"), 1)
                e.wait_ge(S("early"), 2)
                act(early[:, :, :], early[:, :, :], ACT.Exp).then_inc(S("early_exp"), 1)
                e.wait_ge(S("early_mm"), 2 * HEADS)
                act(early_t[:, :, :], ps[0:16, 3, 0:2 * HEADS].rearrange("p (h q) -> p h q", q=2), ACT.Copy)\
                    .then_inc(S("early_t"), 1)
                attention(fox)
            def norm_squares(items):
                for it in items:
                    wait(e, S("n_mm"), it.i - 1)
                    o = n_sq[0:it.rows, it.i % 2, 0:it.sums[-1][2]]
                    if len(it.src.shape) == 3:
                        o = o.rearrange("p (a b) -> p a b", a=2)
                    act(o, it.src, ACT.Square).then_inc(S("n_sq"), 1)

            def norm_roots(items):
                for it in items:
                    e.wait_ge(S("n_mm"), it.i + 1)
                    wait(e, S("n_out"), it.i - 1)
                    act(n_std[0:it.rows, it.i % 2, 0:it.n], ps[0:it.rows, 4 + it.i % 2, 0:it.n], ACT.Sqrt,
                        bias=eps[0:it.rows, 1:2], scale=it.scale).then_inc(S("n_std"), 1)

            def heads(lot):
                for it in lot:
                    if it.rows == 64 and it is lot[5]:
                        e.wait_ge(S("kv_out"), 4)
                    wait(e, S("h_mm"), it.i - 1)
                    o = n_sq[0:it.rows, it.i % 2, 0:it.n]
                    if len(it.src.shape) == 3:
                        o = o.rearrange("p (a b) -> p a b", a=2)
                    act(o, it.src, ACT.Square).then_inc(S("h_sq"), 1)
                e.wait_ge(S("h_mm"), lot[-1].i + 1)
                act(h_std[:, :], ps[0:32, 4, 0:SEQ], ACT.Sqrt, bias=eps[0:32, 1:2]).then_inc(S("h_std"), 1)

            def rms_norm(r, l, s):
                e.wait_ge(S("sq_mm"), KC * (r + 1))
                act(std[:, 0:SEQ], ps[:, 7, 0:SEQ], ACT.Sqrt, bias=eps[:, 1:2]).then_inc(S("std"), 1)
                for k in range(KC):
                    e.wait_ge(S("scaled"), KC * (4 + r) + k + 1)
                    act(xhi[:, k, META:T], dev[:, k, META:T], ACT.Identity, bias=mod[:, l, 24 * s + k:24 * s + k + 1])\
                        .then_inc(S("x_hi"), 1)

            def swiglu(i):
                s, F = st[f"g_in{i}"], NF * (2 + i)

                def h_hi(it):
                    e.wait_ge(acc_free, it.of(s.A) + 3)
                    act(chunk(hhi, it.of(), META), hf[:, it.k % 2, META:T], ACT.Copy).then_inc(S("h_hi"), 1)

                def unit(it, first, last):
                    b, acc = it.k % 2, (s.A + it.k) % 2
                    e.wait_ge(w_used, it.of(s.U) + 3)
                    act(gg[:, b, META:T], ps[:, 2 * acc, 0:SEQ], ACT.Silu).then_inc(S("gelu"), 1)
                    if not first:
                        h_hi(it.next(-1))
                    split(*ahead(s, it))
                sweep(e, s.n, unit, 2, 2)
                h_hi(It(s.n - 1))
                stage_out(f"g_out{i}", META, rms=[1, 3, 4, None][i])

            def act_even():
                rms_norm(1, 0, 1)
                s = st["ev_in"]

                def latent_squares():
                    e.wait_ge(acc_free, s.A + 4)
                    norm_squares(latent_norms)

                def latent_high():
                    e.wait_ge(S("n_out"), 2)
                    for k in range(3):
                        act(lat_hi[:, k, :], z[:, k, META:T], ACT.Copy).then_inc(S("latent_hi"), 1)
                evacuate("ev_in", META, 0, step=2,
                         between={2: latent_squares, 4: lambda: norm_roots(latent_norms), 5: latent_high})
                e.wait_ge(w_used, st["uq"].U + 3)
                for i in range(4):
                    act(q96[:, 2 * i:2 * i + 2, :], ps[0:96, i, :].rearrange("p (a b) -> p a b", a=2), ACT.Copy)\
                        .then_inc(S("q_out"), 1)
                split(st["cmp_w1"], It(0))
                split(st["cmp_w1"], It(1))
                e.wait_ge(S("q_out"), 4)
                heads(mla_heads)
                e.wait_ge(S("vm_mm"), 1)
                for i in range(2):
                    o = act(vm[:, 4 * i:4 * i + 4, :, :].rearrange("p h t c -> p (h t c)"), ps[:, i, :], ACT.Copy)
                o.then_inc(S("vm"), 1)
                e.wait_ge(S("rotated"), 5)
                act(kf[64:96, :, :], z[64:96, 3, META:T].unsqueeze(1).broadcast_to([32, 8, SEQ]), ACT.Copy)\
                    .then_inc(S("k_rope"), 1)
                attention(mla)
                heads(nsa_heads)
                e.wait_ge(S("vn_mm"), 1)
                act(v_nsa[:, :, :].rearrange("p a b -> p (a b)"), ps[:, 2, :], ACT.Copy)
                act(gates[:, :, :], ps[:, 3, 0:256].rearrange("p (t c) -> p t c", t=2)[:, :, 96:120], ACT.Sigmoid)\
                    .then_inc(S("vn"), 1)
                e.wait_ge(S("x2_f"), 8)
                act(x2_hi[:, :, :, :].rearrange("p j i c -> p (j i c)"),
                    x2[:, :, :, :, :].rearrange("p j i g n -> p (j i g n)"), ACT.Copy).then_inc(S("x2_hi"), 1)
                c = st["cmp_w1"]
                split(*ahead(c, It(0)))
                split(*ahead(c, It(1)))
                for u in (1, 3):
                    e.wait_ge(w_used, c.U + u + 3)
                    act(hid_t[:, u // 2, :], ps[0:30, u - 1, 0:256], ACT.Silu).then_inc(S("hid_t"), 1)
                for j in range(2):
                    e.wait_ge(S("hid_mm"), j + 1)
                    act(hid[:, j, :, :], ps[:, 1 + 2 * j, 0:64].rearrange("p (m n) -> p m n", m=2)[:, :, 0:30],
                        ACT.Copy).then_inc(S("hid"), 1)
                split(*ahead(c, It(2)))
                split(*ahead(c, It(3)))
                e.wait_ge(S("cmp_mm"), 1)
                act(k_cmp[:, :], ps[:, 0, 0:30], ACT.Copy)
                act(v_cmp[:, :, :].rearrange("p a b -> p (a b)"), ps[0:15, 1, 0:128], ACT.Copy)\
                    .then_inc(S("cmp_out"), 1)
                e.wait_ge(S("cmp_out"), 1)
                norm_squares(cmp_norms)
                norm_roots(cmp_norms)
                attention(nsa)

            def act_odd():
                rms_norm(4, 1, 1)
                evacuate("od_in", META, 0, step=2)
                s = st["od_in"]
                e.wait_ge(acc_free, s.A + s.n + 2)
                for i in range(4):
                    e.wait_ge(S("vo_mm"), i + 1)
                    act(v_odd[:, 2 * i:2 * i + 2, :, :].rearrange("p a t c -> p (a t c)"), ps[:, i, :], ACT.Copy)\
                        .then_inc(S("vo"), 1)
                heads(odd_heads)
                attention(odd)

            def act_second():
                for k in range(KC):
                    e.wait_ge(S("res_n"), 3 * KC + k + 1)
                    wait(e, S("sq_mm"), k - 1)
                    act(sq[:, k % 2, META:T], res[:, k, META:T], ACT.Square).then_inc(S("sq"), 1)
                rms_norm(0, 0, 0)
                swiglu(0)
                act_even()
                stage_out("ev_out", META, rms=2)
                rms_norm(2, 0, 2)
                swiglu(1)
                rms_norm(3, 1, 0)
                swiglu(2)
                act_odd()
                stage_out("od_out", META, rms=5)
                rms_norm(5, 1, 2)
                swiglu(3)

            stage_out("a_out", 0)
            layer_norm(0, "ln1", 0, 0)
            for l, t0 in ((0, 0), (1, Q0)):
                if l:
                    act_fox()
                    stage_out("b_out", Q0)
                    layer_norm(2, "ln1", 1, Q0)
                ffn_conv(l, t0)
                stage_out(f"f_out{l}", t0)
                layer_norm(2 * l + 1, "ln2", l, t0, x=l == 0)
            act_second()

        @block.vector
        def _(e):
            e.nop().then_inc(w_lo, 2)
            e.nop().then_inc(acc_free, 2)
            tt, stt, ts = e.tensor_tensor, e.scalar_tensor_tensor, e.tensor_scalar

            def split(s, it):
                if s is None:
                    return
                slot = (s.U + it.k) % RING
                e.wait_ge(w_hi, it.of(s.U) + 1)
                tt(wlo[0:s.rows, slot, 0:s.cols], raw[0:s.rows, slot, 0:s.cols],
                   whi[0:s.rows, slot % 2, 0:s.cols].bitcast(f32), ALU.subtract).then_inc(w_lo, 1)

            def log1p_exp(t, base):
                n, step = [base[0]], S("lp_d")

                def go(ins, sem=None):
                    ins.then_inc(step, 1)
                    n[0] += 1
                    e.wait_ge(step, n[0])
                x, nax, ez, w, lw, out, d, eq, r = t
                go(stt(nax, x, -1.0, x, ALU.mult, ALU.min))
                e.wait_ge(S("lp_a"), base[1] + 1)
                go(ts(w, ez, 1.0, None, ALU.add))
                go(ts(d, w, -1.0, None, ALU.add))
                go(ts(eq, d, 0.0, None, ALU.is_equal))
                go(tt(d, d, eq, ALU.add))
                go(e.reciprocal(r, d))
                go(tt(r, r, ez, ALU.mult))
                go(tt(eq, eq, ez, ALU.mult))
                e.wait_ge(S("lp_a"), base[1] + 2)
                go(tt(out, lw, r, ALU.mult))
                go(tt(out, out, eq, ALU.add))
                return n[0]

            for k in range(KC):
                e.wait_ge(S("x_hi"), k + 1)
                tt(xlo[:, k, :], res[:, k, :], xhi[:, k, :].bitcast(f32), ALU.subtract).then_inc(S("x"), 1)

            s = st["a_in"]
            split(s, It(0))
            split(s, It(1))
            e.wait_ge(S("t5_mm"), 1)
            for i, n in enumerate((8, 4, 4, 4)):
                o = e.tensor_copy(t_rows[0:n, i, :], ps[0:n, 4 + i, :])
            o.then_inc(S("t5_out"), 1)
            e.wait_ge(S("par_in"), 16)
            o = PAR["lam"][0]
            lam = par[0:LRU, o:o + NLRU]
            L = lam_t
            done = log1p_exp((lam, L[:, 0], L[:, 1], L[:, 2], L[:, 3], L[:, 4], L[:, 5], L[:, 6], L[:, 7]), (0, 0))
            ts(L[:, 0], lam, -1.0, 0.0, ALU.mult, ALU.max).then_inc(S("lp_d"), 1)
            e.wait_ge(S("lp_d"), done + 1)
            tt(L[:, 0], L[:, 0], L[:, 4], ALU.add).then_inc(S("lp_d"), 1)
            e.wait_ge(S("lp_d"), done + 2)
            ts(sp8[:, :], L[:, 0], -8.0, None, ALU.mult).then_inc(S("lp_d"), 1)
            e.wait_ge(S("lp_d"), done + 3)

            def go(ins, hold=True):
                n.append(ins.then_inc(S("lru_d"), 1))
                if hold:
                    e.wait_ge(S("lru_d"), len(n))

            def low_parts(c):
                e.wait_ge(S("lru_hi"), c + 1)
                go(tt(hlo[0:LRU, 4 * c:4 * c + 4, :], lt[:, :, :], hhi[0:LRU, 4 * c:4 * c + 4, :].bitcast(f32),
                      ALU.subtract), False)
                assert len(n) == (c + 1) * LRU_D

            n = []
            for g in range(GROUPS + 1):
                c = g - 1
                a, v = c * LRU_A, g % 2
                for b in range(4):
                    if g < GROUPS:
                        u = It(4 * g + b)
                        acc, x = (s.A + b) % 2, lx[:, v, b]
                        e.wait_ge(S("lru_x"), 4 * g + b + 1)
                        for tap in (2, 1, 0):
                            d = 3 - tap
                            o = stt(x[:, d:T], ps[0:LRU, 2 * acc + 1, 0:T - d],
                                    pcol("conv_a_w", g * 16 + (4 * b + tap), LRU), x[:, d:T], ALU.mult, ALU.add)
                            if tap:
                                o.then_inc(S("lru_tap"), 1)
                                e.wait_ge(S("lru_tap"), 8 * g + 2 * b + (3 - tap))
                            else:
                                o.then_inc(acc_free, 1)
                        split(*ahead(s, u))
                    if g == 0:
                        continue
                    if c and b == 0:
                        low_parts(c - 1)
                    if b == 1:
                        e.wait_ge(S("lru_a"), a + 4)
                        r = sp8[:, 4 * c:4 * c + 4].unsqueeze(2).broadcast_to([LRU, 4, T])
                        go(tt(lr[:, :, :], lr[:, :, :], r, ALU.mult), False)
                        go(tt(li[:, :, :], li[:, :, :], lx[:, c % 2], ALU.mult), False)
                    if b == 2:
                        e.wait_ge(S("lru_a"), a + 5)
                        go(tt(l2[:, :, :], la[:, :, :], la[:, :, :], ALU.mult))
                        e.wait_ge(S("lru_a"), a + 6)
                        go(stt(l2[:, :, :], l2[:, :, :], 1.0, lt[:, :, :], ALU.add, ALU.mult))
                    if b == 3:
                        e.wait_ge(S("lru_a"), a + 7)
                        go(tt(li[:, :, :], li[:, :, :], l2[:, :, :], ALU.mult))
                        for h in range(4):
                            go(e.tensor_tensor_scan(lt[:, h, :], la[:, h, :], li[:, h, :], 0.0, ALU.mult, ALU.add),
                               h == 3)
                        e.wait_ge(S("lru_a"), a + 8)
                        go(tt(lt[:, :, :], lt[:, :, :], lg[:, c % 2], ALU.mult))
            low_parts(GROUPS - 1)

            def stage_out(name, t0, gate=None):
                s = st[name]
                n, n_m = T - t0, KC * s.per // s.n

                def residual(it):
                    g, acc = it.of(0, s.per), (s.A + it.k // s.per) % 2
                    e.wait_ge(w_used, it.of(s.U) + 3)
                    if gate is None:
                        r = chunk(res, g * n_m, t0, n=n_m)
                        p = ps[:, 2 * acc, 0:n] if n_m == 1 else ps[:, 2 * acc:2 * acc + 2, 0:n]
                        stt(r, r, ALPHA, p, ALU.mult, ALU.add).then_inc(acc_free, 1)
                        return
                    for h in range(n_m):
                        m = g * n_m + h
                        r = chunk(res, m, t0)
                        l, o = gate
                        col = mod[:, l, o + m:o + m + 1] if isinstance(m, int) else mod[:, l, bass.ds(m + o, 1)]
                        o = stt(r, ps[:, 2 * acc + h, 0:n], col, r, ALU.mult, ALU.add)
                    o.then_inc(acc_free, 1)

                def unit(it, first, last):
                    if it.k % s.per == s.per - 1:
                        residual(it)
                    split(*ahead(s, it))
                sweep(e, s.n, unit, RING, RING)

            def layer_norm(i, gb, l, t0, x=None):
                n = T - t0

                def low(k):
                    e.wait_ge(S("x_hi"), x + k + 1)
                    tt(xlo[:, k, t0:T], res[:, k, t0:T], xhi[:, k, t0:T].bitcast(f32), ALU.subtract)\
                        .then_inc(S("x"), 1)
                e.wait_ge(S("mean_mm"), KC * (i + 1))
                for k in range(KC):
                    tt(dev[:, k, t0:T], res[:, k, t0:T], ps[:, 7, 0:n], ALU.subtract).then_inc(S("dev"), 1)
                e.wait_ge(S("std"), NX["std"](i) + 1)
                e.reciprocal(std[:, 0:n], std[:, 0:n]).then_inc(S("rstd"), 1)
                e.wait_ge(S("rstd"), NX["std"](i) + 1)
                for k in range(KC):
                    stt(dev[:, k, t0:T], dev[:, k, t0:T], pcol(gb + "_g", KC * l + k), std[:, 0:n], ALU.mult, ALU.mult)\
                        .then_inc(S("scaled"), 1)
                    if x is not None and k >= 2:
                        low(k - 2)
                if x is not None:
                    low(KC - 2)
                    low(KC - 1)

            def ffn_conv(l, t0):
                s, n, F = st[f"f_in{l}"], T - t0, NF * l
                W = 3 * 2 * NF * l

                def mul(it):
                    b = it.k % 2
                    e.wait_ge(S("gelu"), it.of(F) + 1)
                    e.wait_ge(acc_free, it.of(s.A) + 3)
                    wait(e, S("h_hi"), it.of(F) - 1)
                    tt(hf[:, b, t0:T], gg[:, b, t0:T], cv[:, b, t0:T], ALU.mult).then_inc(S("h_mul"), 1)

                def low(it):
                    e.wait_ge(S("h_hi"), it.of(F) + 1)
                    tt(chunk(hlo, it.of(), t0), hf[:, it.k % 2, t0:T], chunk(hhi, it.of(), t0).bitcast(f32),
                       ALU.subtract).then_inc(S("h_lo"), 1)

                def unit(it, first, last):
                    b, acc = it.k % 2, (s.A + it.k) % 2
                    e.wait_ge(S("tap2"), it.of(F) * 2 + 2)
                    for tap in (1, 0):
                        d = 2 - tap
                        for half, buf in ((0, cg), (1, cv)):
                            if tap == 0:
                                e.wait_ge(S("tap1"), it.of(F) * 2 + (1 + half))
                            o = stt(buf[:, b, t0 + d:T], ps[:, 2 * acc + half, 0:n - d],
                                    pcol("conv_f_w", it.of() * 3 + (W + 3 * NF * half + tap)),
                                    buf[:, b, t0 + d:T], ALU.mult, ALU.add)
                            o.then_inc(S("tap1") if tap else acc_free if half else S("tap0"), 1)
                    if not first:
                        low(it.next(-1))
                    split(*ahead(s, it))
                    mul(it)
                sweep(e, s.n, unit, 2, 2)
                low(It(s.n - 1))

            soft = [0]
            half_base = {'kv': 0, 'qg': KC, 'ev_in': 2 * KC, 'od_in': 3 * KC}
            def attention(run):
                n, lag = len(run.steps), run.lag
                step = S("soft_step")

                def go(ins):
                    ins.then_inc(step, 1)
                    soft[0] += 1
                    e.wait_ge(step, soft[0])

                def scored(i):
                    s, g = run.steps[i], run.B + i
                    e.wait_ge(S("qk_mm"), g + 1)
                    wait(e, S("turn_mm"), g - 5)
                    for tile in range(2):
                        a, b = s.cols[tile]
                        o = e.tensor_tensor_reduce(out=probs[:, g % 6, a:b], in0=ps[:, 4 + g % 2, a:b],
                                                   in1=s.bias[tile], scale=-1.0, scalar=3e38, op0=ALU.add,
                                                   op1=ALU.min, accum_out=small[:, g % 8, tile, 0:1])
                    o.then_inc(S("scored"), 1)
                    if s.ends and len(s.group) > 1:
                        e.wait_ge(S("scored"), g + 1)
                        m = [small[:, (run.B + j) % 8, :, 0] for j in s.group]
                        out = small[:, g % 8, :, 3]
                        go(tt(out, m[0], m[1], ALU.min))
                        tt(out, out, m[2], ALU.min).then_inc(S("joint_max"), 1)

                def normal(i):
                    s, g = run.steps[i], run.B + i
                    e.wait_ge(S("exp"), g + 1)
                    r = g % 8
                    den = small[:, r, :, 1]
                    if s.mask is not None:
                        for tile in range(2):
                            a, b = s.cols[tile]
                            p = probs[:, g % 6, a:b]
                            go(e.tensor_tensor_reduce(out=p, in0=p, in1=s.mask[tile], scale=1.0, scalar=0.0,
                                                      op0=ALU.mult, op1=ALU.add, accum_out=small[:, r, tile, 1:2]))
                        go(ts(den, den, 1e-30, None, ALU.max))
                    if len(s.group) > 1:
                        d = [small[:, (run.B + j) % 8, :, 1] for j in s.group]
                        go(tt(small[:, r, :, 4], d[0], d[1], ALU.add))
                        go(tt(small[:, r, :, 4], small[:, r, :, 4], d[2], ALU.add))
                        den = small[:, r, :, 4]
                    go(e.reciprocal(small[:, r, :, 5], den))
                    if s.gate is not None:
                        go(tt(small[:, r, :, 5], small[:, r, :, 5], s.gate, ALU.mult))
                    for j in s.group:
                        for tile in range(2):
                            a, b = run.steps[j].cols[tile]
                            p = probs[:, (run.B + j) % 6, a:b]
                            o = ts(p, p, small[:, r, tile, 5:6], None, ALU.mult)
                        o.then_inc(S("prob"), 1)

                def out(p, i):
                    g = run.P + p
                    e.wait_ge(S("pv_mm"), run.B + i + 1)
                    if p >= 2:
                        e.wait_ge(S("x"), run.x + p - 1)
                    o, nq = sq[:, g % 2, run.t0:T], T - run.t0
                    if run.out_gate is not None:
                        o = tt(o, ps[:, g % 2, 0:nq], z[:, run.out_gate + p, run.t0:T], ALU.mult)
                    else:
                        o = e.tensor_copy(o, ps[:, g % 2, 0:nq])
                    o.then_inc(S("o_out"), 1)

                def out_lo(p):
                    c = run.first_pair + p
                    e.wait_ge(S("x_hi"), run.x + p + 1)
                    tt(xlo[:, c, run.t0:T], sq[:, (run.P + p) % 2, run.t0:T], xhi[:, c, run.t0:T].bitcast(f32),
                       ALU.subtract).then_inc(S("x"), 1)

                for t in range(n + lag + 4):
                    if t < n:
                        scored(t)
                    if 0 <= t - 1 < n and run.steps[t - 1].ends:
                        normal(t - 1)
                    if t - lag - 2 in run.pair_end:
                        out(run.pair_end[t - lag - 2], t - lag - 2)
                    if t - lag - 3 in run.pair_end:
                        out_lo(run.pair_end[t - lag - 3])

            def evacuate(name, t0, base, step=1, half=1, scale=None, between={}):
                s = st[name]

                def unit(it, first, last):
                    e.wait_ge(S("half_out"), it.of(half_base[name]) + 1)
                    p, o = ps[:, 2 * ((s.A + it.k) % 2) + half, 0:T - t0], chunk(z, it.of() * step + base, t0)
                    (e.tensor_copy(o, p) if scale is None else ts(o, p, scale, None, ALU.mult)).then_inc(acc_free, 1)
                    split(*ahead(s, it))
                    if it.j is None and it.k in between:
                        between[it.k]()
                sweep(e, s.n, unit, 2, 2)

            def dve_fox():
                step, n = S("forget_step"), [0]

                def go(ins, hold=True):
                    ins.then_inc(step, 1)
                    n[0] += 1
                    if hold:
                        e.wait_ge(step, n[0])
                split(*ahead(st["fgate"], It(0)))
                e.wait_ge(S("fg_x"), 1)
                go(e.memset(c_lhs[:, :, :].bitcast(f32), 1.0), False)
                go(e.memset(c_rhs[:, :, :].bitcast(f32), 1.0), False)
                e.memset(ft[:, 8], 1.0).then_inc(acc_free, 1)
                e.wait_ge(acc_free, st["fgate"].A + 3)
                f = [ft[:, i] for i in range(9)]
                log1p_exp((f[0], f[1], f[2], f[3], f[4], f[5], f[6], f[7], fr[:, :]), (13, 2))
                go(stt(f[0], f[0], 0.0, f[5], ALU.min, ALU.subtract))
                go(e.tensor_tensor_scan(f[1], f[8], f[0], 0.0, ALU.mult, ALU.add))
                go(e.tensor_copy(c_part[:, 0], f[1]))
                go(tt(c_part[:, 1], f[1], c_part[:, 0].bitcast(f32), ALU.subtract))
                go(ts(c_part[:, 2], c_part[:, 0].bitcast(f32), -1.0, None, ALU.mult))
                go(ts(c_part[:, 3], c_part[:, 1].bitcast(f32), -1.0, None, ALU.mult))
                assert n[0] == FORGET_STEPS
                evacuate("kv", 0, 8)
                evacuate("qg", Q0, 16, half=0, scale=64 ** -0.5)
                e.wait_ge(S("early_mm"), HEADS)
                m = con("causal0")[0:2, :].unsqueeze(1).broadcast_to([2, HEADS, 16])
                es = S("early_step")
                p0 = ps[0:2, 2, 0:256].rearrange("p (h k) -> p h k", k=16)
                tt(early[:, :, :], p0, m, ALU.add).then_inc(es, 1)
                e.wait_ge(es, 1)
                e.reduce_max(early_m[:, 0], early[:, :, :], AX.X).then_inc(es, 1)
                e.wait_ge(es, 2)
                tt(early[:, :, :], early[:, :, :], early_m[:, 0].unsqueeze(2).broadcast_to([2, HEADS, 16]),
                   ALU.subtract).then_inc(S("early"), 2)
                e.wait_ge(S("early_exp"), 1)
                e.reduce_sum(early_m[:, 1], early[:, :, :], AX.X).then_inc(es, 1)
                e.wait_ge(es, 3)
                e.reciprocal(early_m[:, 2], early_m[:, 1]).then_inc(es, 1)
                e.wait_ge(es, 4)
                tt(early[:, :, :], early[:, :, :], early_m[:, 2].unsqueeze(2).broadcast_to([2, HEADS, 16]),
                   ALU.mult).then_inc(S("early"), 2)
                attention(fox)
            def norms(items):
                for it in items:
                    r, b = it.rows, it.i % 2
                    e.wait_ge(S("n_std"), it.i + 1)
                    sd = n_std[0:r, b, 0:it.n]
                    e.reciprocal(sd, sd).then_inc(S("n_rstd"), 1)
                    e.wait_ge(S("n_rstd"), it.i + 1)
                    for src, g, dst in it.outs:
                        d = sd.rearrange("p (a b) -> p a b", a=2) if len(src.shape) == 3 else sd[:, 0:src.shape[-1]]
                        o = stt(dst, src, g, d, ALU.mult, ALU.mult)
                    o.then_inc(S("n_out"), 1)

            def heads(lot):
                n = lots.index(lot) + 1
                e.wait_ge(S("h_std"), n)
                r = S("h_rstd")
                e.reciprocal(h_std[:, :], h_std[:, :]).then_inc(r, 1)
                e.wait_ge(r, 3 * n - 2)
                e.tensor_copy(h_hi[:, :], h_std[:, :]).then_inc(r, 1)
                e.wait_ge(r, 3 * n - 1)
                tt(h_lo[:, :], h_std[:, :], h_hi[:, :].bitcast(f32), ALU.subtract).then_inc(r, 1)
                for it in lot:
                    e.wait_ge(S("h_mm2"), it.i + 1)
                    p = ps[0:it.rows, 5 + it.i % 3, 0:it.n]
                    if len(it.src.shape) == 3:
                        p = p.rearrange("p (a b) -> p a b", a=2)
                    stt(it.dst, it.src, it.g, p, ALU.mult, ALU.mult).then_inc(S("h_out"), 1)

            def modulation(part):
                e.wait_ge(S("mod_mm"), part + 1)
                l, c = part // 3, part % 3 * MOD_N
                o = PAR["ada_b"][0] + ADA_T * l + c
                tt(mod[:, l, c:c + MOD_N], ps[:, 5, 0:MOD_N], par[:, o:o + MOD_N], ALU.add).then_inc(S("mod_in"), 1)
                if part % 3 == 2:
                    e.wait_ge(S("mod_in"), part + 1)
                    v = mod[:, l, :].rearrange("p (s c k) -> p s c k", s=3, c=3)
                    o = PAR["norm_g"][0] + 3 * KC * l
                    g = par[:, o:o + 3 * KC].rearrange("p (s k) -> p s k", s=3)
                    stt(gs[:, l, :].rearrange("p (s k) -> p s k", s=3), v[:, :, 1, :], 1.0, g, ALU.add, ALU.mult)\
                        .then_inc(S("mod_step"), 1)
                    ts(v[:, 0:3:2, 2, :], v[:, 0:3:2, 2, :], 0.5, None, ALU.mult).then_inc(S("mod_step"), 1)

            def rms_norm(r, l, s, x):
                def low(k):
                    e.wait_ge(S("x_hi"), x + k + 1)
                    stt(xlo[:, k, META:T], dev[:, k, META:T], mod[:, l, 24 * s + k:24 * s + k + 1],
                        xhi[:, k, META:T].bitcast(f32), ALU.add, ALU.subtract).then_inc(S("x"), 1)
                e.wait_ge(S("std"), 4 + r + 1)
                e.reciprocal(std[:, 0:SEQ], std[:, 0:SEQ]).then_inc(S("rstd"), 1)
                e.wait_ge(S("rstd"), 4 + r + 1)
                for k in range(KC):
                    stt(dev[:, k, META:T], res[:, k, META:T], gs[:, l, KC * s + k:KC * s + k + 1], std[:, 0:SEQ],
                        ALU.mult, ALU.mult).then_inc(S("scaled"), 1)
                    if k >= 2:
                        low(k - 2)
                low(KC - 2)
                low(KC - 1)

            def swiglu(i, l, sub):
                s, F = st[f"g_in{i}"], NF * (2 + i)

                def low(it):
                    e.wait_ge(S("h_hi"), it.of(F) + 1)
                    tt(chunk(hlo, it.of(), META), hf[:, it.k % 2, META:T], chunk(hhi, it.of(), META).bitcast(f32),
                       ALU.subtract).then_inc(S("h_lo"), 1)

                def unit(it, first, last):
                    b, acc = it.k % 2, (s.A + it.k) % 2
                    e.wait_ge(S("gelu"), it.of(F) + 1)
                    e.wait_ge(S("h_lo"), it.of(F) - 1)
                    tt(hf[:, b, META:T], ps[:, 2 * acc + 1, 0:SEQ], gg[:, b, META:T], ALU.mult).then_inc(acc_free, 1)
                    if not first:
                        low(it.next(-1))
                    split(*ahead(s, it))
                sweep(e, s.n, unit, 2, 2)
                low(It(s.n - 1))
                stage_out(f"g_out{i}", META, gate=(l, 24 * sub + 16))

            def dve_even():
                rms_norm(1, 0, 1, X["ev"])
                modulation(4)
                def latent_low():
                    for k in range(3):
                        e.wait_ge(S("latent_hi"), k + 1)
                        tt(lat_lo[:, k, :], z[:, k, META:T], lat_hi[:, k, :].bitcast(f32), ALU.subtract)\
                            .then_inc(S("latent"), 1)
                evacuate("ev_in", META, 1, step=2, between={4: lambda: norms(latent_norms), 5: latent_low})
                for i, name in enumerate(("nsa_g", "dil_g", "moba_g")):
                    o = ts(g8[:, i:i + 1], gcol(name), 0.125, None, ALU.mult)
                o.then_inc(S("g8"), 1)
                e.wait_ge(S("g8"), 1)
                e.wait_ge(S("rope_in"), 16)
                e.wait_ge(w_used, st["ukv"].U + 3)
                for i in range(4):
                    e.tensor_copy(zkv[:, 2 * i:2 * i + 2, :], ps[:, i, :].rearrange("p (a b) -> p a b", a=2))\
                        .then_inc(S("kv_out"), 1)
                split(st["cmp_w1"], It(0))
                split(st["cmp_w1"], It(1))
                heads(mla_heads)
                for i in range(5):
                    two = i < 4
                    n = 512 if two else SEQ
                    src = q96[:, 2 * i:2 * i + 2, :] if two else q96[:, 8, :]
                    dst = src if two else z[0:96, 3, META:T]
                    c, s = (rope[:, 2 + j, :] if two else rope[:, j, :] for j in range(2))
                    t0, t1, p = rot_t[:, 0, 0:n], rot_t[:, 1, 0:n], ps[0:96, 2 + i % 2, 0:n]
                    if two:
                        c, s = (v.unsqueeze(1).broadcast_to([96, 2, SEQ]) for v in (c, s))
                        t0, t1, p = (v.rearrange("p (a b) -> p a b", a=2) for v in (t0, t1, p))
                    e.wait_ge(S("rot_mm"), i + 1)
                    tt(t0, src, c, ALU.mult).then_inc(S("rot_step"), 1)
                    tt(t1, p, s, ALU.mult).then_inc(S("rot_step"), 1)
                    e.wait_ge(S("rot_step"), 2 * i + 2)
                    if not two:
                        dst, t0, t1 = dst[64:96], t0[64:96], t1[64:96]
                    tt(dst, t0, t1, ALU.add).then_inc(S("rotated"), 1)
                    e.wait_ge(S("rotated"), i + 1)
                attention(mla)
                heads(nsa_heads)
                for j in range(2):
                    for g in range(2):
                        for hi in range(2):
                            e.wait_ge(S("a2_in"), 16 * 8)
                            v = a2[:, j, g, :].rearrange("p (m l two) -> p l m two", l=8, two=2)
                            o = PAR["cmp_pe"][0] + 16 * j + 8 * hi
                            pe = par[:, o:o + 8].unsqueeze(2).broadcast_to([128, 8, 15])
                            tt(x2[:, j, 8 * hi:8 * hi + 8, g, :], v[:, :, hi:hi + 15, 0], pe, ALU.add)\
                                .then_inc(S("x2_f"), 1)
                e.wait_ge(S("x2_hi"), 1)
                tt(x2_lo[:, :, :, :].rearrange("p j i c -> p (j i c)"),
                   x2[:, :, :, :, :].rearrange("p j i g n -> p (j i g n)"),
                   x2_hi[:, :, :, :].rearrange("p j i c -> p (j i c)").bitcast(f32), ALU.subtract).then_inc(S("x2"), 1)
                c = st["cmp_w1"]
                for u in range(2):
                    split(*ahead(c, It(u)))
                split(*ahead(c, It(2)))
                split(*ahead(c, It(3)))
                norms(cmp_norms)
                attention(nsa)

            def dve_odd():
                rms_norm(4, 1, 1, X["od"])
                evacuate("od_in", META, 1, step=2)
                heads(odd_heads)
                attention(odd)

            def dve_second():
                e.wait_ge(S("mod_step"), 2)
                rms_norm(0, 0, 0, X["g0"])
                swiglu(0, 0, 0)
                dve_even()
                stage_out("ev_out", META, gate=(0, 24 + 16))
                rms_norm(2, 0, 2, X["g1"])
                modulation(5)
                swiglu(1, 0, 2)
                e.wait_ge(S("mod_step"), 4)
                rms_norm(3, 1, 0, X["g2"])
                swiglu(2, 1, 0)
                dve_odd()
                stage_out("od_out", META, gate=(1, 24 + 16))
                rms_norm(5, 1, 2, X["g3"])
                swiglu(3, 1, 2)

            stage_out("a_out", 0)
            layer_norm(0, "ln1", 0, 0, X["f0"])
            modulation(0)
            for l, t0 in ((0, 0), (1, Q0)):
                if l:
                    dve_fox()
                    stage_out("b_out", Q0)
                    layer_norm(2, "ln1", 1, Q0, X["f1"])
                    modulation(2)
                ffn_conv(l, t0)
                stage_out(f"f_out{l}", t0)
                layer_norm(2 * l + 1, "ln2", l, t0, X["fox"] if l == 0 else None)
                modulation(2 * l + 1)
            dve_second()


def kernel(**inputs):
    import concourse.bacc as bacc
    from concourse.bass_utils import run_bass_kernel_spmd

    nc = bacc.Bacc("TRN2", target_bir_lowering=False, num_devices=1)
    arrays = {name: np.ascontiguousarray(a) for name, a in pack(inputs).items()}
    ap = {name: nc.dram_tensor(name, a.shape, mybir.dt.from_np(a.dtype), kind="ExternalInput").ap()
          for name, a in arrays.items()}
    ap["out"] = nc.dram_tensor("out", [128, KC, SEQ], mybir.dt.float32, kind="ExternalOutput").ap()
    build(nc, ap)
    r = run_bass_kernel_spmd(nc, [arrays], core_ids=[0])
    return r.results[0]["out"].transpose(1, 0, 2).reshape(D, SEQ).T[None]
```
